# Optimizing a Trainium2 kernel written in Bass

```python
import math
import jax, jax.numpy as jnp
from jax import lax
import numpy as np

D_MODEL = 1024
BATCH = 1
SEQ = 1024
DEPTH = 1

MIX_WIDTH = D_MODEL
DIFF_WIDTH = MIX_WIDTH // 2
RET_WIDTH = MIX_WIDTH - DIFF_WIDTH
N_DIFF_HEADS = 4
DIFF_HEAD_DIM = DIFF_WIDTH // N_DIFF_HEADS // 2
DIFF_V_DIM = 2 * DIFF_HEAD_DIM
N_RET_HEADS = 4
RET_HEAD_DIM = RET_WIDTH // N_RET_HEADS
D_FF = 4 * D_MODEL
Q_BLOCK = 128
RET_CHUNK = 128
NORM_EPS = 1e-5
IN_WIDTH = 3 * DIFF_WIDTH + 4 * RET_WIDTH


def rms_norm(x, g, eps=NORM_EPS):
    xf = x.astype(jnp.float32)
    y = xf * lax.rsqrt(jnp.mean(xf * xf, axis=-1, keepdims=True) + eps)
    return (y * g.astype(jnp.float32)).astype(x.dtype)

def alibi_slopes(n_heads):
    return jnp.exp2(-8.0 * jnp.arange(1, n_heads + 1, dtype=jnp.float32) / n_heads)

def diff_attention(q, k, v, lam):
    b, s = q.shape[0], q.shape[1]
    nb = s // Q_BLOCK
    scale = DIFF_HEAD_DIM ** -0.5
    slopes = alibi_slopes(N_DIFF_HEADS)
    kpos = jnp.arange(s, dtype=jnp.float32)
    qb = (q * scale).reshape(b, nb, Q_BLOCK, N_DIFF_HEADS, 2, DIFF_HEAD_DIM)
    qb = qb.transpose(1, 0, 3, 4, 2, 5)
    kt = k.transpose(0, 2, 3, 1, 4)
    vt = v.transpose(0, 2, 1, 3)

    def block(args):
        bi, qblk = args
        qpos = (bi * Q_BLOCK + jnp.arange(Q_BLOCK)).astype(jnp.float32)
        dist = qpos[:, None] - kpos[None, :]
        bias = jnp.where(dist >= 0, -slopes[:, None, None] * dist, -jnp.inf)
        scores = jnp.einsum('bhmqd,bhmkd->bhmqk', qblk, kt) + bias[None, :, None]
        p = jax.nn.softmax(scores, axis=-1)
        a = p[:, :, 0] - lam * p[:, :, 1]
        return jnp.einsum('bhqk,bhkv->bhqv', a, vt)

    out = lax.map(block, (jnp.arange(nb), qb))
    return out.transpose(1, 0, 3, 2, 4).reshape(b, s, N_DIFF_HEADS, DIFF_V_DIM)

def retention_chunkwise(q, k, v):
    b, s = q.shape[0], q.shape[1]
    C = RET_CHUNK
    nc = s // C
    log_g = jnp.log1p(-jnp.exp2(-5.0 - jnp.arange(N_RET_HEADS, dtype=jnp.float32)))
    i = jnp.arange(C, dtype=jnp.float32)
    rel = i[:, None] - i[None, :]
    d_intra = jnp.where(rel >= 0, jnp.exp(log_g[:, None, None] * jnp.maximum(rel, 0.0)), 0.0)
    q_decay = jnp.exp(log_g[:, None] * (i + 1.0))[None, :, :, None]
    k_decay = jnp.exp(log_g[:, None] * (C - 1.0 - i))[None, :, :, None]
    chunk_decay = jnp.exp(log_g * C)[None, :, None, None]
    k = k * (RET_HEAD_DIM ** -0.5)

    def to_chunks(t):
        return t.reshape(b, nc, C, N_RET_HEADS, t.shape[-1]).transpose(1, 0, 3, 2, 4)

    def step(state, inp):
        qc, kc, vc = inp
        intra = jnp.einsum('bhqd,bhkd->bhqk', qc, kc) * d_intra[None]
        o = (jnp.einsum('bhqk,bhkv->bhqv', intra, vc)
             + jnp.einsum('bhqd,bhdv->bhqv', qc, state) * q_decay)
        state = state * chunk_decay + jnp.einsum('bhkd,bhkv->bhdv', kc * k_decay, vc)
        return state, o

    state0 = jnp.zeros((b, N_RET_HEADS, RET_HEAD_DIM, RET_HEAD_DIM), jnp.float32)
    _, o = lax.scan(step, state0, (to_chunks(q), to_chunks(k), to_chunks(v)))
    return o.transpose(1, 0, 3, 2, 4).reshape(b, s, N_RET_HEADS, RET_HEAD_DIM)

def first_inputs(seed: int = 0) -> dict:
    key = jax.random.key(seed)
    ks = jax.random.split(key, 16)
    f32 = jnp.float32

    def nrm(k, shape, scale):
        return jax.random.normal(k, shape, f32) * scale

    return {
        "x": nrm(ks[0], (BATCH, SEQ, D_MODEL), 1.0),
        "norm1_g": 1.0 + nrm(ks[1], (DEPTH, D_MODEL), 0.02),
        "w_in": nrm(ks[2], (DEPTH, D_MODEL, IN_WIDTH), D_MODEL ** -0.5),
        "lambda_q1": nrm(ks[3], (DEPTH, DIFF_HEAD_DIM), 0.1),
        "lambda_k1": nrm(ks[4], (DEPTH, DIFF_HEAD_DIM), 0.1),
        "lambda_q2": nrm(ks[5], (DEPTH, DIFF_HEAD_DIM), 0.1),
        "lambda_k2": nrm(ks[6], (DEPTH, DIFF_HEAD_DIM), 0.1),
        "diff_norm_g": 1.0 + nrm(ks[7], (DEPTH, DIFF_V_DIM), 0.02),
        "ret_norm_g": 1.0 + nrm(ks[8], (DEPTH, RET_WIDTH), 0.02),
        "w_out": nrm(ks[9], (DEPTH, MIX_WIDTH, D_MODEL), MIX_WIDTH ** -0.5),
        "norm2_g": 1.0 + nrm(ks[10], (DEPTH, D_MODEL), 0.02),
        "w_up": nrm(ks[11], (DEPTH, D_MODEL, D_FF), D_MODEL ** -0.5),
        "w_down": nrm(ks[12], (DEPTH, D_FF, D_MODEL), D_FF ** -0.5),
        "final_norm_g": 1.0 + nrm(ks[13], (D_MODEL,), 0.02),
    }

def first_block(x, norm1_g, w_in, lambda_q1, lambda_k1, lambda_q2, lambda_k2,
              diff_norm_g, ret_norm_g, w_out, norm2_g, w_up, w_down, final_norm_g):
    b, s = x.shape[0], x.shape[1]
    f32 = jnp.float32
    splits = [DIFF_WIDTH, 2 * DIFF_WIDTH, 3 * DIFF_WIDTH,
              3 * DIFF_WIDTH + RET_WIDTH, 3 * DIFF_WIDTH + 2 * RET_WIDTH,
              3 * DIFF_WIDTH + 3 * RET_WIDTH]
    for l in range(DEPTH):
        lambda_init = 0.8 - 0.6 * math.exp(-0.3 * l)
        h = rms_norm(x, norm1_g[l])
        proj = jnp.einsum('bsd,de->bse', h, w_in[l]).astype(f32)
        dq, dk, dv, rq, rk, rv, rg = jnp.split(proj, splits, axis=-1)

        lam = (jnp.exp(jnp.sum(lambda_q1[l].astype(f32) * lambda_k1[l].astype(f32)))
               - jnp.exp(jnp.sum(lambda_q2[l].astype(f32) * lambda_k2[l].astype(f32)))
               + lambda_init)
        dq = dq.reshape(b, s, N_DIFF_HEADS, 2, DIFF_HEAD_DIM)
        dk = dk.reshape(b, s, N_DIFF_HEADS, 2, DIFF_HEAD_DIM)
        dv = dv.reshape(b, s, N_DIFF_HEADS, DIFF_V_DIM)
        a_out = diff_attention(dq, dk, dv, lam)
        a_out = rms_norm(a_out, diff_norm_g[l]) * (1.0 - lambda_init)
        a_out = a_out.reshape(b, s, DIFF_WIDTH)

        rq = rq.reshape(b, s, N_RET_HEADS, RET_HEAD_DIM)
        rk = rk.reshape(b, s, N_RET_HEADS, RET_HEAD_DIM)
        rv = rv.reshape(b, s, N_RET_HEADS, RET_HEAD_DIM)
        r_out = retention_chunkwise(rq, rk, rv)
        r_out = rms_norm(r_out, ret_norm_g[l].reshape(N_RET_HEADS, RET_HEAD_DIM))
        r_out = r_out.reshape(b, s, RET_WIDTH) * jax.nn.silu(rg)

        mix = jnp.concatenate([a_out, r_out], axis=-1).astype(x.dtype)
        x = x + jnp.einsum('bse,ed->bsd', mix, w_out[l])

        h2 = rms_norm(x, norm2_g[l])
        up = jnp.square(jax.nn.relu(jnp.einsum('bsd,df->bsf', h2, w_up[l])))
        x = x + jnp.einsum('bsf,fd->bsd', up, w_down[l])
    return rms_norm(x, final_norm_g)


_first_inputs = first_inputs


def first_inputs(seed=0):
    import zlib

    import numpy as np

    out = dict(_first_inputs(seed))
    spreads = {}
    factors = {'lambda_q1': 4.024,
     'lambda_k1': 2.917,
     'lambda_q2': 8.0,
     'diff_norm_g': 5.299,
     'ret_norm_g': 7.959,
     'norm2_g': 3.582,
     'final_norm_g': 2.733}
    for name, (base, spread) in spreads.items():
        noise = np.random.default_rng([zlib.crc32(name.encode()), seed]).standard_normal(out[name].shape)
        drawn = base * np.exp(spread * noise) if base else spread * noise
        out[name] = __import__('jax').numpy.asarray(drawn.astype(out[name].dtype))
    for name, factor in factors.items():
        out[name] = (out[name] * factor).astype(out[name].dtype)
    return out


_narrow_inputs = first_inputs


def first_inputs(seed=0):

    out = dict(_narrow_inputs(seed))
    wider = {'lambda_q2': 12.0, 'diff_norm_g': 3.99, 'ret_norm_g': 4.05, 'final_norm_g': 3.07}
    for name, times in wider.items():
        mean = out[name].mean()
        out[name] = (mean + times * (out[name] - mean)).astype(out[name].dtype)
    return out


D_MIX = D_MODEL
GROUP_W = D_MIX // 4
GRID_W = 64
NA_HEADS = 8
NA_HEAD_DIM = GROUP_W // NA_HEADS
NA_ROWS = 8
NA_COLS = 16
CONV_WIDTH = 31
POOL_WINDOWS = (2, 4, 8, 16)
POOL_GROUPS = len(POOL_WINDOWS)
POOL_GROUP_W = GROUP_W // POOL_GROUPS
SGU_HEADS = 4
SGU_HEAD_DIM = GROUP_W // SGU_HEADS
SGU_CHUNK = 128
D_IN = 8 * GROUP_W + D_MIX
RMS_EPS = 1e-6
LN_EPS = 1e-5


def rmsnorm(x, g):
    xf = x.astype(jnp.float32)
    y = xf * lax.rsqrt(jnp.mean(xf * xf, axis=-1, keepdims=True) + RMS_EPS)
    return (y * g.astype(jnp.float32)).astype(x.dtype)

def layernorm(x, g, b):
    xf = x.astype(jnp.float32)
    mu = jnp.mean(xf, axis=-1, keepdims=True)
    var = jnp.mean(jnp.square(xf - mu), axis=-1, keepdims=True)
    y = (xf - mu) * lax.rsqrt(var + LN_EPS)
    return (y * g.astype(jnp.float32) + b.astype(jnp.float32)).astype(x.dtype)

def neighborhood_attention(q, k, v, rpb):
    B, S, _ = q.shape
    rows = S // GRID_W
    kh = min(NA_ROWS, rows)
    kw = NA_COLS
    H, dh = NA_HEADS, NA_HEAD_DIM
    r = jnp.arange(rows)
    row_start = jnp.clip(r - kh // 2, 0, rows - kh)
    row_idx = row_start[:, None] + jnp.arange(kh)[None, :]
    c = jnp.arange(GRID_W)
    col_start = jnp.clip(c - kw // 2, 0, GRID_W - kw)
    col_ok = (c[None, :] >= col_start[:, None]) & (c[None, :] < col_start[:, None] + kw)
    qg = q.reshape(B, rows, GRID_W, H, dh)
    kband = jnp.take(k.reshape(B, rows, GRID_W, H, dh), row_idx, axis=1)
    vband = jnp.take(v.reshape(B, rows, GRID_W, H, dh), row_idx, axis=1)
    s = jnp.einsum('brqhd,brjkhd->bhrqjk', qg, kband).astype(jnp.float32) * (dh ** -0.5)
    dr = row_idx - r[:, None]
    dc = jnp.clip(c[None, :] - c[:, None], -(kw - 1), kw - 1)
    idx_r = (dr + NA_ROWS - 1)[:, None, :, None]
    idx_c = (dc + NA_COLS - 1)[None, :, None, :]
    bias = rpb[:, idx_r, idx_c].astype(jnp.float32)
    s = jnp.where(col_ok[None, None, None, :, None, :], s + bias[None], -jnp.inf)
    p = jax.nn.softmax(s.reshape(B, H, rows, GRID_W, kh * GRID_W), axis=-1)
    p = p.reshape(B, H, rows, GRID_W, kh, GRID_W).astype(v.dtype)
    out = jnp.einsum('bhrqjk,brjkhd->brqhd', p, vband)
    return out.reshape(B, S, H * dh)

def conformer_conv(a, b, dw_w, dw_b, ln_g, ln_b, pw):
    h = a * jax.nn.sigmoid(b)
    h = lax.conv_general_dilated(h, dw_w[:, None, :], window_strides=(1,),
                                 padding=[(CONV_WIDTH // 2, CONV_WIDTH // 2)],
                                 dimension_numbers=('NWC', 'WIO', 'NWC'),
                                 feature_group_count=h.shape[-1]) + dw_b
    h = jax.nn.silu(layernorm(h, ln_g, ln_b))
    return h @ pw

def multiscale_pool(xc, pool_w, pool_scale):
    B, S, _ = xc.shape
    xg = xc.reshape(B, S, POOL_GROUPS, POOL_GROUP_W).astype(jnp.float32)
    csum = jnp.concatenate([jnp.zeros((B, 1, POOL_GROUPS, POOL_GROUP_W), jnp.float32),
                            jnp.cumsum(xg, axis=1)], axis=1)
    t = jnp.arange(S)[:, None]
    w = jnp.array(POOL_WINDOWS, dtype=jnp.int32)[None, :]
    lo = jnp.clip(t - w // 2, 0, S)
    hi = jnp.clip(t - w // 2 + w, 0, S)
    g_idx = jnp.arange(POOL_GROUPS)[None, :]
    win_sum = csum[:, hi, g_idx] - csum[:, lo, g_idx]
    count = (hi - lo).astype(jnp.float32)[None, :, :, None]
    pooled = (win_sum / count - xg).astype(xc.dtype)
    y = jnp.einsum('bsgc,gcd->bsgd', pooled, pool_w).reshape(B, S, GROUP_W)
    return y * pool_scale

def spatial_gating(u, v, ln_g, ln_b, ws, bs):
    B, S, _ = u.shape
    v = layernorm(v, ln_g, ln_b)
    vc = v.reshape(B, S // SGU_CHUNK, SGU_CHUNK, SGU_HEADS, SGU_HEAD_DIM)
    mixed = jnp.einsum('hpq,bnqhd->bnphd', ws, vc) + bs.T[None, None, :, :, None]
    return u * mixed.reshape(B, S, GROUP_W)

def second_inputs(seed: int = 0) -> dict:
    key = jax.random.key(seed)
    ks = jax.random.split(key, 20)
    f32 = jnp.float32
    nrm = lambda k, shape, s: jax.random.normal(k, shape, f32) * s
    return {
        "x": nrm(ks[0], (BATCH, SEQ, D_MODEL), 1.0),
        "norm_g": 1.0 + nrm(ks[1], (DEPTH, D_MODEL), 0.02),
        "w_in": nrm(ks[2], (DEPTH, D_MODEL, D_IN), D_MODEL ** -0.5),
        "na_rpb": nrm(ks[3], (DEPTH, NA_HEADS, 2 * NA_ROWS - 1, 2 * NA_COLS - 1), 0.1),
        "conv_dw_w": nrm(ks[4], (DEPTH, CONV_WIDTH, GROUP_W), CONV_WIDTH ** -0.5),
        "conv_dw_b": nrm(ks[5], (DEPTH, GROUP_W), 0.02),
        "conv_ln_g": 1.0 + nrm(ks[6], (DEPTH, GROUP_W), 0.02),
        "conv_ln_b": nrm(ks[7], (DEPTH, GROUP_W), 0.02),
        "conv_pw": nrm(ks[8], (DEPTH, GROUP_W, GROUP_W), GROUP_W ** -0.5),
        "pool_w": nrm(ks[9], (DEPTH, POOL_GROUPS, POOL_GROUP_W, POOL_GROUP_W), POOL_GROUP_W ** -0.5),
        "pool_scale": 1.0 + nrm(ks[10], (DEPTH, GROUP_W), 0.02),
        "sgu_ln_g": 1.0 + nrm(ks[11], (DEPTH, GROUP_W), 0.02),
        "sgu_ln_b": nrm(ks[12], (DEPTH, GROUP_W), 0.02),
        "sgu_w": nrm(ks[13], (DEPTH, SGU_HEADS, SGU_CHUNK, SGU_CHUNK), SGU_CHUNK ** -0.5),
        "sgu_b": 1.0 + nrm(ks[14], (DEPTH, SGU_HEADS, SGU_CHUNK), 0.02),
        "w_out": nrm(ks[15], (DEPTH, D_MIX, D_MODEL), D_MIX ** -0.5),
        "final_g": 1.0 + nrm(ks[16], (D_MODEL,), 0.02),
    }

def second_block(x, norm_g, w_in, na_rpb, conv_dw_w, conv_dw_b, conv_ln_g, conv_ln_b, conv_pw,
              pool_w, pool_scale, sgu_ln_g, sgu_ln_b, sgu_w, sgu_b, w_out, final_g):
    split_at = [GROUP_W * i for i in range(1, 9)]
    for l in range(DEPTH):
        h = rmsnorm(x, norm_g[l])
        z = h @ w_in[l]
        qa, ka, va, glu_a, glu_b, pool_in, sgu_u, sgu_v, gates = jnp.split(z, split_at, axis=-1)
        y_a = neighborhood_attention(qa, ka, va, na_rpb[l])
        y_b = conformer_conv(glu_a, glu_b, conv_dw_w[l], conv_dw_b[l], conv_ln_g[l], conv_ln_b[l], conv_pw[l])
        y_c = multiscale_pool(pool_in, pool_w[l], pool_scale[l])
        y_d = spatial_gating(jax.nn.gelu(sgu_u), jax.nn.gelu(sgu_v), sgu_ln_g[l], sgu_ln_b[l], sgu_w[l], sgu_b[l])
        y = jnp.concatenate([y_a, y_b, y_c, y_d], axis=-1) * jax.nn.silu(gates)
        x = x + y @ w_out[l]
    return rmsnorm(x, final_g)


_first_inputs_2 = second_inputs


def second_inputs(seed=0):
    import zlib

    import numpy as np

    out = dict(_first_inputs_2(seed))
    spreads = {}
    factors = {'norm_g': 4.372,
     'na_rpb': 30.6,
     'conv_dw_b': 57.344,
     'conv_ln_g': 64.0,
     'conv_ln_b': 64.0,
     'pool_scale': 33.088,
     'sgu_ln_g': 45.603,
     'sgu_ln_b': 45.772,
     'sgu_b': 48.425,
     'final_g': 8.184}
    for name, (base, spread) in spreads.items():
        noise = np.random.default_rng([zlib.crc32(name.encode()), seed]).standard_normal(out[name].shape)
        drawn = base * np.exp(spread * noise) if base else spread * noise
        out[name] = __import__('jax').numpy.asarray(drawn.astype(out[name].dtype))
    for name, factor in factors.items():
        out[name] = (out[name] * factor).astype(out[name].dtype)
    return out


_narrow_inputs_2 = second_inputs


def second_inputs(seed=0):

    out = dict(_narrow_inputs_2(seed))
    wider = {'na_rpb': 7.72,
     'conv_ln_g': 12.0,
     'conv_ln_b': 12.0,
     'pool_scale': 5.72,
     'sgu_ln_g': 5.89,
     'sgu_ln_b': 5.87,
     'sgu_b': 5.92,
     'final_g': 3.22}
    for name, times in wider.items():
        mean = out[name].mean()
        out[name] = (mean + times * (out[name] - mean)).astype(out[name].dtype)
    return out


N_MEM = 256
EPS = 1e-6
MIX_WIDTH_3 = D_MODEL
ATTN_WIDTH = MIX_WIDTH_3 // 2
ATTN_HEAD_DIM = 64
ATTN_Q_HEADS = ATTN_WIDTH // ATTN_HEAD_DIM
ATTN_KV_HEADS = ATTN_Q_HEADS // 4
ATTN_KV_WIDTH = ATTN_KV_HEADS * ATTN_HEAD_DIM
WINDOW = 128
BLOCK = 128
HGRN_WIDTH = MIX_WIDTH_3 - ATTN_WIDTH
HGRN_VAL_DIM = 128
HGRN_HEADS = HGRN_WIDTH // HGRN_VAL_DIM
HGRN_KEY_DIM = 128
HGRN_FDIM = HGRN_HEADS * HGRN_KEY_DIM
CHUNK = 64
IN_SPLITS = (ATTN_WIDTH, ATTN_KV_WIDTH, ATTN_KV_WIDTH, HGRN_FDIM, HGRN_FDIM, HGRN_WIDTH, HGRN_WIDTH)
IN_PROJ_WIDTH = sum(IN_SPLITS)
CA_HEADS = 4
CA_HEAD_DIM = D_MODEL // CA_HEADS
CA_WIDTH = CA_HEADS * CA_HEAD_DIM
D_FF_3 = 2816
CONV_WIDTH_3 = 3


def rms_norm_3(x, w):
    xf = x.astype(jnp.float32)
    y = xf * lax.rsqrt(jnp.mean(xf * xf, axis=-1, keepdims=True) + EPS)
    return (y * w.astype(jnp.float32)).astype(x.dtype)

def sliding_window_sink_attention(q, k, v, sinks):
    B, T, Hq, D = q.shape
    Hkv = k.shape[2]
    G = Hq // Hkv
    nb = T // BLOCK
    qb = q.reshape(B, nb, BLOCK, Hkv, G, D)

    def with_prev(t):
        tb = t.reshape(B, nb, BLOCK, Hkv, D)
        prev = jnp.pad(tb, ((0, 0), (1, 0), (0, 0), (0, 0), (0, 0)))[:, :-1]
        return jnp.concatenate([prev, tb], axis=2)

    kw, vw = with_prev(k), with_prev(v)
    s = jnp.einsum('bnqhgd,bnkhd->bnhgqk', qb, kw).astype(jnp.float32) * (D ** -0.5)
    qi = jnp.arange(BLOCK)[:, None]
    kj = jnp.arange(2 * BLOCK)[None, :]
    diff = qi + BLOCK - kj
    key_pos = jnp.arange(nb)[:, None, None] * BLOCK - BLOCK + kj[None]
    allowed = (diff >= 0) & (diff < WINDOW) & (key_pos >= 0)
    s = jnp.where(allowed[None, :, None, None], s, -jnp.inf)
    sink = sinks.astype(jnp.float32).reshape(Hkv, G)[None, None, :, :, None, None]
    sink = jnp.broadcast_to(sink, s.shape[:-1] + (1,))
    p = jax.nn.softmax(jnp.concatenate([s, sink], axis=-1), axis=-1)[..., :-1]
    o = jnp.einsum('bnhgqk,bnkhd->bnqhgd', p.astype(v.dtype), vw)
    return o.reshape(B, T, Hq * D)

def hgrn2_chunkwise(q, k, v, log_f):
    B, T, H, K = q.shape
    V = v.shape[-1]
    n = T // CHUNK

    def to_chunks(t):
        return t.reshape(B, n, CHUNK, H, t.shape[-1]).transpose(1, 0, 3, 2, 4)

    causal = jnp.tril(jnp.ones((CHUNK, CHUNK), dtype=bool))

    def step(S, xs):
        qc, kc, vc, gc = xs
        bc = jnp.cumsum(gc, axis=2)
        rel = bc[:, :, :, None, :] - bc[:, :, None, :, :]
        decay = jnp.exp(jnp.where(causal[:, :, None], rel, -jnp.inf))
        A = jnp.einsum('bhtk,bhsk,bhtsk->bhts', qc, kc, decay)
        o = jnp.einsum('bhts,bhsv->bhtv', A, vc) + jnp.einsum('bhtk,bhkv->bhtv', qc * jnp.exp(bc), S)
        b_last = bc[:, :, -1:, :]
        S = S * jnp.exp(b_last[:, :, 0, :])[..., None] + jnp.einsum(
            'bhsk,bhsv->bhkv', kc * jnp.exp(b_last - bc), vc)
        return S, o

    S0 = jnp.zeros((B, H, K, V), jnp.float32)
    _, o = lax.scan(step, S0, (to_chunks(q), to_chunks(k), to_chunks(v), to_chunks(log_f)))
    return o.transpose(1, 0, 3, 2, 4).reshape(B, T, H, V)

def hgrn2_group(q_raw, f_raw, i_raw, g_raw, lb, out_norm_w):
    B, T, _ = q_raw.shape
    f32 = jnp.float32
    q = jax.nn.silu(q_raw.astype(f32)).reshape(B, T, HGRN_HEADS, HGRN_KEY_DIM) * (HGRN_KEY_DIM ** -0.5)
    fr = f_raw.astype(f32)
    lb = lb.astype(f32)
    f = lb + (1.0 - lb) * jax.nn.sigmoid(fr)
    k = (1.0 - lb) * jax.nn.sigmoid(-fr)
    log_f = jnp.log(f)
    k = k.reshape(B, T, HGRN_HEADS, HGRN_KEY_DIM)
    log_f = log_f.reshape(B, T, HGRN_HEADS, HGRN_KEY_DIM)
    v = i_raw.astype(f32).reshape(B, T, HGRN_HEADS, HGRN_VAL_DIM)
    o = hgrn2_chunkwise(q, k, v, log_f)
    o = rms_norm_3(o, out_norm_w).reshape(B, T, HGRN_WIDTH)
    return (o * jax.nn.silu(g_raw.astype(f32))).astype(q_raw.dtype)

def memory_cross_attention(h, mem_n, wq, wk, wv, wo):
    B, T, _ = h.shape
    M = mem_n.shape[1]
    q = (h @ wq).reshape(B, T, CA_HEADS, CA_HEAD_DIM)
    k = (mem_n @ wk).reshape(B, M, CA_HEADS, CA_HEAD_DIM)
    v = (mem_n @ wv).reshape(B, M, CA_HEADS, CA_HEAD_DIM)
    s = jnp.einsum('bthd,bmhd->bhtm', q, k).astype(jnp.float32) * (CA_HEAD_DIM ** -0.5)
    p = jax.nn.softmax(s, axis=-1).astype(v.dtype)
    o = jnp.einsum('bhtm,bmhd->bthd', p, v).reshape(B, T, CA_WIDTH)
    return o @ wo

def conv_ffn(h, w_up, conv_w, conv_b, w_down):
    u = h @ w_up
    C = u.shape[-1]
    u = lax.conv_general_dilated(
        u, conv_w.reshape(CONV_WIDTH_3, 1, C).astype(u.dtype), window_strides=(1,),
        padding=[(CONV_WIDTH_3 - 1, 0)], dimension_numbers=('NWC', 'WIO', 'NWC'),
        feature_group_count=C) + conv_b
    gate, val = jnp.split(u, 2, axis=-1)
    return (jax.nn.gelu(gate, approximate=True) * val) @ w_down

def third_inputs(seed: int = 0) -> dict:
    key = jax.random.key(seed)
    ks = jax.random.split(key, 24)
    f32 = jnp.float32

    def w(k, shape, fan_in):
        return jax.random.normal(k, shape, f32) * (fan_in ** -0.5)

    def gain(k, shape):
        return 1.0 + 0.01 * jax.random.normal(k, shape, f32)

    return {
        "x": jax.random.normal(ks[0], (BATCH, SEQ, D_MODEL), f32),
        "mem": jax.random.normal(ks[1], (BATCH, N_MEM, D_MODEL), f32),
        "mix_pre_norm": gain(ks[2], (DEPTH, D_MODEL)),
        "w_in": w(ks[3], (DEPTH, D_MODEL, IN_PROJ_WIDTH), D_MODEL),
        "attn_sinks": 0.5 * jax.random.normal(ks[4], (DEPTH, ATTN_Q_HEADS), f32),
        "hgrn_lb_logits": 0.1 * jax.random.normal(ks[5], (DEPTH + 1, HGRN_FDIM), f32),
        "hgrn_out_norm": gain(ks[6], (DEPTH, HGRN_VAL_DIM)),
        "w_out": w(ks[7], (DEPTH, MIX_WIDTH_3, D_MODEL), MIX_WIDTH_3),
        "mix_post_norm": gain(ks[8], (DEPTH, D_MODEL)),
        "ca_pre_norm": gain(ks[9], (DEPTH, D_MODEL)),
        "mem_norm": gain(ks[10], (DEPTH, D_MODEL)),
        "ca_wq": w(ks[11], (DEPTH, D_MODEL, CA_WIDTH), D_MODEL),
        "ca_wk": w(ks[12], (DEPTH, D_MODEL, CA_WIDTH), D_MODEL),
        "ca_wv": w(ks[13], (DEPTH, D_MODEL, CA_WIDTH), D_MODEL),
        "ca_wo": w(ks[14], (DEPTH, CA_WIDTH, D_MODEL), CA_WIDTH),
        "ca_post_norm": gain(ks[15], (DEPTH, D_MODEL)),
        "ffn_pre_norm": gain(ks[16], (DEPTH, D_MODEL)),
        "ffn_w_up": w(ks[17], (DEPTH, D_MODEL, 2 * D_FF_3), D_MODEL),
        "ffn_conv_w": w(ks[18], (DEPTH, CONV_WIDTH_3, 2 * D_FF_3), CONV_WIDTH_3),
        "ffn_conv_b": 0.01 * jax.random.normal(ks[19], (DEPTH, 2 * D_FF_3), f32),
        "ffn_w_down": w(ks[20], (DEPTH, D_FF_3, D_MODEL), D_FF_3),
        "ffn_post_norm": gain(ks[21], (DEPTH, D_MODEL)),
    }

def third_block(x, mem, mix_pre_norm, w_in, attn_sinks, hgrn_lb_logits, hgrn_out_norm, w_out,
              mix_post_norm, ca_pre_norm, mem_norm, ca_wq, ca_wk, ca_wv, ca_wo, ca_post_norm,
              ffn_pre_norm, ffn_w_up, ffn_conv_w, ffn_conv_b, ffn_w_down, ffn_post_norm):
    B, T, _ = x.shape
    lower_bounds = jnp.cumsum(jax.nn.softmax(hgrn_lb_logits.astype(jnp.float32), axis=0), axis=0)
    split_points = list(np.cumsum(IN_SPLITS)[:-1])
    for l in range(DEPTH):
        h = rms_norm_3(x, mix_pre_norm[l])
        z = h @ w_in[l]
        q_a, k_a, v_a, q_h, f_h, i_h, g_h = jnp.split(z, split_points, axis=-1)
        attn = sliding_window_sink_attention(
            q_a.reshape(B, T, ATTN_Q_HEADS, ATTN_HEAD_DIM),
            k_a.reshape(B, T, ATTN_KV_HEADS, ATTN_HEAD_DIM),
            v_a.reshape(B, T, ATTN_KV_HEADS, ATTN_HEAD_DIM),
            attn_sinks[l])
        rec = hgrn2_group(q_h, f_h, i_h, g_h, lower_bounds[l], hgrn_out_norm[l])
        m = jnp.concatenate([attn.astype(x.dtype), rec.astype(x.dtype)], axis=-1) @ w_out[l]
        x = x + rms_norm_3(m, mix_post_norm[l])
        h = rms_norm_3(x, ca_pre_norm[l])
        mem_n = rms_norm_3(mem, mem_norm[l])
        c = memory_cross_attention(h, mem_n, ca_wq[l], ca_wk[l], ca_wv[l], ca_wo[l])
        x = x + rms_norm_3(c, ca_post_norm[l])
        h = rms_norm_3(x, ffn_pre_norm[l])
        y = conv_ffn(h, ffn_w_up[l], ffn_conv_w[l], ffn_conv_b[l], ffn_w_down[l])
        x = x + rms_norm_3(y, ffn_post_norm[l])
    return x


_first_inputs_3 = third_inputs


def third_inputs(seed=0):
    import zlib

    import numpy as np

    out = dict(_first_inputs_3(seed))
    spreads = {}
    factors = {'mix_pre_norm': 4.723,
     'attn_sinks': 29.971,
     'hgrn_lb_logits': 5.487,
     'hgrn_out_norm': 6.959,
     'mix_post_norm': 7.471,
     'ca_pre_norm': 8.0,
     'mem_norm': 6.035,
     'ca_post_norm': 53.811,
     'ffn_pre_norm': 54.418,
     'ffn_conv_b': 54.055,
     'ffn_post_norm': 64.0}
    for name, (base, spread) in spreads.items():
        noise = np.random.default_rng([zlib.crc32(name.encode()), seed]).standard_normal(out[name].shape)
        drawn = base * np.exp(spread * noise) if base else spread * noise
        out[name] = __import__('jax').numpy.asarray(drawn.astype(out[name].dtype))
    for name, factor in factors.items():
        out[name] = (out[name] * factor).astype(out[name].dtype)
    return out


_narrow_inputs_3 = third_inputs


def third_inputs(seed=0):

    out = dict(_narrow_inputs_3(seed))
    wider = {'ca_post_norm': 5.14, 'ffn_pre_norm': 5.96, 'ffn_conv_b': 5.94, 'ffn_post_norm': 8.08}
    for name, times in wider.items():
        mean = out[name].mean()
        out[name] = (mean + times * (out[name] - mean)).astype(out[name].dtype)
    return out


def setup_inputs(seed=0):
    out = dict(first_inputs(seed))
    for name, value in second_inputs(seed + 1).items():
        if name != "x":
            out[name + "_2"] = value
    for name, value in third_inputs(seed + 2).items():
        if name != "x":
            out[name + "_3"] = value
    return out


def reference(
    x, norm1_g, w_in, lambda_q1, lambda_k1, lambda_q2, lambda_k2, diff_norm_g, ret_norm_g,
    w_out, norm2_g, w_up, w_down, final_norm_g, norm_g_2, w_in_2, na_rpb_2, conv_dw_w_2,
    conv_dw_b_2, conv_ln_g_2, conv_ln_b_2, conv_pw_2, pool_w_2, pool_scale_2, sgu_ln_g_2,
    sgu_ln_b_2, sgu_w_2, sgu_b_2, w_out_2, final_g_2, mem_3, mix_pre_norm_3, w_in_3,
    attn_sinks_3, hgrn_lb_logits_3, hgrn_out_norm_3, w_out_3, mix_post_norm_3, ca_pre_norm_3,
    mem_norm_3, ca_wq_3, ca_wk_3, ca_wv_3, ca_wo_3, ca_post_norm_3, ffn_pre_norm_3, ffn_w_up_3,
    ffn_conv_w_3, ffn_conv_b_3, ffn_w_down_3, ffn_post_norm_3,
):
    x = first_block(
        x, norm1_g, w_in, lambda_q1, lambda_k1, lambda_q2, lambda_k2, diff_norm_g, ret_norm_g,
        w_out, norm2_g, w_up, w_down, final_norm_g,
    )
    x = second_block(
        x, norm_g_2, w_in_2, na_rpb_2, conv_dw_w_2, conv_dw_b_2, conv_ln_g_2, conv_ln_b_2,
        conv_pw_2, pool_w_2, pool_scale_2, sgu_ln_g_2, sgu_ln_b_2, sgu_w_2, sgu_b_2, w_out_2,
        final_g_2,
    )
    return third_block(
        x, mem_3, mix_pre_norm_3, w_in_3, attn_sinks_3, hgrn_lb_logits_3, hgrn_out_norm_3,
        w_out_3, mix_post_norm_3, ca_pre_norm_3, mem_norm_3, ca_wq_3, ca_wk_3, ca_wv_3, ca_wo_3,
        ca_post_norm_3, ffn_pre_norm_3, ffn_w_up_3, ffn_conv_w_3, ffn_conv_b_3, ffn_w_down_3,
        ffn_post_norm_3,
    )


_drawn_inputs = setup_inputs


def setup_inputs(seed=0):
    import zlib

    import numpy as np

    out = dict(_drawn_inputs(seed))
    spreads = {}
    factors = {}
    for name, (base, spread) in spreads.items():
        noise = np.random.default_rng([zlib.crc32(name.encode()), seed]).standard_normal(out[name].shape)
        drawn = base * np.exp(spread * noise) if base else spread * noise
        out[name] = __import__('jax').numpy.asarray(drawn.astype(out[name].dtype))
    for name, factor in factors.items():
        out[name] = (out[name] * factor).astype(out[name].dtype)
    return out
```

```python
import math
from contextlib import ExitStack, contextmanager

import numpy as np
import concourse.bass as bass
from concourse import mybir

F32 = mybir.dt.float32
F32R = mybir.dt.float32r
ALU = mybir.AluOpType
ACT = mybir.ActivationFunctionType
AX = mybir.AxisListType
ds = bass.ds

P = 128
T = 1024
D = 1024
KT = D // P
TT = T // P
BANK = 512
SILU = "silu_and_others"
EXP_LN = "natural_log_exp_and_others"


class Core:

    def __init__(self, nc, ctx):
        self.nc, self.ctx, self.retired = nc, ctx, []
        sb = self.sbuf
        self.x = sb("x_resid", [P, KT * T])
        self.h = tuple(self.sbuf(f"h_{part}", [P, KT * T], dt=F32R) for part in ("hi", "lo"))
        self.work = sb("work", [P, 4 * T + 4])
        self.rstd = sb("rstd", [P, T])
        self.ident = sb("ident", [P, P])
        self.ones = sb("ones", [P, P])
        self.eps5 = sb("eps5", [P, 1])
        self.eps6 = sb("eps6", [P, 1])
        self.ps = ctx.enter_context(nc.psum_tensor("psum_all", [P, 8 * BANK], F32))

    def sbuf(self, name, shape, ctx=None, dt=F32):
        return (ctx or self.ctx).enter_context(self.nc.sbuf_tensor(name, shape, dt))

    def bank(self, b, n=BANK, at=0):
        return self.ps[:, b * BANK + at:b * BANK + at + n]

    @contextmanager
    def phase(self, name, *signals):
        nc = self.nc
        if len(self.retired) + len(signals) > 130:
            nc.clear_and_free_semaphores(self.retired)
            nc.all_engine_barrier()
            self.retired = []
        sems = [nc.alloc_semaphore(f"{name}_{s}") for s in signals]
        with nc.Block() as block:
            yield (block, *sems)
        self.retired += sems


class Chain:

    def __init__(self, eng, sem):
        self.eng, self.sem, self.n = eng, sem, 0

    def mark(self, ins):
        ins.then_inc(self.sem, 1)
        self.n += 1

    def join(self):
        self.eng.wait_ge(self.sem, self.n)

    def link(self, ins):
        self.mark(ins)
        self.join()

    def restart(self):
        self.join()
        self.eng.sem_clear(self.sem)
        self.n = 0


def cols(buf, first, n=T):
    return buf[:, ds(first, n)]


class Weights:

    SIGNALS = ("raw0", "raw1", "hi_ready", "split_done", "used", "slot_seen")

    def __init__(self, core, name, ctx, kts=KT, raw=None):
        self.core, self.nc, self.kts = core, core.nc, kts
        self.chunks, self.pieces = kts // 2, max(kts // 4, 1)
        self.per_piece = self.chunks // self.pieces
        self.slots = min(4, 2 * self.chunks) if self.chunks != 3 else 3
        piece = kts // self.pieces * P
        if raw is None:
            raw = core.sbuf(f"{name}_raw", [P, 2 * piece], ctx)
        self.raw = [raw[:, n * piece:(n + 1) * piece] for n in range(2)]
        self.hi = [core.sbuf(f"{name}_hi{n}", [P, 2 * P], ctx, F32R) for n in range(self.slots)]
        self.lo = [core.sbuf(f"{name}_lo{n}", [P, 2 * P], ctx, F32R) for n in range(self.slots)]

    def signals(self, sems):
        self.raw0, self.raw1, self.hi_ready, self.split_done, self.used, self.slot_seen = sems
        self.raw_loaded = (self.raw0, self.raw1)

    def load(self, sp, t, s, views):
        for r in range(self.pieces):
            slot = (s * self.pieces + r) % 2
            sp.wait_ge(self.split_done, t * self.chunks + (r + 1) * self.per_piece)
            for pick, src in views[r]:
                dst = self.raw[slot].rearrange("p (k n) -> p k n", n=P)
                sp.dma_start(pick(dst), src).then_inc(self.raw_loaded[slot], 16)

    def parts(self, s):
        for c in range(self.chunks):
            r, at = divmod(c, self.per_piece)
            yield c, (s * self.chunks + c) % self.slots, (s * self.pieces + r) % 2, at * 2 * P

    def arrived(self, t, s, slot, dmas):
        if self.pieces == 2:
            return t * (16 * dmas[slot]) + 16 * dmas[slot]
        return (t - s) * (8 * dmas[slot]) + 16 * dmas[slot]

    def split_hi(self, act, t, s, dmas=(1, 1)):
        for c, slot, raw, at in self.parts(s):
            if c % self.per_piece == 0:
                act.wait_ge(self.raw_loaded[raw], self.arrived(t, s, raw, dmas))
            act.wait_ge(self.used, t * self.chunks + (c + 1))
            self.nc.scalar.activation(self.hi[slot][:, :], self.raw[raw][:, at:at + 2 * P], ACT.Copy) \
                .then_inc(self.hi_ready, 1)

    def split(self, pool, t, s, dmas=(1, 1)):
        for c, slot, raw, at in self.parts(s):
            if c % self.per_piece == 0:
                pool.wait_ge(self.raw_loaded[raw], self.arrived(t, s, raw, dmas))
            pool.wait_ge(self.used, t * self.chunks + (c + 1))
            pool.sem_inc(self.slot_seen, 1)
            self.nc.gpsimd.tensor_copy(self.hi[slot][:, :], self.raw[raw][:, at:at + 2 * P]).then_inc(self.hi_ready, 1)
            pool.wait_ge(self.hi_ready, t * self.chunks + (c + 1))
            self.nc.gpsimd.tensor_tensor(self.lo[slot][:, :], self.raw[raw][:, at:at + 2 * P],
                                         self.hi[slot][:, :].bitcast(F32), ALU.subtract).then_inc(self.split_done, 1)

    def split_lo(self, pool, t, s):
        for c, slot, raw, at in self.parts(s):
            pool.wait_ge(self.hi_ready, t * self.chunks + (c + 1))
            self.nc.gpsimd.tensor_tensor(self.lo[slot][:, :], self.raw[raw][:, at:at + 2 * P],
                                         self.hi[slot][:, :].bitcast(F32), ALU.subtract).then_inc(self.split_done, 1)

    def open_raw(self, pool):
        pool.sem_inc(self.split_done, 2 * self.per_piece)

    def open_slots(self, pe):
        pe.sem_inc(self.used, self.slots)

    def product(self, pe, out, act, t, s, tokens=T, stride=T, at=0, src_ready=None, chunks=None):
        hi, lo = act
        step = min(tokens, BANK)
        for c, slot, raw, _ in self.parts(s):
            if chunks is not None and c not in chunks:
                continue
            pe.wait_ge(self.split_done, t * self.chunks + (c + 1 + 2 * self.per_piece))
            for k in (2 * c, 2 * c + 1):
                if src_ready is not None:
                    pe.wait_ge(src_ready, k + 1)
                w = slice((k % 2) * P, (k % 2 + 1) * P)
                for n in range(0, tokens, step):
                    a = slice(k * stride + at + n, k * stride + at + n + step)
                    for m, (wt, x) in enumerate(((self.hi, hi), (self.hi, lo), (self.lo, hi))):
                        last = self.nc.tensor.matmul(out[:, n:n + step], wt[slot][:, w], x[:, a],
                                                     start=(k == 0 and m == 0), stop=(k == self.kts - 1 and m == 2))
            last.then_inc(self.used, 1)

    def wait_product(self, eng, t):
        eng.wait_ge(self.used, t * self.chunks + (self.chunks + self.slots))


def plain_views(w, kts, first):
    tiles = w[0:kts * P, ds(first, P)].rearrange("(k p) n -> p k n", p=P)
    pieces = max(kts // 4, 1)
    piece = kts // pieces
    return [[(lambda d: d, tiles[:, r * piece:(r + 1) * piece, :])] for r in range(pieces)]



def setup(core, c_in, small):
    nc = core.nc
    with core.phase("setup", "loaded") as (block, loaded):
        @block.sync
        def _(sp):
            sp.dma_start(core.ident[:, :], c_in["ident"]).then_inc(loaded, 16)
            for dst, src in small:
                with nc.allow_non_contiguous_dma("gains, one column a partition"):
                    sp.dma_start(dst, src).then_inc(loaded, 16)
            sp.wait_ge(loaded, 16 * (1 + len(small)))

        @block.vector
        def _(dve):
            nc.vector.memset(core.ones[:, :], 1.0)
            nc.vector.memset(core.eps5[:, :], 1e-5)
            nc.vector.memset(core.eps6[:, :], 1e-6)


def load_transposed(core, name, src, dst, tiles):
    nc, ctx = core.nc, ExitStack()
    stage, tok = core.sbuf(name + "_stage", [P, tiles * D], ctx), tiles * P
    group = min(4, tiles)
    steps = [(k, g) for g in range(tiles // group) for k in range(KT)]
    with core.phase(name, "loaded", "turned", "taken") as (block, loaded, turned, taken):
        @block.sync
        def _(sp):
            sp.dma_start(stage[:, 0:tiles * D].rearrange("p (t d) -> p t d", t=tiles),
                         src.rearrange("(t p) d -> p t d", p=P)).then_inc(loaded, 16)

        @block.tensor
        def _(pe):
            pe.wait_ge(loaded, 16)
            for n, (k, g) in enumerate(steps):
                if n >= 4:
                    pe.wait_ge(taken, n - 3)
                for j in range(group):
                    t = g * group + j
                    last = nc.tensor.transpose(core.bank(n % 4, P, j * P),
                                               stage[:, t * D + k * P:t * D + (k + 1) * P], core.ident[:, :])
                last.then_inc(turned, 1)

        @block.vector
        def _(dve):
            for n, (k, g) in enumerate(steps):
                dve.wait_ge(turned, n + 1)
                at = k * tok + g * group * P
                nc.vector.tensor_copy(dst[:, at:at + group * P], core.bank(n % 4, group * P)).then_inc(taken, 1)
    ctx.close()


def store_transposed(core, name, src, out):
    nc, ctx = core.nc, ExitStack()
    stage = core.sbuf(name + "_stage", [P, TT * D], ctx)
    with core.phase(name, "turned", "taken", "stored") as (block, turned, taken, stored):
        @block.tensor
        def _(pe):
            for t in range(TT):
                if t >= 2:
                    pe.wait_ge(taken, t - 1)
                for k in range(KT):
                    last = nc.tensor.transpose(core.bank(2 * (t % 2), P, k * P),
                                               src[:, k * T + t * P:k * T + (t + 1) * P], core.ident[:, :])
                last.then_inc(turned, 1)

        @block.vector
        def _(dve):
            for t in range(TT):
                dve.wait_ge(turned, t + 1)
                nc.vector.tensor_copy(stage[:, t * D:(t + 1) * D],
                                      core.bank(2 * (t % 2), D)).then_inc(taken, 1)

        @block.sync
        def _(sp):
            for t in range(TT):
                sp.wait_ge(taken, t + 1)
                sp.dma_start(out[t * P:(t + 1) * P, :], stage[:, t * D:(t + 1) * D]).then_inc(stored, 16)
            sp.wait_ge(stored, 16 * TT)
    ctx.close()



def rms_norm(core, name, src, gain, dst, eps, tok=T, residual=None):
    nc = core.nc
    acc, sq = core.work[:, 0:tok], core.work[:, T:3 * T]
    tmp = core.work[:, T:3 * T]
    step = min(tok, BANK)
    sems = ("squared", "summed", "stat_ready", "rstd_ready", "act_own", "dve_own")
    with core.phase(name, *sems) as (block, squared, summed, stat_ready, rstd_ready, act_own, dve_own):
        @block.scalar
        def _(act):
            own = Chain(act, act_own)
            nc.scalar.preload_act_table_set(EXP_LN)
            for k in range(KT):
                if k == 0:
                    nc.scalar.activation(acc, src[:, 0:tok], ACT.Square).then_inc(squared, 1)
                    continue
                if k >= 3:
                    act.wait_ge(summed, k - 2)
                nc.scalar.activation(sq[:, (k % 2) * T:(k % 2) * T + tok], src[:, k * tok:(k + 1) * tok],
                                     ACT.Square).then_inc(squared, 1)
            act.wait_ge(stat_ready, 1)
            own.link(nc.scalar.activation(core.rstd[:, 0:tok], core.ps[:, 0:tok], ACT.Ln,
                                          bias=eps[:, :], scale=1.0 / D))
            nc.scalar.activation(core.rstd[:, 0:tok], core.rstd[:, 0:tok], ACT.Exp, scale=-0.5).then_inc(rstd_ready, 1)

        @block.vector
        def _(dve):
            own = Chain(dve, dve_own)
            for k in range(1, KT):
                dve.wait_ge(squared, k + 1)
                if k > 1:
                    dve.wait_ge(summed, k - 1)
                nc.vector.tensor_tensor(acc, acc, sq[:, (k % 2) * T:(k % 2) * T + tok], ALU.add).then_inc(summed, 1)
            dve.wait_ge(rstd_ready, 1)
            for k in range(KT):
                part = slice(k * tok, (k + 1) * tok)
                if residual is None:
                    nc.vector.scalar_tensor_tensor(out=dst[:, part], in0=src[:, part], scalar=gain[:, k:k + 1],
                                                   in1=core.rstd[:, 0:tok], op0=ALU.mult, op1=ALU.mult)
                else:
                    t = tmp[:, (k % 2) * T:(k % 2) * T + tok]
                    own.link(nc.vector.scalar_tensor_tensor(out=t, in0=src[:, part], scalar=gain[:, k:k + 1],
                                                            in1=core.rstd[:, 0:tok], op0=ALU.mult, op1=ALU.mult))
                    own.mark(nc.vector.tensor_tensor(residual[:, part], residual[:, part], t, ALU.add))

        @block.tensor
        def _(pe):
            pe.wait_ge(summed, KT - 1)
            for c in range(0, tok, step):
                last = nc.tensor.matmul(core.ps[:, c:c + step], core.ones[:, :], acc[:, c:c + step],
                                        start=True, stop=True)
            last.then_inc(stat_ready, 1)


class Operand:

    SIGNALS = ("hi_made", "src_ready", "squared", "summed", "stat_ready", "rstd_ready", "norm_own")

    def __init__(self, core, src, gain, pair, eps=None, tok=T, tiles=KT):
        self.core, self.nc = core, core.nc
        self.src, self.gain, self.pair, self.eps, self.tok, self.tiles = src, gain, pair, eps, tok, tiles
        self.acc, self.sq = core.work[:, 0:tok], [core.work[:, (1 + n) * T:(1 + n) * T + tok] for n in range(2)]

    def signals(self, sems):
        (self.hi_made, self.src_ready, self.squared, self.summed, self.stat_ready, self.rstd_ready,
         self.norm_own) = sems

    def part(self, k):
        return slice(k * self.tok, (k + 1) * self.tok)

    def act_hi(self, act):
        for k in range(self.tiles):
            scale = 1.0 if self.gain is None else self.gain[:, k:k + 1]
            self.nc.scalar.activation(self.pair[0][:, self.part(k)], self.src[:, self.part(k)], ACT.Copy, scale=scale) \
                .then_inc(self.hi_made, 1)

    def act_squares(self, act):
        for k in range(self.tiles):
            if k >= 3:
                act.wait_ge(self.summed, k - 2)
            self.nc.scalar.activation(self.acc if k == 0 else self.sq[k % 2], self.src[:, self.part(k)], ACT.Square) \
                .then_inc(self.squared, 1)

    def act_rstd(self, act):
        own = Chain(act, self.norm_own)
        rstd = self.core.rstd[:, 0:self.tok]
        self.nc.scalar.preload_act_table_set(EXP_LN)
        act.wait_ge(self.stat_ready, 1)
        own.link(self.nc.scalar.activation(rstd, self.core.ps[:, 6 * BANK:6 * BANK + self.tok], ACT.Ln,
                                           bias=self.eps[:, :], scale=1.0 / (self.tiles * P)))
        self.nc.scalar.activation(rstd, rstd, ACT.Exp, scale=-0.5).then_inc(self.rstd_ready, 1)

    def dve_lo(self, dve):
        for k in range(self.tiles):
            dve.wait_ge(self.hi_made, k + 1)
            hi = self.pair[0][:, self.part(k)].bitcast(F32)
            lo, x = self.pair[1][:, self.part(k)], self.src[:, self.part(k)]
            if self.gain is None:
                ins = self.nc.vector.tensor_tensor(lo, x, hi, ALU.subtract)
            else:
                ins = self.nc.vector.scalar_tensor_tensor(out=lo, in0=x, scalar=self.gain[:, k:k + 1], in1=hi,
                                                          op0=ALU.mult, op1=ALU.subtract)
            ins.then_inc(self.src_ready, 1)

    def dve_sum(self, dve):
        for k in range(1, self.tiles):
            dve.wait_ge(self.squared, k + 1)
            if k > 1:
                dve.wait_ge(self.summed, k - 1)
            self.nc.vector.tensor_tensor(self.acc, self.acc, self.sq[k % 2], ALU.add).then_inc(self.summed, 1)

    def pe_stat(self, pe):
        pe.wait_ge(self.summed, self.tiles - 1)
        step = min(self.tok, BANK)
        for c in range(0, self.tok, step):
            last = self.nc.tensor.matmul(self.core.ps[:, 6 * BANK + c:6 * BANK + c + step], self.core.ones[:, :],
                                         self.acc[:, c:c + step], start=True, stop=True)
        last.then_inc(self.stat_ready, 1)


def split_operand(core, name, src, pair, tok):
    op = Operand(core, src, None, pair, None, tok)
    with core.phase(name, *Operand.SIGNALS) as (block, *sems):
        op.signals(sems)

        @block.scalar
        def _(act):
            op.act_hi(act)

        @block.vector
        def _(dve):
            op.dve_lo(dve)


def norm_operand(core, name, src, gain, eps, pair=None, tok=T):
    op = Operand(core, src, gain, pair or core.h, eps, tok)
    with core.phase(name, *Operand.SIGNALS) as (block, *sems):
        op.signals(sems)

        @block.scalar
        def _(act):
            op.act_squares(act)
            op.act_hi(act)
            op.act_rstd(act)

        @block.vector
        def _(dve):
            op.dve_sum(dve)
            op.dve_lo(dve)

        @block.tensor
        def _(pe):
            op.pe_stat(pe)



def linear(core, name, w, n_tiles, take, pair=None, kts=KT, operand=None, load=None, dmas=(1, 1),
           mid=None, mids=(0, 1), finish=None, raw=None):
    nc = core.nc
    pair = pair or core.h
    load = load or (lambda i, s: plain_views(w, kts, i * (2 * P) + s * P))
    stats = operand is not None and operand.eps is not None
    prod = [core.ps[:, 2 * s * BANK:2 * s * BANK + T] for s in range(2)]
    turns = n_tiles // 2
    ctx = ExitStack()
    wt = Weights(core, name, ctx, kts, raw)
    sems = Weights.SIGNALS + ("taken", "mid_done", "dve_own") + (Operand.SIGNALS if operand else ())
    with core.phase(name, *sems) as (block, *got):
        wt.signals(got[:6])
        taken, mid_done, dve_own = got[6:9]
        if operand:
            operand.signals(got[9:])

        def loop(eng, body):
            for s in range(2):
                body(0, s)
            if turns > 1:
                with eng.Fori(1, turns) as i:
                    for s in range(2):
                        body(i, s)

        @block.sync
        def _(sp):
            loop(sp, lambda i, s: wt.load(sp, i * 2 + s, s, load(i, s)))

        @block.gpsimd
        def _(pool):
            wt.open_raw(pool)
            loop(pool, lambda i, s: wt.split_lo(pool, i * 2 + s, s))

        @block.tensor
        def _(pe):
            wt.open_slots(pe)
            ready = operand.src_ready if operand else None

            def body(i, s):
                if not (isinstance(i, int) and i == 0):
                    pe.wait_ge(taken, i * 2 + (s - 1))
                if stats and isinstance(i, int) and s == 1:
                    wt.product(pe, prod[s], pair, i * 2 + s, s, src_ready=ready, chunks=(0, 1, 2))
                    operand.pe_stat(pe)
                    wt.product(pe, prod[s], pair, i * 2 + s, s, src_ready=ready, chunks=(3,))
                else:
                    wt.product(pe, prod[s], pair, i * 2 + s, s,
                               src_ready=ready if isinstance(i, int) else None)
            loop(pe, body)

        @block.scalar
        def _(act):
            def middle(i, s):
                if mid and s in mids:
                    act.wait_ge(taken, i * 2 + (s + 1))
                    mid(act, i, s).then_inc(mid_done, 1)

            wt.split_hi(act, 0, 0, dmas)
            if operand:
                operand.act_hi(act)
            wt.split_hi(act, 1, 1, dmas)
            if stats:
                operand.act_squares(act)
                operand.act_rstd(act)
            middle(0, 0)
            if turns > 1:
                with act.Fori(1, turns) as i:
                    wt.split_hi(act, i * 2, 0, dmas)
                    middle(i - 1, 1)
                    wt.split_hi(act, i * 2 + 1, 1, dmas)
                    middle(i, 0)
            middle(turns - 1, 1)

        @block.vector
        def _(dve):
            if operand:
                operand.dve_lo(dve)
                if stats:
                    operand.dve_sum(dve)
                    dve.wait_ge(operand.rstd_ready, 1)

            def body(i, s):
                own = Chain(dve, dve_own)
                wt.wait_product(dve, i * 2 + s)
                own.link(take(dve, own, i, s, prod[s]))
                dve.sem_inc(taken, 1)
                if mid and (s == 1 or len(mids) == 2):
                    dve.wait_ge(mid_done, i * len(mids) + (s + 1 if len(mids) == 2 else 1))
                if finish:
                    finish(dve, own, i, s)
                own.restart()
            loop(dve, body)
    ctx.close()


def add_to(nc, dst):
    def take(dve, own, i, s, product):
        part = cols(dst, i * (2 * T) + s * T)
        return nc.vector.tensor_tensor(part, part, product, ALU.add)
    return take


def copy_to(nc, dst, at=0):
    def take(dve, own, i, s, product):
        return nc.vector.tensor_copy(cols(dst, i * (2 * T) + (s * T + at)), product)
    return take


def scale_to(core, dst, at=0):
    def take(dve, own, i, s, product):
        return core.nc.vector.tensor_tensor(cols(dst, i * (2 * T) + (s * T + at)), product, core.rstd[:, :], ALU.mult)
    return take

HEADS = 4
HD = 128
DIFF = 512
LAMBDA_INIT = 0.8 - 0.6 * math.exp(-0.3 * 0)
RET_K_SCALE = HD ** -0.5
FF1 = 4096
FT1 = FF1 // P
MASKED = -1e30


def lambda_phase(core, lam_in, out):
    nc = core.nc
    n = 64
    vec, prod, sc = core.work[:, 0:4 * n], core.work[:, 4 * n:6 * n], core.work[:, 6 * n:6 * n + 8]
    with core.phase("lam", "loaded", "dotted", "exped", "dve_own") as (block, loaded, dotted, exped, dve_own):
        @block.sync
        def _(sp):
            for j, v in enumerate(lam_in):
                sp.dma_start(vec[:, j * n:(j + 1) * n], v.to_broadcast([P, n])).then_inc(loaded, 16)

        @block.vector
        def _(dve):
            own = Chain(dve, dve_own)
            dve.wait_ge(loaded, 64)
            for j in range(2):
                own.mark(nc.vector.tensor_tensor(prod[:, j * n:(j + 1) * n], vec[:, 2 * j * n:(2 * j + 1) * n],
                                                 vec[:, (2 * j + 1) * n:(2 * j + 2) * n], ALU.mult))
            own.join()
            for j in range(2):
                nc.vector.reduce_sum(sc[:, j:j + 1], prod[:, j * n:(j + 1) * n], axis=AX.X).then_inc(dotted, 1)
            dve.wait_ge(exped, 1)
            own.link(nc.vector.tensor_tensor(sc[:, 4:5], sc[:, 3:4], sc[:, 2:3], ALU.subtract))
            nc.vector.tensor_scalar(out, sc[:, 4:5], -LAMBDA_INIT, None, ALU.add)

        @block.scalar
        def _(act):
            act.wait_ge(dotted, 2)
            nc.scalar.activation(sc[:, 2:4], sc[:, 0:2], ACT.Exp).then_inc(exped, 1)


def diff_attention(core, w, c_in, mix, diff_gain, neg_lam, slopes):
    nc, h = core.nc, core.h
    with ExitStack() as ctx:
        sb = lambda n, shape: core.sbuf("da_" + n, shape, ctx)
        wt = Weights(core, "da", ctx)
        qT, kT, vT = core.work[:, T:2 * T], sb("kT", [P, T]), core.work[:, 2 * T:3 * T]
        v_tok = sb("v_tok", [P, T])
        dist = sb("dist", [P, T])
        probs = sb("probs", [P, 3 * 2 * T])
        aT = sb("aT", [P, 2 * T])
        col = sb("col", [P, 2 * 8])
        oT, sq, hrstd = core.work[:, 0:T], qT, core.work[:, 3 * T:4 * T]
        sems = Weights.SIGNALS + ("const", "q_k_v_ready", "v_turned", "v_ready", "scores_ready",
                "scores_taken", "max_ready", "exp_ready", "a_ready", "a_turned", "aT_ready", "pv_done",
                "o_ready", "sq_ready", "stat_ready", "rstd_ready", "head_done", "dve_own", "act_own")
        with core.phase("da", *sems) as (
                block, *ws, const, qkv_ready, v_turned, v_ready, scores_ready,
                scores_taken, max_ready, exp_ready, a_ready, a_turned, aT_ready, pv_done,
                o_ready, sq_ready, stat_ready, rstd_ready, head_done, dve_own, act_own):
            wt.signals(ws)
            C = lambda q, what, m: col[:, (q % 2) * 8 + 2 * what + m:(q % 2) * 8 + 2 * what + m + 1]

            @block.sync
            def _(sp):
                sp.dma_start(dist[:, :], c_in["dist"]).then_inc(const, 16)
                with sp.Fori(0, HEADS) as i:
                    for j in range(3):
                        wt.load(sp, i * 3 + j, 0, plain_views(w, KT, i * HD + j * DIFF))

            @block.gpsimd
            def _(pool):
                wt.open_raw(pool)
                with pool.Fori(0, HEADS) as i:
                    for j in range(3):
                        wt.split(pool, i * 3 + j, 0)

            @block.tensor
            def _(pe):
                wt.open_slots(pe)

                def scores(i, q):
                    if q >= 1:
                        pe.wait_ge(scores_taken, i * 8 + q)
                    width = (q + 1) * P
                    for m in range(2):
                        for c in range(0, width, BANK):
                            n = min(BANK, width - c)
                            last = nc.tensor.matmul(core.bank(4 + 2 * m, n, c), qT[64 * m:64 * m + 64, q * P:(q + 1) * P],
                                                    kT[64 * m:64 * m + 64, c:c + n], start=True, stop=True)
                    last.then_inc(scores_ready, 1)

                def weigh(i, q):
                    pe.wait_ge(aT_ready, i * 8 + (q + 1))
                    for t in range(q + 1):
                        at = (q % 2) * T + t * P
                        last = nc.tensor.matmul(core.bank(2, P, q * P), v_tok[:, t * P:(t + 1) * P], aT[:, at:at + P],
                                                start=(t == 0), stop=(t == q))
                    last.then_inc(pv_done, 1)

                with pe.Fori(0, HEADS) as i:
                    for j in range(3):
                        if j == 2:
                            pe.wait_ge(qkv_ready, i * 3 + 1)
                        wt.product(pe, core.bank(2 * (j % 2), T), h, i * 3 + j, 0)
                    pe.wait_ge(qkv_ready, i * 3 + 3)
                    for t in range(TT):
                        last = nc.tensor.transpose(core.bank(2, P, t * P), vT[:, t * P:(t + 1) * P], core.ident[:, :])
                    last.then_inc(v_turned, 1)
                    scores(i, 0)
                    pe.wait_ge(v_ready, i + 1)
                    scores(i, 1)
                    for q in range(TT):
                        if q + 2 < TT:
                            scores(i, q + 2)
                        pe.wait_ge(a_ready, i * 8 + (q + 1))
                        if q >= 1:
                            pe.wait_ge(aT_ready, i * 8 + q)
                        for t in range(q + 1):
                            at = (q % 3) * 2 * T + t * P
                            last = nc.tensor.transpose(core.bank(0, P, t * P), probs[:, at:at + P], core.ident[:, :])
                        last.then_inc(a_turned, 1)
                        if q >= 1:
                            weigh(i, q - 1)
                    weigh(i, TT - 1)
                    pe.wait_ge(sq_ready, i + 1)
                    for c in range(0, T, BANK):
                        last = nc.tensor.matmul(core.bank(4, BANK, c), core.ones[:, :], sq[:, c:c + BANK],
                                                start=True, stop=True)
                    last.then_inc(stat_ready, 1)

            @block.scalar
            def _(act):
                with act.Fori(0, HEADS) as i:
                    own = Chain(act, act_own)
                    nc.scalar.preload_act_table_set(EXP_LN)
                    act.wait_ge(v_turned, i + 1)
                    nc.scalar.activation(v_tok[:, :], core.bank(2, T), ACT.Identity).then_inc(v_ready, 1)
                    def turned(q):
                        act.wait_ge(a_turned, i * 8 + (q + 1))
                        if q >= 2:
                            act.wait_ge(pv_done, i * 8 + (q - 1))
                        nc.scalar.activation(aT[:, (q % 2) * T:(q % 2) * T + (q + 1) * P], core.bank(0, (q + 1) * P),
                                             ACT.Identity).then_inc(aT_ready, 1)
                    for q in range(TT):
                        for m in range(2):
                            act.wait_ge(max_ready, i * 16 + (2 * q + m + 1))
                            s = probs[:, ((q % 3) * 2 + m) * T:((q % 3) * 2 + m) * T + (q + 1) * P]
                            nc.scalar.activation(s, s, ACT.Exp, bias=C(q, 0, m),
                                                 accum_out=C(q, 1, m)).then_inc(exp_ready, 1)
                        if q >= 1:
                            turned(q - 1)
                    turned(TT - 1)
                    act.wait_ge(pv_done, i * 8 + TT)
                    own.link(nc.scalar.activation(oT, core.bank(2, T), ACT.Identity))
                    nc.scalar.activation(sq, oT, ACT.Square).then_inc(sq_ready, 1)
                    act.wait_ge(stat_ready, i + 1)
                    own.link(nc.scalar.activation(hrstd, core.bank(4, T), ACT.Ln, bias=core.eps5[:, :],
                                                  scale=1.0 / HD))
                    nc.scalar.activation(hrstd, hrstd, ACT.Exp, scale=-0.5).then_inc(rstd_ready, 1)
                    own.restart()

            @block.vector
            def _(dve):
                dve.wait_ge(const, 16)
                with dve.Fori(0, HEADS) as i:
                    own = Chain(dve, dve_own)
                    def soft(q):
                        width = (q + 1) * P
                        dve.wait_ge(scores_ready, i * 8 + (q + 1))
                        if q >= 3:
                            dve.wait_ge(a_turned, i * 8 + (q - 2))
                        for m in range(2):
                            s = probs[:, ((q % 3) * 2 + m) * T:((q % 3) * 2 + m) * T + width]
                            own.mark(nc.vector.scalar_tensor_tensor(
                                out=s, in0=dist[:, T - width:T], scalar=cols(slopes, i, 1),
                                in1=core.bank(4 + 2 * m, width), op0=ALU.mult, op1=ALU.add))
                        own.join()
                        dve.sem_inc(scores_taken, 1)
                        for m in range(2):
                            s = probs[:, ((q % 3) * 2 + m) * T:((q % 3) * 2 + m) * T + width]
                            nc.vector.tensor_reduce(out=C(q, 0, m), in_=s, axis=AX.X, op=ALU.max,
                                                    negate=True).then_inc(max_ready, 1)

                    def combine(q):
                        width = (q + 1) * P
                        dve.wait_ge(exp_ready, i * 16 + (2 * q + 2))
                        s0 = probs[:, (q % 3) * 2 * T:(q % 3) * 2 * T + width]
                        s1 = probs[:, ((q % 3) * 2 + 1) * T:((q % 3) * 2 + 1) * T + width]
                        own.link(nc.vector.reciprocal(col[:, (q % 2) * 8 + 4:(q % 2) * 8 + 6],
                                                      col[:, (q % 2) * 8 + 2:(q % 2) * 8 + 4]))
                        own.mark(nc.vector.tensor_tensor(C(q, 3, 0), C(q, 2, 1), neg_lam, ALU.mult))
                        own.mark(nc.vector.tensor_scalar(s0, s0, C(q, 2, 0), None, ALU.mult))
                        own.join()
                        nc.vector.scalar_tensor_tensor(out=s0, in0=s1, scalar=C(q, 3, 0), in1=s0,
                                                       op0=ALU.mult, op1=ALU.add).then_inc(a_ready, 1)

                    for j, (dst, scale) in enumerate(((qT, 64 ** -0.5), (kT[:, :], 1.0), (vT, 1.0))):
                        wt.wait_product(dve, i * 3 + j)
                        own.link(nc.vector.scalar_tensor_tensor(out=dst, in0=core.bank(2 * (j % 2), T), scalar=scale,
                                                                in1=core.rstd[:, :], op0=ALU.mult, op1=ALU.mult))
                        dve.sem_inc(qkv_ready, 1)
                    soft(0)
                    for q in range(TT):
                        if q + 1 < TT:
                            soft(q + 1)
                        combine(q)
                    dve.wait_ge(rstd_ready, i + 1)
                    own.link(nc.vector.scalar_tensor_tensor(out=cols(mix, i * T), in0=oT, scalar=diff_gain,
                                                            in1=hrstd, op0=ALU.mult, op1=ALU.mult))
                    dve.sem_inc(head_done, 1)
                    own.restart()


def retention(core, w, c_in, mix, gain):
    nc, h = core.nc, core.h
    first = 3 * DIFF
    with ExitStack() as ctx:
        sb = lambda n, shape: core.sbuf("re_" + n, shape, ctx)
        wt = Weights(core, "re", ctx)
        qT, kT, gT = (sb(n, [P, T]) for n in ("qT", "kT", "gT"))
        vT = core.work[:, 2 * T:3 * T]
        qd = sb("q_decayed", [P, T])
        k_tok, v_tok, intra = sb("k_tok", [P, T]), sb("v_tok", [P, T]), sb("intra", [P, T])
        state = sb("state", [P, T])
        mask = sb("mask", [P, HEADS * P])
        qdec = sb("qdec", [P, HEADS * P])
        kdec = sb("kdec", [P, 2 * HEADS])
        oT, sq, hrstd = core.work[:, 0:T], core.work[:, T:2 * T], core.work[:, 3 * T:4 * T]
        sems = Weights.SIGNALS + ("const", "q_ready", "turned", "kv_ready", "intra_ready",
                "intra_masked", "update_ready", "state_ready", "o_done", "sq_ready", "stat_ready",
                "rstd_ready", "dve_own", "act_own", "mix_done", "v_ready", "silu_done")
        with core.phase("re", *sems) as (
                block, *ws, const, q_ready, turned, kv_ready, intra_ready,
                intra_masked, update_ready, state_ready, o_done, sq_ready, stat_ready,
                rstd_ready, dve_own, act_own, mix_done, v_ready, silu_done):
            wt.signals(ws)

            @block.sync
            def _(sp):
                for dst, name in ((mask, "ret_mask"), (qdec, "ret_qdec"), (kdec, "ret_kdec")):
                    sp.dma_start(dst[:, :], c_in[name]).then_inc(const, 16)
                with sp.Fori(0, HEADS) as i:
                    for j in range(4):
                        wt.load(sp, i * 4 + j, 0, plain_views(w, KT, i * HD + (first + j * DIFF)))

            @block.gpsimd
            def _(pool):
                wt.open_raw(pool)
                with pool.Fori(0, HEADS) as i:
                    for j in range(4):
                        wt.split(pool, i * 4 + j, 0)

            @block.tensor
            def _(pe):
                wt.open_slots(pe)
                with pe.Fori(0, HEADS) as i:
                    for j in range(4):
                        if j >= 2:
                            pe.wait_ge(q_ready, i * 4 + (j - 1))
                        wt.product(pe, core.bank(2 * (j % 2), T), h, i * 4 + j, 0)
                    pe.wait_ge(q_ready, i * 4 + 3)
                    for src, b in ((kT, 4), (vT, 6)):
                        for c in range(TT):
                            last = nc.tensor.transpose(core.bank(b, P, c * P), src[:, c * P:(c + 1) * P], core.ident[:, :])
                        last.then_inc(turned, 1)
                    pe.wait_ge(q_ready, i * 4 + 4)
                    for c in range(TT):
                        last = nc.tensor.matmul(core.bank(0, P, c * P), kT[:, c * P:(c + 1) * P], qT[:, c * P:(c + 1) * P],
                                                start=True, stop=True)
                    last.then_inc(intra_ready, 1)
                    pe.wait_ge(kv_ready, i + 1)
                    pe.wait_ge(v_ready, i + 1)
                    for c in range(TT - 1):
                        last = nc.tensor.matmul(core.bank(2, P, c * P), k_tok[:, c * P:(c + 1) * P],
                                                v_tok[:, c * P:(c + 1) * P], start=True, stop=True)
                    last.then_inc(update_ready, 1)
                    pe.wait_ge(intra_masked, i + 1)
                    pe.wait_ge(state_ready, i + 1)
                    for c in range(TT):
                        last = nc.tensor.matmul(core.bank(4, P, c * P), v_tok[:, c * P:(c + 1) * P],
                                                intra[:, c * P:(c + 1) * P], start=True, stop=(c == 0))
                        if c:
                            last = nc.tensor.matmul(core.bank(4, P, c * P), state[:, c * P:(c + 1) * P],
                                                    qd[:, c * P:(c + 1) * P], start=False, stop=True)
                    last.then_inc(o_done, 1)
                    pe.wait_ge(sq_ready, i + 1)
                    for c in range(0, T, BANK):
                        last = nc.tensor.matmul(core.bank(6, BANK, c), core.ones[:, :], sq[:, c:c + BANK],
                                                start=True, stop=True)
                    last.then_inc(stat_ready, 1)

            @block.scalar
            def _(act):
                with act.Fori(0, HEADS) as i:
                    own = Chain(act, act_own)
                    nc.scalar.preload_act_table_set(SILU)
                    act.wait_ge(q_ready, i * 4 + 4)
                    nc.scalar.activation(gT[:, :], gT[:, :], ACT.Silu).then_inc(silu_done, 1)
                    act.wait_ge(turned, i * 2 + 2)
                    nc.scalar.activation(v_tok[:, :], core.bank(6, T), ACT.Identity).then_inc(v_ready, 1)
                    nc.scalar.preload_act_table_set(EXP_LN)
                    act.wait_ge(o_done, i + 1)
                    own.link(nc.scalar.activation(oT, core.bank(4, T), ACT.Identity))
                    nc.scalar.activation(sq, oT, ACT.Square).then_inc(sq_ready, 1)
                    act.wait_ge(stat_ready, i + 1)
                    own.link(nc.scalar.activation(hrstd, core.bank(6, T), ACT.Ln, bias=core.eps5[:, :],
                                                  scale=1.0 / HD))
                    own.link(nc.scalar.activation(hrstd, hrstd, ACT.Exp, scale=-0.5))
                    act.sem_inc(rstd_ready, 1)
                    own.restart()
                    act.wait_ge(mix_done, i + 1)

            @block.vector
            def _(dve):
                dve.wait_ge(const, 48)
                nc.vector.memset(state[:, 0:P], 0.0)
                with dve.Fori(0, HEADS) as i:
                    own = Chain(dve, dve_own)
                    v3 = lambda b: b[:, 0:T].rearrange("p (c n) -> p c n", n=P)
                    for j, dst in enumerate((qT, kT, vT, gT)):
                        wt.wait_product(dve, i * 4 + j)
                        own.link(nc.vector.tensor_tensor(dst[:, :], core.bank(2 * (j % 2), T), core.rstd[:, :], ALU.mult))
                        dve.sem_inc(q_ready, 1)
                    own.mark(nc.vector.tensor_tensor(
                        v3(qd), v3(qT), cols(qdec, i * P, P).unsqueeze(1).to_broadcast([P, TT, P]), ALU.mult))
                    dve.wait_ge(turned, i * 2 + 1)
                    own.mark(nc.vector.tensor_scalar(k_tok[:, :], core.bank(4, T), cols(kdec, i, 1), None, ALU.mult))
                    own.join()
                    dve.sem_inc(kv_ready, 1)
                    dve.wait_ge(intra_ready, i + 1)
                    for b in range(2):
                        own.mark(nc.vector.tensor_tensor(
                            intra[:, b * BANK:(b + 1) * BANK].rearrange("p (c n) -> p c n", n=P),
                            core.bank(b).rearrange("p (c n) -> p c n", n=P),
                            cols(mask, i * P, P).unsqueeze(1).to_broadcast([P, BANK // P, P]), ALU.mult))
                    own.join()
                    dve.sem_inc(intra_masked, 1)
                    dve.wait_ge(update_ready, i + 1)
                    for c in range(TT - 1):
                        own.link(nc.vector.scalar_tensor_tensor(
                            out=state[:, (c + 1) * P:(c + 2) * P], in0=state[:, c * P:(c + 1) * P],
                            scalar=cols(kdec, i + HEADS, 1), in1=core.bank(2, P, c * P), op0=ALU.mult, op1=ALU.add))
                    dve.sem_inc(state_ready, 1)
                    dve.wait_ge(rstd_ready, i + 1)
                    dve.wait_ge(silu_done, i + 1)
                    own.link(nc.vector.scalar_tensor_tensor(out=sq, in0=oT, scalar=cols(gain, i, 1),
                                                            in1=hrstd, op0=ALU.mult, op1=ALU.mult))
                    own.link(nc.vector.tensor_tensor(cols(mix, i * T + HEADS * T), sq, gT[:, :], ALU.mult))
                    dve.sem_inc(mix_done, 1)
                    own.restart()


def squared_relu_ffn(core, w_up, w_down, gain):
    nc = core.nc
    with ExitStack() as ctx:
        up = tuple(core.sbuf(f"ff_up_{p}", [P, KT * T], ctx, F32R) for p in ("hi", "lo"))
        row = [core.work[:, 3 * T:4 * T], core.sbuf("ff_row", [P, T], ctx)[:, :]]

        def rectified_square(dve, own, i, s, product):
            return nc.vector.tensor_tensor(row[s], product, core.rstd[:, :], ALU.mult)

        def split(dve, own, i, s):
            own.link(nc.vector.scalar_tensor_tensor(out=row[s], in0=row[s], scalar=0.0, in1=row[s],
                                                    op0=ALU.max, op1=ALU.mult))
            hi, lo = (cols(u, i * (2 * T) + s * T) for u in up)
            own.link(nc.vector.tensor_copy(hi, row[s]))
            own.link(nc.vector.tensor_tensor(lo, row[s], hi.bitcast(F32), ALU.subtract))

        for n in range(FT1 // KT):
            linear(core, f"up{n}", w_up[:, n * D:(n + 1) * D], KT, rectified_square, mids=(0, 1), finish=split,
                   operand=Operand(core, core.x, gain, core.h, core.eps5) if n == 0 else None)
            linear(core, f"down{n}", w_down[n * D:(n + 1) * D, :], KT, add_to(nc, core.x), pair=up)


def first_block(core, a, c_in, g):
    nc = core.nc
    norm_operand(core, "n1", core.x, g["norm1_g"], core.eps5)
    lambda_phase(core, [a[n] for n in ("lambda_q1", "lambda_k1", "lambda_q2", "lambda_k2")], g["neg_lam"])
    with ExitStack() as ctx:
        mix = core.sbuf("mix1", [P, KT * T], ctx)
        diff_attention(core, a["w_in"][0], c_in, mix, g["diff_norm_g"], g["neg_lam"], g["slopes"])
        retention(core, a["w_in"][0], c_in, mix, g["ret_norm_g"])
        linear(core, "out1", a["w_out"][0], KT, add_to(nc, core.x), operand=Operand(core, mix, None, core.h))
    squared_relu_ffn(core, a["w_up"][0], a["w_down"][0], g["norm2_g"])
    rms_norm(core, "nf1", core.x, g["final_norm_g"], core.x, core.eps5)

GW = 256
COLS_W, ROWS = 64, T // 64
NA_H, NA_D, NA_KR, NA_KC = 8, 32, 8, 16
BAND = NA_KR * COLS_W
REL_R, REL_C = 2 * NA_KR - 1, 2 * NA_KC - 1
RPB_PAD = COLS_W - NA_KC
RPB_W = REL_C + 2 * RPB_PAD
CONV = 31
POOL_WINDOWS = (2, 4, 8, 16)
PADC = CONV // 2
POOL_PAD = 16
QKV2 = dict(q=0, k=2, v=4)
REST2 = dict(pool=0, u=2, v_gate=4)
CONV_STEP = 5


def second_gains(core, a, c_in, g, column, by_tile):
    column("norm_g_2", by_tile(a["norm_g_2"][0]), KT)
    column("final_g_2", by_tile(a["final_g_2"]), KT)
    for name in ("conv_dw_b_2", "conv_ln_g_2", "conv_ln_b_2", "pool_scale_2", "sgu_ln_g_2", "sgu_ln_b_2"):
        column(name, by_tile(a[name][0]), 2)


def row_start(r):
    return min(max(r - NA_KR // 2, 0), ROWS - NA_KR)


def neighbourhood_attention(core, c_in, rpb, z, mix):
    nc = core.nc
    with ExitStack() as ctx:
        sb = lambda n, shape: core.sbuf("na_" + n, shape, ctx)
        qbd = sb("q_blockdiag", [P, ROWS * P])
        raw = mix[:, 4 * T:4 * T + REL_R * COLS_W]
        bias = sb("bias", [P, 2 * REL_R * COLS_W])
        probs, pT = mix[:, 5 * T:5 * T + 2 * BAND], mix[:, 6 * T:6 * T + 2 * BAND]
        flip, edge = sb("flip", [P, P]), sb("edge", [P, COLS_W])
        col = sb("col", [P, 2 * 4])
        kS, vS = core.work[:, 0:T], core.work[:, T:2 * T]
        v_al, v_sh = mix[:, 2 * T:3 * T], mix[:, 3 * T:4 * T]
        n_bias = REL_R * COLS_W
        units = [(p, r) for p in range(2) for r in range(ROWS)]
        U = len(units)
        sems = ("const", "raw_loaded", "staged", "flipped", "bias_ready", "v_turned", "v_ready", "scores_ready",
                "max_ready", "exp_ready", "p_ready", "p_turned", "pT_ready", "pv_done", "out_taken", "dve_own")
        with core.phase("na", *sems) as (
                block, const, raw_loaded, staged, flipped, bias_ready, v_turned, v_ready, scores_ready,
                max_ready, exp_ready, p_ready, p_turned, pT_ready, pv_done, out_taken, dve_own):

            def raw_view(i, pair):
                head = REL_R * RPB_W
                return [bass.AP(tensor=rpb.tensor, offset=i * (4 * head) + (2 * pair + hh) * head,
                                ap=[[1, COLS_W], [RPB_W, REL_R], [1, COLS_W]]) for hh in range(2)]

            @block.sync
            def _(sp):
                sp.dma_start(flip[:, :], c_in["flip"]).then_inc(const, 16)
                sp.dma_start(edge[:, :], c_in["edge"]).then_inc(const, 16)
                with sp.Fori(0, 2) as i:
                    for pair in range(2):
                        sp.wait_ge(flipped, i * 2 + (pair + 1))
                        for hh, view in enumerate(raw_view(i, pair)):
                            sp.dma_start(raw[hh * COLS_W:(hh + 1) * COLS_W, :].rearrange("p (r c) -> p r c", c=COLS_W),
                                         view).then_inc(raw_loaded, 16)

            @block.tensor
            def _(pe):
                pe.wait_ge(const, 32)
                pe.sem_inc(flipped, 1)
                def score(i, n):
                    p, r = units[n]
                    s0 = row_start(r) * COLS_W
                    if n >= 2:
                        pe.wait_ge(max_ready, i * U + (n - 1))
                    nc.tensor.matmul(core.bank(n % 2), qbd[64 * p:64 * p + 64, r * P:(r + 1) * P],
                                     kS[64 * p:64 * p + 64, s0:s0 + BAND], start=True, stop=True).then_inc(scores_ready, 1)
                def weigh(i, n):
                    p, r = units[n]
                    s0 = row_start(r)
                    v, first = (v_al, s0 // 2) if s0 % 2 == 0 else (v_sh, (s0 - 1) // 2)
                    pe.wait_ge(pT_ready, i * U + (n + 1))
                    for c in range(BAND // P):
                        vt = v[:, (first + c) * P + 64 * p:(first + c) * P + 64 * p + 64]
                        last = nc.tensor.matmul(core.ps[64 * p:64 * p + 64, 4 * BANK + r * P:4 * BANK + (r + 1) * P],
                                                vt, pT[:, (n % 2) * BAND + c * P:(n % 2) * BAND + (c + 1) * P],
                                                start=(c == 0), stop=(c == BAND // P - 1))
                    last.then_inc(pv_done, 1)
                with pe.Fori(0, 2) as i:
                    for pair in range(2):
                        pe.wait_ge(raw_loaded, i * 64 + (pair + 1) * 32)
                        if pair == 1:
                            pe.wait_ge(bias_ready, i * 2 + 1)
                        for at in range(0, n_bias, 480):
                            last = nc.tensor.matmul(core.bank(at // 480, 480), flip[:, :], raw[:, at:at + 480],
                                                    start=True, stop=True)
                        last.then_inc(flipped, 1)
                    pe.wait_ge(staged, i + 1)
                    for t in range(TT):
                        last = nc.tensor.transpose(core.bank(4, P, t * P), vS[:, t * P:(t + 1) * P], core.ident[:, :])
                    for t in range(TT - 1):
                        last = nc.tensor.transpose(core.bank(6, P, t * P), vS[:, t * P + 64:(t + 1) * P + 64],
                                                   core.ident[:, :])
                    last.then_inc(v_turned, 1)
                    pe.wait_ge(bias_ready, i * 2 + 2)
                    score(i, 0)
                    score(i, 1)
                    pe.wait_ge(v_ready, i + 1)
                    for n in range(U):
                        if n + 2 < U:
                            score(i, n + 2)
                        pe.wait_ge(p_ready, i * U + (n + 1))
                        if n >= 2:
                            pe.wait_ge(pT_ready, i * U + (n - 1))
                        for c in range(BAND // P):
                            last = nc.tensor.transpose(core.bank(2 + n % 2, P, c * P),
                                                       probs[:, (n % 2) * BAND + c * P:(n % 2) * BAND + (c + 1) * P],
                                                       core.ident[:, :])
                        last.then_inc(p_turned, 1)
                        if n >= 1:
                            weigh(i, n - 1)
                    weigh(i, U - 1)
                    pe.wait_ge(out_taken, i + 1)

            @block.scalar
            def _(act):
                with act.Fori(0, 2) as i:
                    nc.scalar.preload_act_table_set(EXP_LN)
                    act.wait_ge(v_turned, i + 1)
                    nc.scalar.activation(v_al, core.bank(4, T), ACT.Identity)
                    nc.scalar.activation(v_sh[:, 0:T - P], core.bank(6, T - P), ACT.Identity).then_inc(v_ready, 1)
                    def turned(n):
                        act.wait_ge(p_turned, i * U + (n + 1))
                        if n >= 2:
                            act.wait_ge(pv_done, i * U + (n - 1))
                        nc.scalar.activation(pT[:, (n % 2) * BAND:(n % 2 + 1) * BAND], core.bank(2 + n % 2),
                                             ACT.Identity).then_inc(pT_ready, 1)
                    for n in range(U):
                        act.wait_ge(max_ready, i * U + (n + 1))
                        s, c = probs[:, (n % 2) * BAND:(n % 2 + 1) * BAND], (n % 2) * 4
                        nc.scalar.activation(s, s, ACT.Exp, bias=col[:, c:c + 1], accum_out=col[:, c + 1:c + 2]) \
                            .then_inc(exp_ready, 1)
                        if n >= 1:
                            turned(n - 1)
                    turned(U - 1)

            @block.vector
            def _(dve):
                dve.wait_ge(const, 32)
                zeroed = Chain(dve, dve_own)
                zeroed.mark(nc.vector.memset(qbd[:, :], 0.0))
                zeroed.restart()
                with dve.Fori(0, 2) as i:
                    own = Chain(dve, dve_own)
                    for g in range(4):
                        rows = slice(32 * g, 32 * g + 32)
                        own.mark(nc.vector.tensor_scalar(
                            qbd[rows, :].rearrange("p (r n) -> p r n", n=P)[:, :, (g % 2) * 64:(g % 2) * 64 + 64],
                            z[rows, ds(i * T, T)].rearrange("p (r n) -> p r n", n=COLS_W),
                            NA_D ** -0.5, None, ALU.mult))
                    own.mark(nc.vector.tensor_copy(kS, cols(z, i * T + QKV2["k"] * T)))
                    own.mark(nc.vector.tensor_copy(vS, cols(z, i * T + QKV2["v"] * T)))
                    own.join()
                    dve.sem_inc(staged, 1)
                    for pair in range(2):
                        dve.wait_ge(flipped, i * 2 + (pair + 2))
                        for at in range(0, n_bias, 480):
                            own.mark(nc.vector.tensor_copy(bias[:, pair * n_bias + at:pair * n_bias + at + 480],
                                                           core.bank(at // 480, 480)))
                        own.join()
                        dve.sem_inc(bias_ready, 1)
                        b = bias[:, pair * n_bias:(pair + 1) * n_bias].rearrange("p (r c) -> p r c", c=COLS_W)
                        own.link(nc.vector.tensor_tensor(b, b, edge[:, :].unsqueeze(1).to_broadcast([P, REL_R, COLS_W]),
                                                         ALU.add))

                    def soft(n):
                        p, r = units[n]
                        off = (row_start(r) - r + NA_KR - 1) * COLS_W + p * n_bias
                        s, c = probs[:, (n % 2) * BAND:(n % 2 + 1) * BAND], (n % 2) * 4
                        dve.wait_ge(scores_ready, i * U + (n + 1))
                        if n >= 2:
                            dve.wait_ge(p_turned, i * U + (n - 1))
                        own.link(nc.vector.tensor_tensor(s, core.bank(n % 2), bias[:, off:off + BAND], ALU.add))
                        nc.vector.tensor_reduce(out=col[:, c:c + 1], in_=s, axis=AX.X, op=ALU.max,
                                                negate=True).then_inc(max_ready, 1)

                    def divide(n):
                        s, c = probs[:, (n % 2) * BAND:(n % 2 + 1) * BAND], (n % 2) * 4
                        dve.wait_ge(exp_ready, i * U + (n + 1))
                        own.link(nc.vector.reciprocal(col[:, c + 2:c + 3], col[:, c + 1:c + 2]))
                        nc.vector.tensor_scalar(s, s, col[:, c + 2:c + 3], None, ALU.mult).then_inc(p_ready, 1)

                    soft(0)
                    for n in range(U):
                        if n + 1 < U:
                            soft(n + 1)
                        divide(n)
                    dve.wait_ge(pv_done, i * U + U)
                    for g in range(4):
                        rows = slice(32 * g, 32 * g + 32)
                        own.mark(nc.vector.tensor_copy(
                            mix[rows, ds(i * T, T)].rearrange("p (r n) -> p r n", n=COLS_W),
                            core.ps[rows, 4 * BANK:8 * BANK].rearrange("p (r n) -> p r n", n=P)[
                                :, :, (g % 2) * 64:(g % 2) * 64 + 64]))
                    own.join()
                    dve.sem_inc(out_taken, 1)
                    own.restart()


def layer_norm(core, name, src, gain, bias, dst, func, eps):
    nc = core.nc
    sq, rstd = core.work[:, 0:2 * T], core.work[:, 2 * T:3 * T]
    sems = ("summed", "centred", "squared", "var_ready", "rstd_ready", "scaled", "dve_own", "act_own")
    with core.phase(name, *sems) as (block, summed, centred, squared, var_ready, rstd_ready, scaled, dve_own, act_own):
        @block.tensor
        def _(pe):
            def total(rows, bank):
                for c in range(0, T, BANK):
                    for k in range(2):
                        last = nc.tensor.matmul(core.bank(bank, BANK, c), core.ones[:, :],
                                                rows[:, k * T + c:k * T + c + BANK], start=(k == 0), stop=(k == 1))
                return last
            total(src, 0).then_inc(summed, 1)
            pe.wait_ge(squared, 2)
            total(sq, 2).then_inc(var_ready, 1)

        @block.vector
        def _(dve):
            own = Chain(dve, dve_own)
            dve.wait_ge(summed, 1)
            for k in range(2):
                own.link(nc.vector.scalar_tensor_tensor(out=src[:, k * T:(k + 1) * T], in0=core.bank(0, T),
                                                        scalar=-1.0 / GW, in1=src[:, k * T:(k + 1) * T],
                                                        op0=ALU.mult, op1=ALU.add))
                dve.sem_inc(centred, 1)
            dve.wait_ge(rstd_ready, 1)
            for k in range(2):
                nc.vector.scalar_tensor_tensor(out=sq[:, k * T:(k + 1) * T], in0=src[:, k * T:(k + 1) * T],
                                               scalar=gain[:, k:k + 1], in1=rstd, op0=ALU.mult,
                                               op1=ALU.mult).then_inc(scaled, 1)

        @block.scalar
        def _(act):
            own = Chain(act, act_own)
            nc.scalar.preload_act_table_set(EXP_LN)
            for k in range(2):
                act.wait_ge(centred, k + 1)
                nc.scalar.activation(sq[:, k * T:(k + 1) * T], src[:, k * T:(k + 1) * T], ACT.Square).then_inc(squared, 1)
            act.wait_ge(var_ready, 1)
            own.link(nc.scalar.activation(rstd, core.bank(2, T), ACT.Ln, bias=eps[:, :], scale=1.0 / GW))
            nc.scalar.activation(rstd, rstd, ACT.Exp, scale=-0.5).then_inc(rstd_ready, 1)
            for k in range(2):
                act.wait_ge(scaled, k + 1)
                nc.scalar.activation(dst[:, k * T:(k + 1) * T], sq[:, k * T:(k + 1) * T], func, bias=bias[:, k:k + 1])


def gated_input(core, w, pad):
    nc = core.nc
    wide = T + 2 * PADC
    half = [core.work[:, s * T:(s + 1) * T] for s in range(2)]

    def load(i, s):
        return plain_views(w, KT, i * P + (3 + s) * GW)

    def take(dve, own, i, s, product):
        return nc.vector.tensor_tensor(half[s], product, core.rstd[:, :], ALU.mult)

    def sigmoid(act, i, s):
        return nc.scalar.activation(half[1], half[1], ACT.Sigmoid)

    def gate(dve, own, i, s):
        if s == 1:
            own.link(nc.vector.tensor_tensor(cols(pad, i * wide + PADC), half[0], half[1], ALU.mult))

    with core.phase("cvz") as (block,):
        @block.vector
        def _(dve):
            for k in range(2):
                nc.vector.memset(pad[:, k * wide:k * wide + PADC], 0.0)
                nc.vector.memset(pad[:, (k + 1) * wide - PADC:(k + 1) * wide], 0.0)
    linear(core, "glu", w, 4, take, load=load, mid=sigmoid, mids=(1,), finish=gate)


def load_taps(core, a, taps):
    nc = core.nc
    with core.phase("tap", "loaded") as (block, loaded):
        @block.sync
        def _(sp):
            with nc.allow_non_contiguous_dma("taps, a channel a partition"):
                for k in range(2):
                    sp.dma_start(taps[:, k * CONV:(k + 1) * CONV],
                                 a["conv_dw_w_2"][0][:, k * P:(k + 1) * P].rearrange("j p -> p j")).then_inc(loaded, 16)
            sp.wait_ge(loaded, 32)


def rest_and_convolution(core, w, g, z, pad, taps, acc):
    nc = core.nc
    wide = T + 2 * PADC
    tiles = 6
    assert tiles * CONV_STEP == CONV - 1

    def tap(own, j, first=False):
        for k in range(2):
            o, x, c = acc[:, k * T:(k + 1) * T], cols(pad, j + k * wide), cols(taps, j + k * CONV, 1)
            if first:
                own.mark(nc.vector.tensor_scalar(o, x, c, g["conv_dw_b_2"][:, k:k + 1], ALU.mult, ALU.add))
            else:
                own.mark(nc.vector.scalar_tensor_tensor(out=o, in0=x, scalar=c, in1=o, op0=ALU.mult, op1=ALU.add))
        own.join()

    with core.phase("cv0", "dve_own") as (block, dve_own):
        @block.vector
        def _(dve):
            tap(Chain(dve, dve_own), 0, True)

    def more_taps(dve, own, i, s):
        for j in range(CONV_STEP):
            tap(own, i * (2 * CONV_STEP) + (s * CONV_STEP + 1 + j))

    linear(core, "rest", w, tiles, scale_to(core, z), load=lambda i, s: plain_views(w, KT, i * (2 * P) + (s * P + 5 * GW)),
           finish=more_taps)


def conformer_tail(core, a, g, acc, mix):
    layer_norm(core, "cvln", acc, g["conv_ln_g_2"], g["conv_ln_b_2"], acc, ACT.Silu, core.eps5)
    with ExitStack() as ctx:
        pair = tuple(core.sbuf(f"cv_{p}", [P, 2 * T], ctx, F32R) for p in ("hi", "lo"))
        linear(core, "pw", a["conv_pw_2"][0], 2, copy_to(core.nc, mix, 2 * T), pair, kts=2,
               operand=Operand(core, acc, None, pair, tiles=2))


def multiscale_pool(core, a, c_in, g, z, mix):
    nc = core.nc
    wide = T + 2 * POOL_PAD
    with ExitStack() as ctx:
        sb = lambda n, shape: core.sbuf("po_" + n, shape, ctx)
        bufs = [sb(f"sum{n}", [P, wide]) for n in range(2)]
        inv = sb("inv_count", [P, 2 * T])
        wts = sb("weights", [P, 2 * P])
        win = core.work[:, 0:2 * T]
        sems = ("const", "zeroed", "weights", "pooled", "mixed", "dve_own")
        with core.phase("po", *sems) as (block, const, zeroed, weights, pooled, mixed, dve_own):
            @block.sync
            def _(sp):
                sp.dma_start(inv[:, :], c_in["inv_count"]).then_inc(const, 16)
                sp.wait_ge(zeroed, 1)
                for j in range(4):
                    r = 64 * (j % 2)
                    sp.dma_start(wts[r:r + 64, (j // 2) * P + r:(j // 2) * P + r + 64], a["pool_w_2"][0][j]) \
                        .then_inc(weights, 16)

            @block.vector
            def _(dve):
                own = Chain(dve, dve_own)
                nc.vector.memset(wts[:, :], 0.0).then_inc(zeroed, 1)
                dve.wait_ge(const, 16)
                for k in range(2):
                    x = z[:, (REST2["pool"] + k) * T:(REST2["pool"] + k + 1) * T]
                    own.mark(nc.vector.memset(bufs[0][:, :], 0.0))
                    own.mark(nc.vector.memset(bufs[1][:, :], 0.0))
                    own.join()
                    own.link(nc.vector.tensor_copy(bufs[0][:, POOL_PAD:POOL_PAD + T], x))
                    src, reach = 0, 0
                    for level, window in enumerate(POOL_WINDOWS[:2 * k + 2]):
                        s, d = bufs[src], bufs[1 - src]
                        if window == 2:
                            lo, up = -1, 0
                        else:
                            lo, up = -window // 4, window // 4
                        reach += max(-lo, up)
                        n = wide - 2 * reach
                        own.link(nc.vector.tensor_tensor(d[:, reach:reach + n], s[:, reach + lo:reach + lo + n],
                                                         s[:, reach + up:reach + up + n], ALU.add))
                        src = 1 - src
                        if level >= 2 * k:
                            r = slice(64 * (level % 2), 64 * (level % 2) + 64)
                            own.link(nc.vector.tensor_tensor(win[r, k * T:(k + 1) * T],
                                                             bufs[src][r, POOL_PAD:POOL_PAD + T],
                                                             inv[r, k * T:(k + 1) * T], ALU.mult))
                    w = win[:, k * T:(k + 1) * T]
                    nc.vector.tensor_tensor(w, w, x, ALU.subtract).then_inc(pooled, 1)
                dve.wait_ge(mixed, 1)
                for k in range(2):
                    nc.vector.tensor_scalar(mix[:, (4 + k) * T:(5 + k) * T], core.bank(2 * k, T),
                                            g["pool_scale_2"][:, k:k + 1], None, ALU.mult)

            @block.tensor
            def _(pe):
                pe.wait_ge(weights, 64)
                pe.wait_ge(pooled, 2)
                for k in range(2):
                    for c in range(0, T, BANK):
                        last = nc.tensor.matmul(core.bank(2 * k, BANK, c), wts[:, k * P:(k + 1) * P],
                                                win[:, k * T + c:k * T + c + BANK], start=True, stop=True)
                last.then_inc(mixed, 1)


def spatial_gating(core, a, g, z, mix):
    nc = core.nc
    u = z[:, REST2["u"] * T:(REST2["u"] + 2) * T]
    v = z[:, REST2["v_gate"] * T:(REST2["v_gate"] + 2) * T]
    with core.phase("gelu", "done") as (block, done):
        @block.scalar
        def _(act):
            for part in (u, v):
                nc.scalar.activation(part, part, ACT.Gelu_apprx_tanh).then_inc(done, 1)
            act.wait_ge(done, 2)
    layer_norm(core, "sgln", v, g["sgu_ln_g_2"], g["sgu_ln_b_2"], v, ACT.Identity, core.eps5)
    with ExitStack() as ctx:
        sb = lambda n, shape: core.sbuf("sg_" + n, shape, ctx)
        ws, wsT = sb("ws", [P, 4 * P]), sb("wsT", [P, 4 * P])
        bs = sb("bs", [P, 2 * P])
        v_tok = sb("v_tok", [P, 2 * T])
        tmp = core.work[:, 0:2 * T]
        sems = ("loaded", "w_turned", "w_ready", "v_turned", "v_ready", "mixed", "dve_own")
        with core.phase("sg", *sems) as (block, loaded, w_turned, w_ready, v_turned, v_ready, mixed, dve_own):
            @block.sync
            def _(sp):
                sp.dma_start(ws[:, :].rearrange("p (h q) -> p h q", h=4),
                             a["sgu_w_2"][0].rearrange("h p q -> p h q")).then_inc(loaded, 16)
                for hh in range(4):
                    r = 64 * (hh % 2)
                    sp.dma_start(bs[r:r + 64, (hh // 2) * P:(hh // 2 + 1) * P],
                                 a["sgu_b_2"][0][hh:hh + 1, :].to_broadcast([64, P])).then_inc(loaded, 16)

            @block.tensor
            def _(pe):
                pe.wait_ge(loaded, 80)
                for hh in range(4):
                    last = nc.tensor.transpose(core.bank(0, P, hh * P), ws[:, hh * P:(hh + 1) * P], core.ident[:, :])
                last.then_inc(w_turned, 1)
                for k in range(2):
                    for n in range(TT):
                        last = nc.tensor.transpose(core.bank(2 + 2 * k, P, n * P), v[:, k * T + n * P:k * T + (n + 1) * P],
                                                   core.ident[:, :])
                    last.then_inc(v_turned, 1)
                pe.wait_ge(w_ready, 1)
                pe.wait_ge(v_ready, 2)
                for k in range(2):
                    for n in range(TT):
                        for hh in range(2):
                            last = nc.tensor.matmul(
                                core.ps[64 * hh:64 * hh + 64, (2 + 2 * k) * BANK + n * P:(2 + 2 * k) * BANK + (n + 1) * P],
                                v_tok[:, k * T + n * P + 64 * hh:k * T + n * P + 64 * hh + 64],
                                wsT[:, (2 * k + hh) * P:(2 * k + hh + 1) * P], start=True, stop=True)
                    last.then_inc(mixed, 1)

            @block.vector
            def _(dve):
                own = Chain(dve, dve_own)
                dve.wait_ge(w_turned, 1)
                nc.vector.tensor_copy(wsT[:, :], core.bank(0)).then_inc(w_ready, 1)
                for k in range(2):
                    dve.wait_ge(v_turned, k + 1)
                    nc.vector.tensor_copy(v_tok[:, k * T:(k + 1) * T], core.bank(2 + 2 * k, T)).then_inc(v_ready, 1)
                for k in range(2):
                    dve.wait_ge(mixed, k + 1)
                    t = tmp[:, k * T:(k + 1) * T]
                    own.link(nc.vector.tensor_tensor(t.rearrange("p (n q) -> p n q", q=P),
                                                     core.bank(2 + 2 * k, T).rearrange("p (n q) -> p n q", q=P),
                                                     bs[:, k * P:(k + 1) * P].unsqueeze(1).to_broadcast([P, TT, P]), ALU.add))
                    nc.vector.tensor_tensor(mix[:, (6 + k) * T:(7 + k) * T], t, u[:, k * T:(k + 1) * T], ALU.mult)


def second_block(core, a, c_in, g):
    nc = core.nc
    w = a["w_in_2"][0]
    with ExitStack() as block_ctx:
        mix = core.sbuf("mix2", [P, KT * T], block_ctx)
        with ExitStack() as ctx:
            z = core.sbuf("z_qkv", [P, 6 * T], ctx)
            linear(core, "qkv2", w, 6, scale_to(core, z), operand=Operand(core, core.x, g["norm_g_2"], core.h, core.eps6))
            neighbourhood_attention(core, c_in, a["na_rpb_2"], z, mix)
        with ExitStack() as ctx:
            acc = core.sbuf("cv_acc", [P, 2 * T], ctx)
            z_ctx = ctx.enter_context(ExitStack())
            z = core.sbuf("z_rest", [P, 6 * T], z_ctx)
            with ExitStack() as conv_ctx:
                pad = core.sbuf("cv_padded", [P, 2 * (T + 2 * PADC)], conv_ctx)
                taps = core.sbuf("cv_taps", [P, 2 * CONV], conv_ctx)
                load_taps(core, a, taps)
                gated_input(core, w, pad)
                rest_and_convolution(core, w, g, z, pad, taps, acc)
            multiscale_pool(core, a, c_in, g, z, mix)
            spatial_gating(core, a, g, z, mix)
            z_ctx.close()
            conformer_tail(core, a, g, acc, mix)
        with ExitStack() as ctx:
            gate = core.sbuf("g2_gate", [P, 2 * T], ctx)

            def take(dve, own, i, s, product):
                return nc.vector.tensor_tensor(gate[:, s * T:(s + 1) * T], product, core.rstd[:, :], ALU.mult)

            def silu(act, i, s):
                return nc.scalar.activation(gate[:, s * T:(s + 1) * T], gate[:, s * T:(s + 1) * T], ACT.Silu)

            def times(dve, own, i, s):
                tile = cols(mix, i * (2 * T) + s * T)
                own.link(nc.vector.tensor_tensor(tile, tile, gate[:, s * T:(s + 1) * T], ALU.mult))

            linear(core, "gates2", w, KT, take, load=lambda i, s: plain_views(w, KT, i * (2 * P) + (s * P + 8 * GW)),
                   mid=silu, finish=times)
        linear(core, "out2", a["w_out_2"][0], KT, add_to(nc, core.x), operand=Operand(core, mix, None, core.h))
    rms_norm(core, "nf2", core.x, g["final_g_2"], core.x, core.eps6)

AH, AKV, AD = 8, 2, 64
WIN = 128
MEM = 256
CA_D = 256
FF3 = 2816
FT3 = FF3 // P
FF3_GROUP = 6
W3 = dict(q=0, k=512, v=640, hq=768, hf=1280, hi=1792, hg=2304)
LEVELS = (64, 32, 16, 8, 4, 2, 1)
LN_LEAST = 6e-20


def third_gains(core, a, c_in, g, column, by_tile):
    for name in ("mix_pre_norm_3", "mix_post_norm_3", "ca_pre_norm_3", "mem_norm_3", "ca_post_norm_3",
                 "ffn_pre_norm_3", "ffn_post_norm_3"):
        column(name, by_tile(a[name][0]), KT)
    column("hgrn_out_norm_3", by_tile(a["hgrn_out_norm_3"][0]), 1)
    for n in range(2):
        column(f"lb_logits{n}", by_tile(a["hgrn_lb_logits_3"][n]), HEADS)
    column("sinks", a["attn_sinks_3"].to_broadcast([P, AH]), AH)
    g["lb"] = core.sbuf("g_lb", [P, 4 * HEADS])


def lower_bound(core, g):
    nc, lb = core.nc, g["lb"]
    l0, l1 = g["lb_logits0"], g["lb_logits1"]
    H = HEADS
    with core.phase("lb", "shifted", "exped", "dve_own") as (block, shifted, exped, dve_own):
        @block.vector
        def _(dve):
            own = Chain(dve, dve_own)
            own.link(nc.vector.tensor_tensor(lb[:, 0:H], l0[:, :], l1[:, :], ALU.max))
            nc.vector.tensor_tensor(lb[:, 2 * H:3 * H], l0[:, :], lb[:, 0:H], ALU.subtract).then_inc(shifted, 1)
            nc.vector.tensor_tensor(lb[:, 3 * H:4 * H], l1[:, :], lb[:, 0:H], ALU.subtract).then_inc(shifted, 1)
            dve.wait_ge(exped, 1)
            own.link(nc.vector.tensor_tensor(lb[:, H:2 * H], lb[:, 2 * H:3 * H], lb[:, 3 * H:4 * H], ALU.add))
            own.link(nc.vector.reciprocal(lb[:, H:2 * H], lb[:, H:2 * H]))
            own.link(nc.vector.tensor_tensor(lb[:, 0:H], lb[:, 2 * H:3 * H], lb[:, H:2 * H], ALU.mult))
            nc.vector.tensor_scalar(lb[:, H:2 * H], lb[:, 0:H], -1.0, 1.0, ALU.mult, ALU.add)

        @block.scalar
        def _(act):
            act.wait_ge(shifted, 2)
            nc.scalar.activation(lb[:, 2 * H:4 * H], lb[:, 2 * H:4 * H], ACT.Exp).then_inc(exped, 1)


def window_attention(core, w, c_in, sinks, mix):
    nc, h = core.nc, core.h
    with ExitStack() as ctx:
        sb = lambda n, shape: core.sbuf("wa_" + n, shape, ctx)
        wt = Weights(core, "wa", ctx)
        kP, vT, qT = sb("k_padded", [P, WIN + T]), sb("vT", [P, T]), sb("qT", [P, T])
        v_tok = sb("v_tok", [P, WIN + T])
        mask = sb("mask", [P, 4 * WIN])
        probs, pT = sb("probs", [P, 2 * 4 * WIN]), sb("probsT", [P, 2 * 4 * WIN])
        col = sb("col", [P, 2 * 16])
        sems = Weights.SIGNALS + ("const", "kv_taken", "v_turned", "kv_ready", "q_ready", "scores_ready",
                "max_ready", "exp_ready", "p_ready", "p_turned", "pT_ready", "pv_done", "o_taken", "dve_own", "scores_taken")
        with core.phase("wa", *sems) as (
                block, *ws, const, kv_taken, v_turned, kv_ready, q_ready, scores_ready,
                max_ready, exp_ready, p_ready, p_turned, pT_ready, pv_done, o_taken, dve_own, scores_taken):

            wt.signals(ws)

            def halves(first, second):
                views = [w[0:D, ds(c, AD)].rearrange("(k p) n -> p k n", p=P) for c in (first, second)]
                return [[(lambda d: d[:, :, 0:AD], views[0][:, 4 * r:4 * r + 4, :]),
                         (lambda d: d[:, :, AD:P], views[1][:, 4 * r:4 * r + 4, :])] for r in range(2)]

            @block.sync
            def _(sp):
                sp.dma_start(mask[:, :], c_in["window"]).then_inc(const, 16)
                wt.load(sp, 0, 0, halves(W3["k"], W3["k"] + AD))
                wt.load(sp, 1, 0, halves(W3["v"], W3["v"] + AD))
                with sp.Fori(0, 4) as i:
                    wt.load(sp, i + 2, 0, halves(i * AD + W3["q"], i * AD + (W3["q"] + AH // 2 * AD)))

            @block.gpsimd
            def _(pool):
                wt.open_raw(pool)
                wt.split(pool, 0, 0, (2, 2))
                wt.split(pool, 1, 0, (2, 2))
                with pool.Fori(0, 4) as i:
                    wt.split(pool, i + 2, 0, (2, 2))

            @block.tensor
            def _(pe):
                wt.open_slots(pe)
                for t in range(2):
                    wt.product(pe, core.bank(2 * t, T), h, t, 0)
                pe.wait_ge(kv_taken, 2)
                for t in range(TT):
                    last = nc.tensor.transpose(core.bank(4, P, t * P), vT[:, t * P:(t + 1) * P], core.ident[:, :])
                last.then_inc(v_turned, 1)

                def score(i, b):
                    if b >= 2:
                        pe.wait_ge(scores_taken, i * TT + (b - 1))
                    for g in range(2):
                        last = nc.tensor.matmul(core.bank(4 * (1 - b % 2) + g, 2 * WIN), qT[64 * g:64 * g + 64, b * WIN:(b + 1) * WIN],
                                                kP[64 * g:64 * g + 64, b * WIN:(b + 2) * WIN], start=True, stop=True)
                    last.then_inc(scores_ready, 1)

                def weigh(i, b):
                    pe.wait_ge(pT_ready, i * TT + (b + 1))
                    for g in range(2):
                        for j in range(2):
                            last = nc.tensor.matmul(
                                core.ps[64 * g:64 * g + 64, 2 * BANK + b * WIN:2 * BANK + (b + 1) * WIN],
                                v_tok[:, (b + j) * P + 64 * g:(b + j) * P + 64 * g + 64],
                                pT[:, (b % 2) * BANK + (2 * g + j) * P:(b % 2) * BANK + (2 * g + j + 1) * P],
                                start=(j == 0), stop=(j == 1))
                    last.then_inc(pv_done, 1)

                with pe.Fori(0, 4) as i:
                    pe.wait_ge(kv_ready, 3)
                    wt.product(pe, core.bank(0, T), h, i + 2, 0)
                    pe.wait_ge(q_ready, i + 1)
                    score(i, 0)
                    score(i, 1)
                    for b in range(TT):
                        if b + 2 < TT:
                            score(i, b + 2)
                        pe.wait_ge(p_ready, i * TT + (b + 1))
                        if b >= 2:
                            pe.wait_ge(pT_ready, i * TT + (b - 1))
                        for j in range(4):
                            last = nc.tensor.transpose(core.bank(6 + b % 2, P, j * P),
                                                       probs[:, (b % 2) * BANK + j * P:(b % 2) * BANK + (j + 1) * P],
                                                       core.ident[:, :])
                        last.then_inc(p_turned, 1)
                        if b >= 1:
                            weigh(i, b - 1)
                    weigh(i, TT - 1)
                    pe.wait_ge(o_taken, i + 1)

            @block.scalar
            def _(act):
                nc.scalar.preload_act_table_set(EXP_LN)
                act.wait_ge(v_turned, 1)
                nc.scalar.activation(v_tok[:, WIN:WIN + T], core.bank(4, T), ACT.Identity).then_inc(kv_ready, 1)
                with act.Fori(0, 4) as i:
                    def turned(b):
                        act.wait_ge(p_turned, i * TT + (b + 1))
                        if b >= 2:
                            act.wait_ge(pv_done, i * TT + (b - 1))
                        nc.scalar.activation(pT[:, (b % 2) * BANK:(b % 2 + 1) * BANK], core.bank(6 + b % 2),
                                             ACT.Identity).then_inc(pT_ready, 1)
                    for b in range(TT):
                        act.wait_ge(max_ready, i * TT + (b + 1))
                        c = (b % 2) * 16
                        for g in range(2):
                            s = probs[:, (b % 2) * BANK + 2 * g * WIN:(b % 2) * BANK + 2 * (g + 1) * WIN]
                            nc.scalar.activation(s, s, ACT.Exp, bias=col[:, c + g:c + g + 1],
                                                 accum_out=col[:, c + 2 + g:c + 3 + g]).then_inc(exp_ready, 1)
                        nc.scalar.activation(col[:, c + 6:c + 8], col[:, c + 4:c + 6], ACT.Exp).then_inc(exp_ready, 1)
                        if b >= 1:
                            turned(b - 1)
                    turned(TT - 1)
                    act.wait_ge(pv_done, i * TT + TT)
                    nc.scalar.activation(cols(mix, i * T), core.bank(2, T), ACT.Identity).then_inc(o_taken, 1)

            @block.vector
            def _(dve):
                nc.vector.memset(kP[:, 0:WIN], 0.0).then_inc(kv_ready, 1)
                nc.vector.memset(v_tok[:, 0:WIN], 0.0).then_inc(kv_ready, 1)
                dve.wait_ge(const, 16)
                for t, dst in enumerate((kP[:, WIN:WIN + T], vT[:, :])):
                    wt.wait_product(dve, t)
                    nc.vector.tensor_tensor(dst, core.bank(2 * t, T), core.rstd[:, :], ALU.mult).then_inc(kv_taken, 1)
                with dve.Fori(0, 4) as i:
                    own = Chain(dve, dve_own)
                    wt.wait_product(dve, i + 2)
                    nc.vector.scalar_tensor_tensor(out=qT[:, :], in0=core.bank(0, T), scalar=AD ** -0.5,
                                                   in1=core.rstd[:, :], op0=ALU.mult, op1=ALU.mult).then_inc(q_ready, 1)
                    sink = sinks[:, :].rearrange("p (g n) -> p n g", g=2)[:, ds(i, 1), :].rearrange("p n g -> p (n g)")

                    def soft(b):
                        dve.wait_ge(scores_ready, i * TT + (b + 1))
                        if b >= 2:
                            dve.wait_ge(p_turned, i * TT + (b - 1))
                        c = (b % 2) * 16
                        s = probs[:, (b % 2) * BANK:(b % 2 + 1) * BANK].rearrange("p (g k) -> p g k", g=2)
                        m = mask[:, (0 if b == 0 else 2 * WIN):(0 if b == 0 else 2 * WIN) + 2 * WIN]
                        own.link(nc.vector.tensor_tensor(
                            s, core.bank(4 * (1 - b % 2), 2 * BANK).rearrange("p (g k) -> p g k", g=2)[:, :, 0:2 * WIN],
                            m.unsqueeze(1).to_broadcast([P, 2, 2 * WIN]), ALU.add))
                        dve.sem_inc(scores_taken, 1)
                        own.link(nc.vector.tensor_reduce(out=col[:, c + 8:c + 10], in_=s, axis=AX.X, op=ALU.max))
                        own.link(nc.vector.tensor_tensor(col[:, c + 10:c + 12], col[:, c + 8:c + 10], sink, ALU.max))
                        own.mark(nc.vector.tensor_scalar(col[:, c:c + 2], col[:, c + 10:c + 12], -1.0, None, ALU.mult))
                        own.mark(nc.vector.tensor_tensor(col[:, c + 4:c + 6], sink, col[:, c + 10:c + 12], ALU.subtract))
                        own.join()
                        dve.sem_inc(max_ready, 1)

                    def divide(b):
                        c = (b % 2) * 16
                        dve.wait_ge(exp_ready, i * (3 * TT) + (3 * b + 3))
                        own.link(nc.vector.tensor_tensor(col[:, c + 12:c + 14], col[:, c + 2:c + 4], col[:, c + 6:c + 8], ALU.add))
                        own.link(nc.vector.reciprocal(col[:, c + 14:c + 16], col[:, c + 12:c + 14]))
                        for g in range(2):
                            s = probs[:, (b % 2) * BANK + 2 * g * WIN:(b % 2) * BANK + 2 * (g + 1) * WIN]
                            own.mark(nc.vector.tensor_scalar(s, s, col[:, c + 14 + g:c + 15 + g], None, ALU.mult))
                        own.join()
                        dve.sem_inc(p_ready, 1)

                    soft(0)
                    for b in range(TT):
                        if b + 1 < TT:
                            soft(b + 1)
                        divide(b)
                    own.restart()


def hgrn(core, w, c_in, g, mix):
    nc, h = core.nc, core.h
    lb = g["lb"]
    with ExitStack() as ctx:
        sb = lambda n, shape: core.sbuf("hg_" + n, shape, ctx)
        wt = Weights(core, "hg", ctx)
        qT, kT, bT = (sb(n, [P, T]) for n in ("qT", "kT", "bT"))
        qL, kL = sb("q_level", [P, 2 * T]), sb("k_level", [P, 2 * T])
        dec = sb("decay", [P, 2 * T])
        mask = sb("mask", [P, 8 * P])
        cdec = sb("chunk_decay", [P, TT])
        A, sig, k_tok, v_tok = (core.work[:, n * T:(n + 1) * T] for n in range(4))
        iT, sig_g = kL[:, 0:T], dec[:, T:2 * T]
        qd, state = qL[:, 0:T], qL[:, T:2 * T]
        oT, sq, hrstd = A, sig, dec[:, T:2 * T]
        n_lev = len(LEVELS)
        sems = Weights.SIGNALS + ("const", "raw_ready", "sig_ready", "proj_taken", "ln_in", "ln_ready",
                "e_in", "e_ready", "level_in", "level_ready", "level_taken", "kd_ready", "turned", "kv_tok_ready",
                "update_ready", "state_ready", "o_done", "sq_ready", "stat_ready", "rstd_ready", "mix_done",
                "dve_own", "act_own", "level_seen")
        with core.phase("hg", *sems) as (
                block, *ws, const, raw_ready, sig_ready, proj_taken, ln_in, ln_ready,
                e_in, e_ready, level_in, level_ready, level_taken, kd_ready, turned, kv_tok_ready,
                update_ready, state_ready, o_done, sq_ready, stat_ready, rstd_ready, mix_done,
                dve_own, act_own, level_seen):
            wt.signals(ws)
            gate = lambda i: cols(mix, i * T + HEADS * T)
            first = (W3["hq"], W3["hf"], W3["hi"], W3["hg"])
            v3 = lambda b: b.rearrange("p (c n) -> p c n", n=P)

            @block.sync
            def _(sp):
                sp.dma_start(mask[:, :], c_in["levels"]).then_inc(const, 16)
                with sp.Fori(0, HEADS) as i:
                    for j in range(4):
                        wt.load(sp, i * 4 + j, 0, plain_views(w, KT, i * HD + first[j]))

            @block.gpsimd
            def _(pool):
                wt.open_raw(pool)
                with pool.Fori(0, HEADS) as i:
                    for j in range(4):
                        wt.split(pool, i * 4 + j, 0)

            @block.tensor
            def _(pe):
                wt.open_slots(pe)
                with pe.Fori(0, HEADS) as i:
                    for j in range(4):
                        if j >= 2:
                            pe.wait_ge(proj_taken, i * 4 + (j - 1))
                        wt.product(pe, core.bank(2 * (j % 2), T), h, i * 4 + j, 0)
                    pe.wait_ge(proj_taken, i * 4 + 3)
                    for c in range(TT):
                        last = nc.tensor.transpose(core.bank(6, P, c * P), iT[:, c * P:(c + 1) * P], core.ident[:, :])
                    last.then_inc(turned, 1)
                    pe.wait_ge(proj_taken, i * 4 + 4)
                    pe.wait_ge(raw_ready, i + 1)
                    for n in range(n_lev + 1):
                        if n == 0:
                            a, b = kT[:, :], qT[:, :]
                        else:
                            pe.wait_ge(level_in, i * n_lev + n)
                            a, b = (x[:, (n % 2) * T:(n % 2 + 1) * T] for x in (kL, qL))
                        if n >= 2:
                            pe.wait_ge(level_taken, i * (n_lev + 1) + (n - 1))
                        for c in range(TT):
                            last = nc.tensor.matmul(core.bank(2 * (n % 2), P, c * P), a[:, c * P:(c + 1) * P],
                                                    b[:, c * P:(c + 1) * P], start=True, stop=True)
                        last.then_inc(level_ready, 1)
                    pe.wait_ge(kd_ready, i + 1)
                    for c in range(TT):
                        last = nc.tensor.transpose(core.bank(4, P, c * P), kL[:, c * P:(c + 1) * P], core.ident[:, :])
                    last.then_inc(turned, 1)
                    pe.wait_ge(kv_tok_ready, i * 2 + 2)
                    for c in range(TT - 1):
                        last = nc.tensor.matmul(core.bank(4, P, c * P), k_tok[:, c * P:(c + 1) * P],
                                                v_tok[:, c * P:(c + 1) * P], start=True, stop=True)
                    last.then_inc(update_ready, 1)
                    pe.wait_ge(state_ready, i + 1)
                    for c in range(TT):
                        last = nc.tensor.matmul(core.bank(6, P, c * P), v_tok[:, c * P:(c + 1) * P],
                                                A[:, c * P:(c + 1) * P], start=True, stop=(c == 0))
                        if c:
                            last = nc.tensor.matmul(core.bank(6, P, c * P), state[:, c * P:(c + 1) * P],
                                                    qd[:, c * P:(c + 1) * P], start=False, stop=True)
                    last.then_inc(o_done, 1)
                    pe.wait_ge(sq_ready, i + 1)
                    for c in range(0, T, BANK):
                        last = nc.tensor.matmul(core.bank(4, BANK, c), core.ones[:, :], sq[:, c:c + BANK],
                                                start=True, stop=True)
                    last.then_inc(stat_ready, 1)

            @block.scalar
            def _(act):
                with act.Fori(0, HEADS) as i:
                    own = Chain(act, act_own)
                    nc.scalar.preload_act_table_set("sigmoid_and_others")
                    act.wait_ge(proj_taken, i * 4 + 1)
                    nc.scalar.activation(sig, qT[:, :], ACT.Sigmoid).then_inc(sig_ready, 1)
                    act.wait_ge(proj_taken, i * 4 + 2)
                    nc.scalar.activation(kT[:, :], bT[:, :], ACT.Sigmoid, scale=-1.0).then_inc(sig_ready, 1)
                    nc.scalar.activation(bT[:, :], bT[:, :], ACT.Sigmoid).then_inc(sig_ready, 1)
                    act.wait_ge(proj_taken, i * 4 + 4)
                    nc.scalar.activation(sig_g, gate(i), ACT.Sigmoid).then_inc(sig_ready, 1)
                    nc.scalar.preload_act_table_set(EXP_LN)
                    act.wait_ge(turned, i * 2 + 1)
                    nc.scalar.activation(v_tok, core.bank(6, T), ACT.Identity).then_inc(kv_tok_ready, 1)
                    act.wait_ge(ln_in, i + 1)
                    nc.scalar.activation(dec[:, 0:T], bT[:, :], ACT.Ln).then_inc(ln_ready, 1)
                    for n in range(n_lev):
                        act.wait_ge(e_in, i * (n_lev + 2) + (n + 1))
                        d = dec[:, (n % 2) * T:(n % 2 + 1) * T]
                        nc.scalar.activation(d, d, ACT.Exp).then_inc(e_ready, 1)
                    act.wait_ge(e_in, i * (n_lev + 2) + (n_lev + 1))
                    d = dec[:, (n_lev % 2) * T:(n_lev % 2 + 1) * T]
                    nc.scalar.activation(d, d, ACT.Exp, scale=-1.0).then_inc(e_ready, 1)
                    act.wait_ge(e_in, i * (n_lev + 2) + (n_lev + 2))
                    d = dec[:, ((n_lev + 1) % 2) * T:((n_lev + 1) % 2 + 1) * T]
                    nc.scalar.activation(cdec[:, :], v3(bT[:, :])[:, :, P - 1:P].rearrange("p c n -> p (c n)"), ACT.Exp) \
                        .then_inc(e_ready, 1)
                    nc.scalar.activation(d, bT[:, :], ACT.Exp).then_inc(e_ready, 1)
                    act.wait_ge(turned, i * 2 + 2)
                    nc.scalar.activation(k_tok, core.bank(4, T), ACT.Identity).then_inc(kv_tok_ready, 1)
                    act.wait_ge(o_done, i + 1)
                    own.link(nc.scalar.activation(oT, core.bank(6, T), ACT.Identity))
                    nc.scalar.activation(sq, oT, ACT.Square).then_inc(sq_ready, 1)
                    act.wait_ge(stat_ready, i + 1)
                    own.link(nc.scalar.activation(hrstd, core.bank(4, T), ACT.Ln, bias=core.eps6[:, :],
                                                  scale=1.0 / HD))
                    nc.scalar.activation(hrstd, hrstd, ACT.Exp, scale=-0.5).then_inc(rstd_ready, 1)
                    own.restart()
                    act.wait_ge(mix_done, i + 1)

            @block.vector
            def _(dve):
                dve.wait_ge(const, 16)
                with dve.Fori(0, HEADS) as i:
                    own = Chain(dve, dve_own)
                    lower, rest = cols(lb, i, 1), cols(lb, i + HEADS, 1)
                    own.mark(nc.vector.memset(A, 0.0))

                    def take_raw(j, dst):
                        wt.wait_product(dve, i * 4 + j)
                        own.link(nc.vector.tensor_tensor(dst, core.bank(2 * (j % 2), T), core.rstd[:, :], ALU.mult))
                        dve.sem_inc(proj_taken, 1)

                    take_raw(0, qT[:, :])
                    take_raw(1, bT[:, :])
                    dve.wait_ge(sig_ready, i * 4 + 1)
                    own.mark(nc.vector.scalar_tensor_tensor(out=qT[:, :], in0=sig, scalar=HD ** -0.5, in1=qT[:, :],
                                                            op0=ALU.mult, op1=ALU.mult))
                    take_raw(2, iT)
                    dve.wait_ge(sig_ready, i * 4 + 3)
                    own.mark(nc.vector.tensor_scalar(kT[:, :], kT[:, :], rest, None, ALU.mult))
                    own.link(nc.vector.tensor_scalar(bT[:, :], bT[:, :], rest, lower, ALU.mult, ALU.add))
                    dve.sem_inc(raw_ready, 1)
                    own.link(nc.vector.tensor_scalar(bT[:, :], bT[:, :], LN_LEAST, None, ALU.max))
                    take_raw(3, gate(i))
                    dve.sem_inc(ln_in, 1)
                    dve.wait_ge(sig_ready, i * 4 + 4)
                    own.link(nc.vector.tensor_tensor(gate(i), gate(i), sig_g, ALU.mult))
                    dve.wait_ge(ln_ready, i + 1)
                    for c in range(0, T, P):
                        own.mark(nc.vector.tensor_tensor_scan(bT[:, c:c + P], core.ones[:, :], dec[:, c:c + P], 0.0,
                                                              ALU.mult, ALU.add))
                    own.join()

                    def decay_in(n):
                        size = LEVELS[n]
                        d = dec[:, (n % 2) * T:(n % 2 + 1) * T]
                        blocks = lambda x: x.rearrange("p (m s) -> p m s", s=2 * size)
                        own.link(nc.vector.tensor_tensor(
                            blocks(d), blocks(bT[:, :]),
                            blocks(bT[:, :])[:, :, size - 1:size].to_broadcast([P, T // (2 * size), 2 * size]), ALU.subtract))
                        own.link(nc.vector.scalar_tensor_tensor(out=d, in0=d, scalar=-1.0, in1=d, op0=ALU.mult, op1=ALU.min))
                        dve.sem_inc(e_in, 1)

                    def take(n):
                        dve.wait_ge(level_ready, i * (n_lev + 1) + (n + 1))
                        dve.sem_inc(level_seen, 1)
                        own.link(nc.vector.copy_predicated(
                            v3(A), mask[:, n * P:(n + 1) * P].bitcast(mybir.dt.uint32)
                            .unsqueeze(1).to_broadcast([P, TT, P]), v3(core.bank(2 * (n % 2), T))))
                        dve.sem_inc(level_taken, 1)

                    decay_in(0)
                    for n in range(1, n_lev + 1):
                        if n < n_lev:
                            decay_in(n)
                        dve.wait_ge(e_ready, i * (n_lev + 3) + n)
                        d = dec[:, ((n - 1) % 2) * T:((n - 1) % 2 + 1) * T]
                        if n >= 3:
                            dve.wait_ge(level_ready, i * (n_lev + 1) + (n - 1))
                        own.mark(nc.vector.tensor_tensor(kL[:, (n % 2) * T:(n % 2 + 1) * T], kT[:, :], d, ALU.mult))
                        own.mark(nc.vector.tensor_tensor(qL[:, (n % 2) * T:(n % 2 + 1) * T], qT[:, :], d, ALU.mult))
                        own.join()
                        dve.sem_inc(level_in, 1)
                        take(n - 1)
                    d = dec[:, (n_lev % 2) * T:(n_lev % 2 + 1) * T]
                    own.link(nc.vector.tensor_tensor(
                        v3(d), v3(bT[:, :]), v3(bT[:, :])[:, :, P - 1:P].to_broadcast([P, TT, P]), ALU.subtract))
                    dve.sem_inc(e_in, 2)
                    dve.wait_ge(e_ready, i * (n_lev + 3) + (n_lev + 1))
                    own.link(nc.vector.tensor_tensor(kL[:, 0:T], kT[:, :], d, ALU.mult))
                    dve.sem_inc(kd_ready, 1)
                    take(n_lev)
                    own.mark(nc.vector.memset(state[:, 0:P], 0.0))
                    dve.wait_ge(e_ready, i * (n_lev + 3) + (n_lev + 3))
                    d = dec[:, ((n_lev + 1) % 2) * T:((n_lev + 1) % 2 + 1) * T]
                    own.link(nc.vector.tensor_tensor(qd, qT[:, :], d, ALU.mult))
                    dve.wait_ge(update_ready, i + 1)
                    for c in range(TT - 1):
                        own.link(nc.vector.scalar_tensor_tensor(
                            out=state[:, (c + 1) * P:(c + 2) * P], in0=state[:, c * P:(c + 1) * P],
                            scalar=cdec[:, c:c + 1], in1=core.bank(4, P, c * P), op0=ALU.mult, op1=ALU.add))
                    dve.sem_inc(state_ready, 1)
                    dve.wait_ge(rstd_ready, i + 1)
                    own.link(nc.vector.scalar_tensor_tensor(out=sq, in0=oT, scalar=g["hgrn_out_norm_3"][:, 0:1],
                                                            in1=hrstd, op0=ALU.mult, op1=ALU.mult))
                    own.link(nc.vector.tensor_tensor(gate(i), sq, gate(i), ALU.mult))
                    dve.sem_inc(mix_done, 1)
                    own.restart()


def cross_attention(core, a, mem, mix):
    nc, h = core.nc, core.h
    W = [a["ca_wq_3"][0], a["ca_wk_3"][0], a["ca_wv_3"][0]]
    with ExitStack() as ctx:
        sb = lambda n, shape: core.sbuf("ca_" + n, shape, ctx)
        wt = Weights(core, "ca", ctx)
        qT = sb("qT", [P, 2 * T])
        kT, vT, v_tok = sb("kT", [P, 2 * MEM]), sb("vT", [P, 2 * MEM]), sb("v_tok", [P, 2 * MEM])
        probs = sb("probs", [P, 2 * MEM])
        pT = sb("probsT", [P, 2 * T])
        col = sb("col", [P, 2 * 4])
        sems = Weights.SIGNALS + ("proj_taken", "v_turned", "v_ready", "scores_ready",
                "max_ready", "exp_ready", "p_ready", "p_turned", "pT_ready", "o_done", "o_taken", "dve_own")
        with core.phase("ca", *sems) as (
                block, *ws, proj_taken, v_turned, v_ready, scores_ready,
                max_ready, exp_ready, p_ready, p_turned, pT_ready, o_done, o_taken, dve_own):
            wt.signals(ws)

            @block.sync
            def _(sp):
                with sp.Fori(0, 4) as i:
                    for j in range(6):
                        wt.load(sp, i * 6 + j, 0, plain_views(W[j // 2], KT, i * CA_D + (j % 2) * P))

            @block.gpsimd
            def _(pool):
                wt.open_raw(pool)
                with pool.Fori(0, 4) as i:
                    for j in range(6):
                        wt.split_lo(pool, i * 6 + j, 0)

            @block.tensor
            def _(pe):
                def score(i, b):
                    if b >= 2:
                        pe.wait_ge(exp_ready, i * TT + (b - 1))
                    for k in range(2):
                        last = nc.tensor.matmul(core.bank(4 + b % 2, MEM), qT[:, k * T + b * P:k * T + (b + 1) * P],
                                                kT[:, k * MEM:(k + 1) * MEM], start=(k == 0), stop=(k == 1))
                    last.then_inc(scores_ready, 1)
                wt.open_slots(pe)
                with pe.Fori(0, 4) as i:
                    for j in range(6):
                        if j >= 2:
                            pe.wait_ge(proj_taken, i * 6 + (j - 1))
                        src, n = (h, T) if j < 2 else (mem, MEM)
                        wt.product(pe, core.bank(2 * (j % 2), n), src, i * 6 + j, 0, n, n)
                    pe.wait_ge(proj_taken, i * 6 + 6)
                    for k in range(2):
                        for m in range(2):
                            last = nc.tensor.transpose(core.bank(6, P, m * MEM + k * P),
                                                       vT[:, k * MEM + m * P:k * MEM + (m + 1) * P], core.ident[:, :])
                    last.then_inc(v_turned, 1)
                    score(i, 0)
                    score(i, 1)
                    pe.wait_ge(v_ready, i + 1)
                    for b in range(TT):
                        if b + 2 < TT:
                            score(i, b + 2)
                        pe.wait_ge(p_ready, i * TT + (b + 1))
                        if b >= 2:
                            pe.wait_ge(pT_ready, i * TT + (b - 1))
                        for m in range(2):
                            last = nc.tensor.transpose(core.bank(6 + b % 2, P, m * P),
                                                       probs[:, (b % 2) * MEM + m * P:(b % 2) * MEM + (m + 1) * P],
                                                       core.ident[:, :])
                        last.then_inc(p_turned, 1)
                    pe.wait_ge(pT_ready, i * TT + TT)
                    for k in range(2):
                        for c in range(0, T, BANK):
                            for m in range(2):
                                last = nc.tensor.matmul(core.bank(2 * k, BANK, c), v_tok[:, m * MEM + k * P:m * MEM + (k + 1) * P],
                                                        pT[:, m * T + c:m * T + c + BANK], start=(m == 0), stop=(m == 1))
                    last.then_inc(o_done, 1)
                    pe.wait_ge(o_taken, i + 1)

            @block.scalar
            def _(act):
                with act.Fori(0, 4) as i:
                    nc.scalar.preload_act_table_set(EXP_LN)
                    for j in range(6):
                        wt.split_hi(act, i * 6 + j, 0)
                    act.wait_ge(v_turned, i + 1)
                    nc.scalar.activation(v_tok[:, :], core.bank(6), ACT.Identity).then_inc(v_ready, 1)
                    def turned(b):
                        act.wait_ge(p_turned, i * TT + (b + 1))
                        nc.scalar.activation(pT[:, :].rearrange("p (m n) -> p m n", m=2)[:, :, b * P:(b + 1) * P],
                                             core.bank(6 + b % 2, MEM).rearrange("p (m n) -> p m n", m=2),
                                             ACT.Identity).then_inc(pT_ready, 1)
                    for b in range(TT):
                        act.wait_ge(max_ready, i * TT + (b + 1))
                        if b >= 2:
                            act.wait_ge(p_turned, i * TT + (b - 1))
                        c = (b % 2) * 4
                        nc.scalar.activation(probs[:, (b % 2) * MEM:(b % 2 + 1) * MEM], core.bank(4 + b % 2, MEM), ACT.Exp,
                                             bias=col[:, c:c + 1], accum_out=col[:, c + 1:c + 2]).then_inc(exp_ready, 1)
                        if b >= 1:
                            turned(b - 1)
                    turned(TT - 1)
                    act.wait_ge(o_done, i + 1)
                    nc.scalar.activation(cols(mix, i * (2 * T), 2 * T), core.bank(0, 2 * T), ACT.Identity).then_inc(o_taken, 1)

            @block.vector
            def _(dve):
                with dve.Fori(0, 4) as i:
                    own = Chain(dve, dve_own)
                    for j in range(6):
                        wt.wait_product(dve, i * 6 + j)
                        if j < 2:
                            own.link(nc.vector.scalar_tensor_tensor(out=qT[:, j * T:(j + 1) * T], in0=core.bank(2 * j, T),
                                                                    scalar=CA_D ** -0.5, in1=core.rstd[:, :],
                                                                    op0=ALU.mult, op1=ALU.mult))
                        else:
                            own.link(nc.vector.tensor_copy((kT, vT)[j // 2 - 1][:, (j % 2) * MEM:(j % 2 + 1) * MEM],
                                                           core.bank(2 * (j % 2), MEM)))
                        dve.sem_inc(proj_taken, 1)

                    def peak(b):
                        dve.wait_ge(scores_ready, i * TT + (b + 1))
                        nc.vector.tensor_reduce(out=col[:, (b % 2) * 4:(b % 2) * 4 + 1], in_=core.bank(4 + b % 2, MEM),
                                                axis=AX.X, op=ALU.max, negate=True).then_inc(max_ready, 1)
                    peak(0)
                    for b in range(TT):
                        if b + 1 < TT:
                            peak(b + 1)
                        c, s = (b % 2) * 4, probs[:, (b % 2) * MEM:(b % 2 + 1) * MEM]
                        dve.wait_ge(exp_ready, i * TT + (b + 1))
                        own.link(nc.vector.reciprocal(col[:, c + 2:c + 3], col[:, c + 1:c + 2]))
                        nc.vector.tensor_scalar(s, s, col[:, c + 2:c + 3], None, ALU.mult).then_inc(p_ready, 1)
                    own.restart()


def conv_ffn(core, a, gain, dst):
    nc = core.nc
    w_up, w_down = a["ffn_w_up_3"][0], a["ffn_w_down_3"][0]
    wide = T + 2
    with ExitStack() as ctx:
        sb = lambda n, shape, dt=F32: core.sbuf("cf_" + n, shape, ctx, dt)
        gated = tuple(sb(f"gated_{p}", [P, FF3_GROUP * T], F32R) for p in ("hi", "lo"))
        taps, bias = sb("taps", [P, 3 * 2 * FT3]), sb("bias", [P, 2 * FT3])
        pad, raw = core.work[:, 0:wide], core.work[:, wide + 2 * T:wide + 3 * T]
        conv = [core.work[:, wide + s * T:wide + (s + 1) * T] for s in range(2)]
        with core.phase("cfc", "loaded") as (block, loaded):
            @block.sync
            def _(sp):
                with nc.allow_non_contiguous_dma("taps, a channel a partition"):
                    for j in range(3):
                        sp.dma_start(taps[:, j * 2 * FT3:(j + 1) * 2 * FT3],
                                     a["ffn_conv_w_3"][0][j].rearrange("(k p) -> p k", p=P)).then_inc(loaded, 16)
                    sp.dma_start(bias[:, :], a["ffn_conv_b_3"][0].rearrange("(k p) -> p k", p=P)).then_inc(loaded, 16)
                sp.wait_ge(loaded, 64)

        def up(base, tiles):
            def take(dve, own, i, s, product):
                tap = lambda j: cols(taps, i + (base + j * 2 * FT3 + s * FT3), 1)
                own.link(nc.vector.memset(pad[:, 0:2], 0.0))
                own.link(nc.vector.tensor_tensor(pad[:, 2:2 + T], product, core.rstd[:, :], ALU.mult))
                own.link(nc.vector.tensor_scalar(conv[s], pad[:, 2:2 + T], tap(2), cols(bias, i + (base + s * FT3), 1),
                                                 ALU.mult, ALU.add))
                own.link(nc.vector.scalar_tensor_tensor(out=conv[s], in0=pad[:, 0:T], scalar=tap(0), in1=conv[s],
                                                        op0=ALU.mult, op1=ALU.add))
                return nc.vector.scalar_tensor_tensor(out=conv[s], in0=pad[:, 1:1 + T], scalar=tap(1), in1=conv[s],
                                                      op0=ALU.mult, op1=ALU.add)

            def gelu(act, i, s):
                return nc.scalar.activation(conv[0], conv[0], ACT.Gelu_apprx_tanh)

            def gate(dve, own, i, s):
                if s == 1:
                    hi, lo = (cols(part, i * T) for part in gated)
                    own.link(nc.vector.tensor_tensor(conv[1], conv[1], conv[0], ALU.mult))
                    own.link(nc.vector.tensor_copy(hi, conv[1]))
                    own.link(nc.vector.tensor_tensor(lo, conv[1], hi.bitcast(F32), ALU.subtract))

            linear(core, f"up3_{base}", w_up, 2 * tiles, take, mid=gelu, mids=(0,), finish=gate,
                   raw=raw, load=lambda i, s: plain_views(w_up, KT, i * P + (base * P + s * FF3)),
                   operand=Operand(core, core.x, gain, core.h, core.eps6) if base == 0 else None)

        for base in range(0, FT3, FF3_GROUP):
            tiles = min(FF3_GROUP, FT3 - base)
            up(base, tiles)
            linear(core, f"down3_{base}", w_down[base * P:(base + tiles) * P, :], KT,
                   (add_to if base else copy_to)(nc, dst), pair=gated, kts=tiles, raw=core.work)


def third_block(core, a, c_in, g):
    nc = core.nc
    w = a["w_in_3"][0]
    w_out = a["w_out_3"][0]
    lower_bound(core, g)

    def out_views(i, s):
        c = i * (2 * P) + s * P
        heads = [(lambda d, at=AD * n: d[at:at + AD, :, :],
                  w_out[n * 256:(n + 1) * 256, ds(c, P)].rearrange("(k p) n -> p k n", p=AD)) for n in range(2)]
        return [heads, [(lambda d: d, w_out[512:1024, ds(c, P)].rearrange("(k p) n -> p k n", p=P))]]

    with ExitStack() as ctx:
        mix = core.sbuf("mix3", [P, KT * T], ctx)
        norm_operand(core, "n4", core.x, g["mix_pre_norm_3"], core.eps6)
        window_attention(core, w, c_in, g["sinks"], mix)
        hgrn(core, w, c_in, g, mix)
        linear(core, "out3", w_out, KT, copy_to(nc, mix), load=out_views, dmas=(2, 1),
               operand=Operand(core, mix, None, core.h))
        rms_norm(core, "np1", mix, g["mix_post_norm_3"], None, core.eps6, residual=core.x)
        with ExitStack() as mem_ctx:
            mem = tuple(core.sbuf(f"mem_{p}", [P, KT * MEM], mem_ctx, F32R) for p in ("hi", "lo"))
            with ExitStack() as raw_ctx:
                memT = core.sbuf("memT", [P, KT * MEM], raw_ctx)
                load_transposed(core, "mem", a["mem_3"][0], memT, MEM // P)
                rms_norm(core, "nm", memT, g["mem_norm_3"], memT, core.eps6, tok=MEM)
                split_operand(core, "ms", memT, mem, MEM)
            norm_operand(core, "n5", core.x, g["ca_pre_norm_3"], core.eps6)
            cross_attention(core, a, mem, mix)
        linear(core, "cao", a["ca_wo_3"][0], KT, copy_to(nc, mix), operand=Operand(core, mix, None, core.h))
        rms_norm(core, "np2", mix, g["ca_post_norm_3"], None, core.eps6, residual=core.x)
        conv_ffn(core, a, g["ffn_pre_norm_3"], mix)
        rms_norm(core, "np3", mix, g["ffn_post_norm_3"], None, core.eps6, residual=core.x)

def shape_constants():
    f = np.float32
    p = np.arange(P, dtype=np.float64)
    j = np.arange(T, dtype=np.float64)
    rel = j[None, :] - (T - P) - p[:, None]
    dist = np.where(rel > 0, MASKED, rel)
    log_g = np.log1p(-np.exp2(-5.0 - np.arange(HEADS)))
    d = p[None, :] - p[:, None]
    mask = np.concatenate([np.where(d >= 0, np.exp(g * np.maximum(d, 0)), 0) * RET_K_SCALE for g in log_g], 1)
    qdec = np.concatenate([np.broadcast_to(np.exp(g * (p + 1)), (P, P)) for g in log_g], 1)
    kdec = np.concatenate([np.stack([np.exp(g * (P - 1 - p)) * RET_K_SCALE for g in log_g], 1),
                           np.broadcast_to(np.exp(log_g * P), (P, HEADS))], 1)
    slopes = np.broadcast_to(np.exp2(-8.0 * np.arange(1, HEADS + 1) / HEADS), (P, HEADS))
    flip = np.kron(np.eye(2), np.eye(COLS_W)[::-1])
    c = np.arange(COLS_W)
    start = np.clip(c - NA_KC // 2, 0, COLS_W - NA_KC)
    ok = (c[None, :] >= start[:, None]) & (c[None, :] < start[:, None] + NA_KC)
    edge = np.tile(np.where(ok, 0.0, MASKED), (2, 1))
    t = np.arange(T)
    inv = np.concatenate([1.0 / (np.clip(t - w // 2 + w, 0, T) - np.clip(t - w // 2, 0, T)) for w in POOL_WINDOWS])
    inv = np.repeat(inv.reshape(2, 2, T), 64, 1).reshape(2, P, T).transpose(1, 0, 2).reshape(P, 2 * T)
    q, k = np.arange(WIN)[:, None], np.arange(2 * WIN)[None, :]
    diff = q + WIN - k
    seen = (diff >= 0) & (diff < WIN)
    window = np.where(np.concatenate([seen & (k >= WIN), seen], 1), 0.0, MASKED)
    key, query = np.arange(P)[:, None], np.arange(P)[None, :]
    levels = [np.eye(P)] + [(key // (2 * s) == query // (2 * s)) & (key // s % 2 == 0) & (query // s % 2 == 1)
                            for s in LEVELS]
    return {k: np.ascontiguousarray(v.astype(f)) for k, v in dict(
        ident=np.eye(P), dist=dist, ret_mask=mask, ret_qdec=qdec, ret_kdec=kdec, slopes=slopes,
        flip=flip, edge=edge, inv_count=inv, window=window,
        levels=np.concatenate(levels, 1)).items()}


def build(nc, a, c_in, out, blocks=(1, 2, 3)):
    with ExitStack() as ctx:
        core = Core(nc, ctx)
        g, small = {}, []
        by_tile = lambda v: v.rearrange("(k p) -> p k", p=P)
        def column(name, src, n):
            g[name] = core.sbuf("g_" + name, [P, n])
            small.append((g[name][:, :], src))
        for name in ("norm1_g", "norm2_g"):
            column(name, by_tile(a[name][0]), KT)
        column("final_norm_g", by_tile(a["final_norm_g"]), KT)
        column("diff_norm_g0", by_tile(a["diff_norm_g"][0]), 1)
        column("ret_norm_g", by_tile(a["ret_norm_g"][0]), HEADS)
        column("slopes", c_in["slopes"], HEADS)
        g["neg_lam"] = core.sbuf("g_neg_lam", [P, 1])[:, :]
        g["diff_norm_g"] = core.sbuf("g_diff_gain", [P, 1])[:, :]
        if 2 in blocks:
            second_gains(core, a, c_in, g, column, by_tile)
        if 3 in blocks:
            third_gains(core, a, c_in, g, column, by_tile)
        setup(core, c_in, small)
        with core.phase("fold") as (block,):
            @block.vector
            def _(dve):
                nc.vector.tensor_scalar(g["diff_norm_g"], g["diff_norm_g0"][:, :], 1.0 - LAMBDA_INIT, None, ALU.mult)
        load_transposed(core, "xin", a["x"][0], core.x, TT)
        if 1 in blocks:
            first_block(core, a, c_in, g)
        if 2 in blocks:
            second_block(core, a, c_in, g)
        if 3 in blocks:
            third_block(core, a, c_in, g)
        store_transposed(core, "xout", core.x, out[0])


def kernel(**inputs):
    import concourse.bacc as bacc
    from concourse.bass_utils import run_bass_kernel_spmd

    nc = bacc.Bacc("TRN2", target_bir_lowering=False, num_devices=1)
    arrays, handles, c_in = {}, {}, {}
    for name, value in inputs.items():
        v = np.ascontiguousarray(value)
        if name == "na_rpb_2":
            v = np.pad(v, ((0, 0), (0, 0), (0, 0), (RPB_PAD, RPB_PAD)))
        arrays[name + "_dram"] = v
        handles[name] = nc.dram_tensor(name + "_dram", v.shape, F32, kind="ExternalInput").ap()
    for name, value in shape_constants().items():
        arrays["const_" + name] = value
        c_in[name] = nc.dram_tensor("const_" + name, value.shape, F32, kind="ExternalInput").ap()
    out = nc.dram_tensor("y_dram", (1, T, D), F32, kind="ExternalOutput").ap()
    build(nc, handles, c_in, out)
    result = run_bass_kernel_spmd(nc, [arrays], core_ids=[0])
    return result.results[0]["y_dram"]
```

```python
import math
from contextlib import ExitStack, contextmanager

import numpy as np
import concourse.bass as bass
from concourse import mybir

F32 = mybir.dt.float32
F32R = mybir.dt.float32r
ALU = mybir.AluOpType
ACT = mybir.ActivationFunctionType
AX = mybir.AxisListType
ds = bass.ds

P = 128
T = 1024
D = 1024
KT = D // P
TT = T // P
BANK = 512
SILU = "silu_and_others"
EXP_LN = "natural_log_exp_and_others"


class Core:

    def __init__(self, nc, ctx):
        self.nc, self.ctx, self.retired = nc, ctx, []
        sb = self.sbuf
        self.x = sb("x_resid", [P, KT * T])
        self.h = tuple(self.sbuf(f"h_{part}", [P, KT * T], dt=F32R) for part in ("hi", "lo"))
        self.work = sb("work", [P, 4 * T])
        self.rstd = sb("rstd", [P, T])
        self.ident = sb("ident", [P, P])
        self.ones = sb("ones", [P, P])
        self.eps5 = sb("eps5", [P, 1])
        self.eps6 = sb("eps6", [P, 1])
        self.ps = ctx.enter_context(nc.psum_tensor("psum_all", [P, 8 * BANK], F32))

    def sbuf(self, name, shape, ctx=None, dt=F32):
        return (ctx or self.ctx).enter_context(self.nc.sbuf_tensor(name, shape, dt))

    def bank(self, b, n=BANK, at=0):
        return self.ps[:, b * BANK + at:b * BANK + at + n]

    @contextmanager
    def phase(self, name, *signals):
        nc = self.nc
        if len(self.retired) + len(signals) > 130:
            nc.clear_and_free_semaphores(self.retired)
            nc.all_engine_barrier()
            self.retired = []
        sems = [nc.alloc_semaphore(f"{name}_{s}") for s in signals]
        with nc.Block() as block:
            yield (block, *sems)
        self.retired += sems


class Chain:

    def __init__(self, eng, sem):
        self.eng, self.sem, self.n = eng, sem, 0

    def mark(self, ins):
        ins.then_inc(self.sem, 1)
        self.n += 1

    def join(self):
        self.eng.wait_ge(self.sem, self.n)

    def link(self, ins):
        self.mark(ins)
        self.join()

    def restart(self):
        self.join()
        self.eng.sem_clear(self.sem)
        self.n = 0


def cols(buf, first, n=T):
    return buf[:, ds(first, n)]


class Weights:

    SIGNALS = ("raw0", "raw1", "hi_ready", "split_done", "used", "slot_seen")
    SLOTS = 4

    def __init__(self, core, name, ctx, of=None):
        self.core, self.nc = core, core.nc
        if of:
            self.raw, self.hi, self.lo, self.sems = of.raw, of.hi, of.lo, of.sems
            self.signals(self.sems)
            return
        self.raw = [core.sbuf(f"{name}_raw{n}", [P, 4 * P], ctx) for n in range(2)]
        self.hi = [core.sbuf(f"{name}_hi{n}", [P, 2 * P], ctx, F32R) for n in range(self.SLOTS)]
        self.lo = [core.sbuf(f"{name}_lo{n}", [P, 2 * P], ctx, F32R) for n in range(self.SLOTS)]
        self.geometry(KT, 0, (0, 0), (1, 1))

    def geometry(self, kts, before, raw_before, dmas):
        self.kts, self.before, self.raw_before, self.dmas = kts, before, raw_before, dmas
        self.chunks, self.pieces = kts // 2, max(kts // 4, 1)
        self.per_piece = self.chunks // self.pieces

    def stage(self, kts, dmas, last=None, tiles=0):
        new = Weights(self.core, None, None, self)
        if last is None:
            new.geometry(kts, 0, (0, 0), dmas)
        else:
            loads = tiles if last.pieces == 2 else tiles // 2
            new.geometry(kts, last.before + tiles * last.chunks,
                         tuple(last.raw_before[n] + 16 * last.dmas[n] * loads for n in range(2)), dmas)
        return new

    def signals(self, sems):
        self.sems = sems
        self.raw0, self.raw1, self.hi_ready, self.split_done, self.used, self.slot_seen = sems
        self.raw_loaded = (self.raw0, self.raw1)

    def load(self, sp, t, s, views):
        for r in range(self.pieces):
            slot = (s * self.pieces + r) % 2
            sp.wait_ge(self.split_done, t * self.chunks + (self.before + r * self.per_piece + self.SLOTS - self.per_piece))
            for pick, src in views[r]:
                dst = self.raw[slot][:, 0:self.kts // self.pieces * P].rearrange("p (k n) -> p k n", n=P)
                sp.dma_start(pick(dst), src).then_inc(self.raw_loaded[slot], 16)

    def parts(self, t, s):
        first = self.before + (t if isinstance(t, int) else s) * self.chunks
        for c in range(self.chunks):
            r, at = divmod(c, self.per_piece)
            yield c, (first + c) % self.SLOTS, (s * self.pieces + r) % 2, at * 2 * P

    def arrived(self, t, s, slot):
        step = 16 * self.dmas[slot]
        if self.pieces == 2:
            return t * step + (self.raw_before[slot] + step)
        return (t - s) * (step // 2) + (self.raw_before[slot] + step)

    def split_hi(self, act, t, s, in_turn=False):
        for c, slot, raw, at in self.parts(t, s):
            if c % self.per_piece == 0:
                act.wait_ge(self.raw_loaded[raw], self.arrived(t, s, raw))
            act.wait_ge(self.used, t * self.chunks + (self.before + c + 1))
            if in_turn:
                act.wait_ge(self.hi_ready, t * self.chunks + (self.before + c))
            self.nc.scalar.activation(self.hi[slot][:, :], self.raw[raw][:, at:at + 2 * P], ACT.Copy) \
                .then_inc(self.hi_ready, 1)

    def split(self, pool, t, s, chunks=None):
        for c, slot, raw, at in self.parts(t, s):
            if chunks is not None and c not in chunks:
                continue
            if c % self.per_piece == 0:
                pool.wait_ge(self.raw_loaded[raw], self.arrived(t, s, raw))
            pool.wait_ge(self.used, t * self.chunks + (self.before + c + 1))
            pool.sem_inc(self.slot_seen, 1)
            self.nc.gpsimd.tensor_copy(self.hi[slot][:, :], self.raw[raw][:, at:at + 2 * P]).then_inc(self.hi_ready, 1)
            self.lo_of(pool, t, c, slot, raw, at)

    def split_lo(self, pool, t, s):
        for c, slot, raw, at in self.parts(t, s):
            self.lo_of(pool, t, c, slot, raw, at)

    def lo_of(self, pool, t, c, slot, raw, at):
        pool.wait_ge(self.hi_ready, t * self.chunks + (self.before + c + 1))
        self.nc.gpsimd.tensor_tensor(self.lo[slot][:, :], self.raw[raw][:, at:at + 2 * P],
                                     self.hi[slot][:, :].bitcast(F32), ALU.subtract).then_inc(self.split_done, 1)

    def open_raw(self, pool):
        pool.sem_inc(self.split_done, self.SLOTS)

    def open_slots(self, pe):
        pe.sem_inc(self.used, self.SLOTS)

    def product(self, pe, out, act, t, s, tokens=T, stride=T, src_ready=None, src_before=0, chunks=None):
        hi, lo = act
        step = min(tokens, BANK)
        for c, slot, raw, _ in self.parts(t, s):
            if chunks is not None and c not in chunks:
                continue
            pe.wait_ge(self.split_done, t * self.chunks + (self.before + c + 1 + self.SLOTS))
            for k in (2 * c, 2 * c + 1):
                if src_ready is not None:
                    pe.wait_ge(src_ready, src_before + k + 1)
                w = slice((k % 2) * P, (k % 2 + 1) * P)
                for n in range(0, tokens, step):
                    a = slice(k * stride + n, k * stride + n + step)
                    for m, (wt, x) in enumerate(((self.hi, hi), (self.hi, lo), (self.lo, hi))):
                        last = self.nc.tensor.matmul(out[:, n:n + step], wt[slot][:, w], x[:, a],
                                                     start=(k == 0 and m == 0), stop=(k == self.kts - 1 and m == 2))
            last.then_inc(self.used, 1)

    def wait_product(self, eng, t):
        eng.wait_ge(self.used, t * self.chunks + (self.before + self.chunks + self.SLOTS))


def plain_views(w, kts, first):
    tiles = w[0:kts * P, ds(first, P)].rearrange("(k p) n -> p k n", p=P)
    pieces = max(kts // 4, 1)
    piece = kts // pieces
    return [[(lambda d: d, tiles[:, r * piece:(r + 1) * piece, :])] for r in range(pieces)]



def setup(core, c_in, small):
    nc = core.nc
    with core.phase("setup", "loaded") as (block, loaded):
        @block.sync
        def _(sp):
            sp.dma_start(core.ident[:, :], c_in["ident"]).then_inc(loaded, 16)
            for dst, src in small:
                with nc.allow_non_contiguous_dma("gains, one column a partition"):
                    sp.dma_start(dst, src).then_inc(loaded, 16)
            sp.wait_ge(loaded, 16 * (1 + len(small)))

        @block.vector
        def _(dve):
            nc.vector.memset(core.ones[:, :], 1.0)
            nc.vector.memset(core.eps5[:, :], 1e-5)
            nc.vector.memset(core.eps6[:, :], 1e-6)


def load_transposed(core, name, src, dst, tiles):
    nc, ctx = core.nc, ExitStack()
    stage, tok = core.sbuf(name + "_stage", [P, tiles * D], ctx), tiles * P
    group = min(4, tiles)
    steps = [(k, g) for g in range(tiles // group) for k in range(KT)]
    with core.phase(name, "loaded", "turned", "taken") as (block, loaded, turned, taken):
        @block.sync
        def _(sp):
            sp.dma_start(stage[:, 0:tiles * D].rearrange("p (t d) -> p t d", t=tiles),
                         src.rearrange("(t p) d -> p t d", p=P)).then_inc(loaded, 16)

        @block.tensor
        def _(pe):
            pe.wait_ge(loaded, 16)
            for n, (k, g) in enumerate(steps):
                if n >= 4:
                    pe.wait_ge(taken, n - 3)
                for j in range(group):
                    t = g * group + j
                    last = nc.tensor.transpose(core.bank(n % 4, P, j * P),
                                               stage[:, t * D + k * P:t * D + (k + 1) * P], core.ident[:, :])
                last.then_inc(turned, 1)

        @block.vector
        def _(dve):
            for n, (k, g) in enumerate(steps):
                dve.wait_ge(turned, n + 1)
                at = k * tok + g * group * P
                nc.vector.tensor_copy(dst[:, at:at + group * P], core.bank(n % 4, group * P)).then_inc(taken, 1)
    ctx.close()


def store_transposed(core, name, src, out):
    nc, ctx = core.nc, ExitStack()
    stage = core.sbuf(name + "_stage", [P, TT * D], ctx)
    with core.phase(name, "turned", "taken", "stored") as (block, turned, taken, stored):
        @block.tensor
        def _(pe):
            for t in range(TT):
                if t >= 2:
                    pe.wait_ge(taken, t - 1)
                for k in range(KT):
                    last = nc.tensor.transpose(core.bank(2 * (t % 2), P, k * P),
                                               src[:, k * T + t * P:k * T + (t + 1) * P], core.ident[:, :])
                last.then_inc(turned, 1)

        @block.vector
        def _(dve):
            for t in range(TT):
                dve.wait_ge(turned, t + 1)
                nc.vector.tensor_copy(stage[:, t * D:(t + 1) * D],
                                      core.bank(2 * (t % 2), D)).then_inc(taken, 1)

        @block.sync
        def _(sp):
            for t in range(TT):
                sp.wait_ge(taken, t + 1)
                sp.dma_start(out[t * P:(t + 1) * P, :], stage[:, t * D:(t + 1) * D]).then_inc(stored, 16)
            sp.wait_ge(stored, 16 * TT)
    ctx.close()



def rms_norm(core, name, src, gain, dst, eps, tok=T, residual=None, squared_before=False):
    nc = core.nc
    acc, sq = core.work[:, 0:tok], core.work[:, T:3 * T]
    tmp = core.work[:, T:3 * T]
    step = min(tok, BANK)
    sems = ("squared", "summed", "stat_ready", "rstd_ready", "act_own", "dve_own")
    with core.phase(name, *sems) as (block, squared, summed, stat_ready, rstd_ready, act_own, dve_own):
        @block.scalar
        def _(act):
            own = Chain(act, act_own)
            nc.scalar.preload_act_table_set(EXP_LN)
            for k in range(0 if squared_before else KT):
                if k == 0:
                    nc.scalar.activation(acc, src[:, 0:tok], ACT.Square).then_inc(squared, 1)
                    continue
                if k >= 3:
                    act.wait_ge(summed, k - 2)
                nc.scalar.activation(sq[:, (k % 2) * T:(k % 2) * T + tok], src[:, k * tok:(k + 1) * tok],
                                     ACT.Square).then_inc(squared, 1)
            act.wait_ge(stat_ready, 1)
            own.link(nc.scalar.activation(core.rstd[:, 0:tok], core.ps[:, 0:tok], ACT.Ln,
                                          bias=eps[:, :], scale=1.0 / D))
            nc.scalar.activation(core.rstd[:, 0:tok], core.rstd[:, 0:tok], ACT.Exp, scale=-0.5).then_inc(rstd_ready, 1)

        @block.vector
        def _(dve):
            own = Chain(dve, dve_own)
            for k in range(1, 1 if squared_before else KT):
                dve.wait_ge(squared, k + 1)
                if k > 1:
                    dve.wait_ge(summed, k - 1)
                nc.vector.tensor_tensor(acc, acc, sq[:, (k % 2) * T:(k % 2) * T + tok], ALU.add).then_inc(summed, 1)
            dve.wait_ge(rstd_ready, 1)
            for k in range(KT):
                part = slice(k * tok, (k + 1) * tok)
                if residual is None:
                    nc.vector.scalar_tensor_tensor(out=dst[:, part], in0=src[:, part], scalar=gain[:, k:k + 1],
                                                   in1=core.rstd[:, 0:tok], op0=ALU.mult, op1=ALU.mult)
                else:
                    t = tmp[:, (k % 2) * T:(k % 2) * T + tok]
                    own.link(nc.vector.scalar_tensor_tensor(out=t, in0=src[:, part], scalar=gain[:, k:k + 1],
                                                            in1=core.rstd[:, 0:tok], op0=ALU.mult, op1=ALU.mult))
                    own.mark(nc.vector.tensor_tensor(residual[:, part], residual[:, part], t, ALU.add))

        @block.tensor
        def _(pe):
            if not squared_before:
                pe.wait_ge(summed, KT - 1)
            for c in range(0, tok, step):
                last = nc.tensor.matmul(core.ps[:, c:c + step], core.ones[:, :], acc[:, c:c + step],
                                        start=True, stop=True)
            last.then_inc(stat_ready, 1)


class Operand:

    SIGNALS = ("hi_made", "src_ready", "squared", "summed", "stat_ready", "rstd_ready", "norm_own")

    def __init__(self, core, src, gain, pair, eps=None, tok=T, tiles=KT):
        self.core, self.nc = core, core.nc
        self.src, self.gain, self.pair, self.eps, self.tok, self.tiles = src, gain, pair, eps, tok, tiles
        self.acc, self.sq = core.work[:, 0:tok], [core.work[:, (1 + n) * T:(1 + n) * T + tok] for n in range(2)]

    def signals(self, sems):
        (self.hi_made, self.src_ready, self.squared, self.summed, self.stat_ready, self.rstd_ready,
         self.norm_own) = sems

    def part(self, k):
        return slice(k * self.tok, (k + 1) * self.tok)

    def act_hi(self, act):
        for k in range(self.tiles):
            scale = 1.0 if self.gain is None else self.gain[:, k:k + 1]
            self.nc.scalar.activation(self.pair[0][:, self.part(k)], self.src[:, self.part(k)], ACT.Copy, scale=scale) \
                .then_inc(self.hi_made, 1)

    def act_squares(self, act):
        for k in range(self.tiles):
            if k >= 3:
                act.wait_ge(self.summed, k - 2)
            self.nc.scalar.activation(self.acc if k == 0 else self.sq[k % 2], self.src[:, self.part(k)], ACT.Square) \
                .then_inc(self.squared, 1)

    def act_rstd(self, act):
        own = Chain(act, self.norm_own)
        rstd = self.core.rstd[:, 0:self.tok]
        self.nc.scalar.preload_act_table_set(EXP_LN)
        act.wait_ge(self.stat_ready, 1)
        own.link(self.nc.scalar.activation(rstd, self.core.ps[:, 6 * BANK:6 * BANK + self.tok], ACT.Ln,
                                           bias=self.eps[:, :], scale=1.0 / (self.tiles * P)))
        self.nc.scalar.activation(rstd, rstd, ACT.Exp, scale=-0.5).then_inc(self.rstd_ready, 1)

    def dve_lo(self, dve):
        for k in range(self.tiles):
            dve.wait_ge(self.hi_made, k + 1)
            hi = self.pair[0][:, self.part(k)].bitcast(F32)
            lo, x = self.pair[1][:, self.part(k)], self.src[:, self.part(k)]
            if self.gain is None:
                ins = self.nc.vector.tensor_tensor(lo, x, hi, ALU.subtract)
            else:
                ins = self.nc.vector.scalar_tensor_tensor(out=lo, in0=x, scalar=self.gain[:, k:k + 1], in1=hi,
                                                          op0=ALU.mult, op1=ALU.subtract)
            ins.then_inc(self.src_ready, 1)

    def dve_sum(self, dve):
        for k in range(1, self.tiles):
            dve.wait_ge(self.squared, k + 1)
            if k > 1:
                dve.wait_ge(self.summed, k - 1)
            self.nc.vector.tensor_tensor(self.acc, self.acc, self.sq[k % 2], ALU.add).then_inc(self.summed, 1)

    def pe_stat(self, pe):
        pe.wait_ge(self.summed, self.tiles - 1)
        step = min(self.tok, BANK)
        for c in range(0, self.tok, step):
            last = self.nc.tensor.matmul(self.core.ps[:, 6 * BANK + c:6 * BANK + c + step], self.core.ones[:, :],
                                         self.acc[:, c:c + step], start=True, stop=True)
        last.then_inc(self.stat_ready, 1)


def split_operand(core, name, src, pair, tok):
    op = Operand(core, src, None, pair, None, tok)
    with core.phase(name, *Operand.SIGNALS) as (block, *sems):
        op.signals(sems)

        @block.scalar
        def _(act):
            op.act_hi(act)

        @block.vector
        def _(dve):
            op.dve_lo(dve)


def norm_operand(core, name, src, gain, eps, pair=None, tok=T):
    op = Operand(core, src, gain, pair or core.h, eps, tok)
    with core.phase(name, *Operand.SIGNALS) as (block, *sems):
        op.signals(sems)

        @block.scalar
        def _(act):
            op.act_squares(act)
            op.act_hi(act)
            op.act_rstd(act)

        @block.vector
        def _(dve):
            op.dve_sum(dve)
            op.dve_lo(dve)

        @block.tensor
        def _(pe):
            op.pe_stat(pe)



class Stage:

    def __init__(self, w, tiles, take, pair, kts=KT, load=None, dmas=(1, 1), mid=None, mids=(0, 1), finish=None,
                 feeds=(), unroll=False):
        self.w, self.tiles, self.take, self.pair, self.kts, self.dmas = w, tiles, take, pair, kts, dmas
        self.load = load or (lambda i, s: plain_views(w, kts, i * (2 * P) + s * P))
        self.mid, self.mids, self.finish, self.feeds, self.unroll = mid, mids if mid else (), finish, feeds, unroll
        self.turns = tiles // 2
        self.straight = kts < 4

    def after(self, wt, last):
        self.wt = wt.stage(self.kts, self.dmas, last and last.wt, last and last.tiles)
        self.tiles_before = last.tiles_before + last.tiles if last else 0
        self.mids_before = last.mids_before + len(last.mids) * last.turns if last else 0
        self.fed_before = last.fed_before + len(last.feeds) * last.turns if last else 0
        self.src_before = last.fed_before if last and last.feeds else None

    def loop(self, eng, body, straight=False):
        straight = straight or self.straight
        for i in range(self.turns if straight else 1):
            for s in range(2):
                body(i, s)
        if self.turns > 1 and not straight:
            with eng.Fori(1, self.turns) as i:
                for s in range(2):
                    body(i, s)


def linears(core, name, stages, operand=None):
    nc = core.nc
    stats = operand is not None and operand.eps is not None
    prod = [core.ps[:, 2 * s * BANK:2 * s * BANK + T] for s in range(2)]
    ctx = ExitStack()
    stream = Weights(core, name, ctx)
    sems = Weights.SIGNALS + ("taken", "mid_done", "fed", "dve_own") + (Operand.SIGNALS if operand else ())
    with core.phase(name, *sems) as (block, *got):
        stream.signals(got[:6])
        taken, mid_done, fed, dve_own = got[6:10]
        if operand:
            operand.signals(got[10:])
        for st, last in zip(stages, [None] + stages[:-1]):
            st.after(stream, last)

        @block.sync
        def _(sp):
            for st in stages:
                st.loop(sp, lambda i, s: st.wt.load(sp, i * 2 + s, s, st.load(i, s)))

        @block.gpsimd
        def _(pool):
            stream.open_raw(pool)
            for st in stages:
                st.loop(pool, lambda i, s: st.wt.split_lo(pool, i * 2 + s, s))

        @block.tensor
        def _(pe):
            stream.open_slots(pe)

            def body(st, i, s):
                first = isinstance(i, int) and i == 0
                if not (first and st.tiles_before == 0):
                    pe.wait_ge(taken, i * 2 + (st.tiles_before + s - 1))
                if operand and st is stages[0] and first:
                    ready, before = operand.src_ready, 0
                elif st.src_before is not None and first and s == 0:
                    ready, before = fed, st.src_before
                else:
                    ready, before = None, 0
                run = lambda chunks: st.wt.product(pe, prod[s], st.pair, i * 2 + s, s, src_ready=ready,
                                                   src_before=before, chunks=chunks)
                if stats and st is stages[0] and first and s == 1:
                    run((0, 1, 2))
                    operand.pe_stat(pe)
                    run((3,))
                else:
                    run(None)
            for st in stages:
                st.loop(pe, lambda i, s: body(st, i, s))

        @block.scalar
        def _(act):
            def middle(st, i, s):
                if s in st.mids:
                    act.wait_ge(taken, i * 2 + (st.tiles_before + s + 1))
                    st.mid(act, i, s).then_inc(mid_done, 1)

            def turn(st, i, before):
                st.wt.split_hi(act, i * 2, 0)
                if operand and st is stages[0] and isinstance(i, int) and i == 0:
                    operand.act_hi(act)
                if before:
                    middle(*before)
                st.wt.split_hi(act, i * 2 + 1, 1)
                if stats and st is stages[0] and isinstance(i, int) and i == 0:
                    operand.act_squares(act)
                    operand.act_rstd(act)
                middle(st, i, 0)

            before = None
            for st in stages:
                turn(st, 0, before)
                if st.straight:
                    for i in range(1, st.turns):
                        turn(st, i, (st, i - 1, 1))
                elif st.turns > 1:
                    with act.Fori(1, st.turns) as i:
                        turn(st, i, (st, i - 1, 1))
                before = (st, st.turns - 1, 1)
            middle(*before)

        @block.vector
        def _(dve):
            if operand:
                operand.dve_lo(dve)
                if stats:
                    operand.dve_sum(dve)
                    dve.wait_ge(operand.rstd_ready, 1)

            def body(st, i, s):
                own = Chain(dve, dve_own)
                st.wt.wait_product(dve, i * 2 + s)
                own.link(st.take(dve, own, i, s, prod[s]))
                dve.sem_inc(taken, 1)
                if st.mids and st.finish and (s == 1 or len(st.mids) == 2):
                    done = s + 1 if len(st.mids) == 2 else 1
                    dve.wait_ge(mid_done, i * len(st.mids) + (st.mids_before + done))
                if st.finish:
                    st.finish(dve, own, i, s)
                if s in st.feeds:
                    dve.sem_inc(fed, 1)
                own.restart()
            for st in stages:
                st.loop(dve, lambda i, s: body(st, i, s), st.unroll)
    ctx.close()


def linear(core, name, w, tiles, take, pair=None, operand=None, **more):
    linears(core, name, [Stage(w, tiles, take, pair or core.h, **more)], operand)


def add_to(nc, dst):
    def take(dve, own, i, s, product):
        part = cols(dst, i * (2 * T) + s * T)
        return nc.vector.tensor_tensor(part, part, product, ALU.add)
    return take


def copy_to(nc, dst, at=0):
    def take(dve, own, i, s, product):
        return nc.vector.tensor_copy(cols(dst, i * (2 * T) + (s * T + at)), product)
    return take


def scale_to(core, dst, at=0):
    def take(dve, own, i, s, product):
        return core.nc.vector.tensor_tensor(cols(dst, i * (2 * T) + (s * T + at)), product, core.rstd[:, :], ALU.mult)
    return take


def sum_squares(core, dst):
    nc = core.nc
    acc, sq = core.work[:, 0:T], [core.work[:, (1 + s) * T:(2 + s) * T] for s in range(2)]

    def square(act, i, s):
        return nc.scalar.activation(sq[s], cols(dst, i * (2 * T) + s * T), ACT.Square)

    def add(dve, own, i, s):
        if isinstance(i, int) and i == 0 and s == 0:
            own.link(nc.vector.tensor_copy(acc, sq[0]))
        else:
            own.link(nc.vector.tensor_tensor(acc, acc, sq[s], ALU.add))
    return dict(mid=square, finish=add)



HEADS = 4
HD = 128
DIFF = 512
LAMBDA_INIT = 0.8 - 0.6 * math.exp(-0.3 * 0)
RET_K_SCALE = HD ** -0.5
FF1 = 4096
FT1 = FF1 // P
MASKED = -1e30


def lambda_phase(core, lam_in, out):
    nc = core.nc
    n = 64
    vec, prod, sc = core.work[:, 0:4 * n], core.work[:, 4 * n:6 * n], core.work[:, 6 * n:6 * n + 8]
    with core.phase("lam", "loaded", "dotted", "exped", "dve_own") as (block, loaded, dotted, exped, dve_own):
        @block.sync
        def _(sp):
            for j, v in enumerate(lam_in):
                sp.dma_start(vec[:, j * n:(j + 1) * n], v.to_broadcast([P, n])).then_inc(loaded, 16)

        @block.vector
        def _(dve):
            own = Chain(dve, dve_own)
            dve.wait_ge(loaded, 64)
            for j in range(2):
                own.mark(nc.vector.tensor_tensor(prod[:, j * n:(j + 1) * n], vec[:, 2 * j * n:(2 * j + 1) * n],
                                                 vec[:, (2 * j + 1) * n:(2 * j + 2) * n], ALU.mult))
            own.join()
            for j in range(2):
                nc.vector.reduce_sum(sc[:, j:j + 1], prod[:, j * n:(j + 1) * n], axis=AX.X).then_inc(dotted, 1)
            dve.wait_ge(exped, 1)
            own.link(nc.vector.tensor_tensor(sc[:, 4:5], sc[:, 3:4], sc[:, 2:3], ALU.subtract))
            nc.vector.tensor_scalar(out, sc[:, 4:5], -LAMBDA_INIT, None, ALU.add)

        @block.scalar
        def _(act):
            act.wait_ge(dotted, 2)
            nc.scalar.activation(sc[:, 2:4], sc[:, 0:2], ACT.Exp).then_inc(exped, 1)


def diff_attention(core, w, c_in, mix, diff_gain, neg_lam, slopes):
    nc, h = core.nc, core.h
    with ExitStack() as ctx:
        sb = lambda n, shape: core.sbuf("da_" + n, shape, ctx)
        wt = Weights(core, "da", ctx)
        qT, kT, vT = core.work[:, T:2 * T], sb("kT", [P, T]), core.work[:, 2 * T:3 * T]
        v_tok = sb("v_tok", [P, T])
        dist = sb("dist", [P, T])
        probs = sb("probs", [P, 3 * 2 * T])
        aT = sb("aT", [P, 2 * T])
        col = sb("col", [P, 2 * 8])
        oT, sq, hrstd = core.work[:, 0:T], qT, core.work[:, 3 * T:4 * T]
        sems = Weights.SIGNALS + ("const", "q_k_v_ready", "v_turned", "v_ready", "scores_ready",
                "scores_taken", "max_ready", "exp_ready", "a_ready", "a_turned", "aT_ready", "pv_done",
                "o_ready", "sq_ready", "stat_ready", "rstd_ready", "head_done", "dve_own", "act_own")
        with core.phase("da", *sems) as (
                block, *ws, const, qkv_ready, v_turned, v_ready, scores_ready,
                scores_taken, max_ready, exp_ready, a_ready, a_turned, aT_ready, pv_done,
                o_ready, sq_ready, stat_ready, rstd_ready, head_done, dve_own, act_own):
            wt.signals(ws)
            C = lambda q, what, m: col[:, (q % 2) * 8 + 2 * what + m:(q % 2) * 8 + 2 * what + m + 1]

            @block.sync
            def _(sp):
                sp.dma_start(dist[:, :], c_in["dist"]).then_inc(const, 16)
                with sp.Fori(0, HEADS) as i:
                    for j in range(3):
                        wt.load(sp, i * 3 + j, 0, plain_views(w, KT, i * HD + j * DIFF))

            @block.gpsimd
            def _(pool):
                wt.open_raw(pool)
                with pool.Fori(0, HEADS) as i:
                    for j in range(3):
                        wt.split(pool, i * 3 + j, 0)

            @block.tensor
            def _(pe):
                wt.open_slots(pe)

                def scores(i, q):
                    if q >= 1:
                        pe.wait_ge(scores_taken, i * 8 + q)
                    width = (q + 1) * P
                    for m in range(2):
                        for c in range(0, width, BANK):
                            n = min(BANK, width - c)
                            last = nc.tensor.matmul(core.bank(4 + 2 * m, n, c), qT[64 * m:64 * m + 64, q * P:(q + 1) * P],
                                                    kT[64 * m:64 * m + 64, c:c + n], start=True, stop=True)
                    last.then_inc(scores_ready, 1)

                def weigh(i, q):
                    pe.wait_ge(aT_ready, i * 8 + (q + 1))
                    for t in range(q + 1):
                        at = (q % 2) * T + t * P
                        last = nc.tensor.matmul(core.bank(2, P, q * P), v_tok[:, t * P:(t + 1) * P], aT[:, at:at + P],
                                                start=(t == 0), stop=(t == q))
                    last.then_inc(pv_done, 1)

                with pe.Fori(0, HEADS) as i:
                    for j in range(3):
                        if j == 2:
                            pe.wait_ge(qkv_ready, i * 3 + 1)
                        wt.product(pe, core.bank(2 * (j % 2), T), h, i * 3 + j, 0)
                    pe.wait_ge(qkv_ready, i * 3 + 3)
                    for t in range(TT):
                        last = nc.tensor.transpose(core.bank(2, P, t * P), vT[:, t * P:(t + 1) * P], core.ident[:, :])
                    last.then_inc(v_turned, 1)
                    scores(i, 0)
                    pe.wait_ge(v_ready, i + 1)
                    scores(i, 1)
                    for q in range(TT):
                        if q + 2 < TT:
                            scores(i, q + 2)
                        pe.wait_ge(a_ready, i * 8 + (q + 1))
                        if q >= 1:
                            pe.wait_ge(aT_ready, i * 8 + q)
                        for t in range(q + 1):
                            at = (q % 3) * 2 * T + t * P
                            last = nc.tensor.transpose(core.bank(0, P, t * P), probs[:, at:at + P], core.ident[:, :])
                        last.then_inc(a_turned, 1)
                        if q >= 1:
                            weigh(i, q - 1)
                    weigh(i, TT - 1)
                    pe.wait_ge(sq_ready, i + 1)
                    for c in range(0, T, BANK):
                        last = nc.tensor.matmul(core.bank(4, BANK, c), core.ones[:, :], sq[:, c:c + BANK],
                                                start=True, stop=True)
                    last.then_inc(stat_ready, 1)

            @block.scalar
            def _(act):
                with act.Fori(0, HEADS) as i:
                    own = Chain(act, act_own)
                    nc.scalar.preload_act_table_set(EXP_LN)
                    act.wait_ge(v_turned, i + 1)
                    nc.scalar.activation(v_tok[:, :], core.bank(2, T), ACT.Identity).then_inc(v_ready, 1)
                    def turned(q):
                        act.wait_ge(a_turned, i * 8 + (q + 1))
                        if q >= 2:
                            act.wait_ge(pv_done, i * 8 + (q - 1))
                        nc.scalar.activation(aT[:, (q % 2) * T:(q % 2) * T + (q + 1) * P], core.bank(0, (q + 1) * P),
                                             ACT.Identity).then_inc(aT_ready, 1)
                    for q in range(TT):
                        for m in range(2):
                            act.wait_ge(max_ready, i * 16 + (2 * q + m + 1))
                            s = probs[:, ((q % 3) * 2 + m) * T:((q % 3) * 2 + m) * T + (q + 1) * P]
                            nc.scalar.activation(s, s, ACT.Exp, bias=C(q, 0, m),
                                                 accum_out=C(q, 1, m)).then_inc(exp_ready, 1)
                        if q >= 1:
                            turned(q - 1)
                    turned(TT - 1)
                    act.wait_ge(pv_done, i * 8 + TT)
                    own.link(nc.scalar.activation(oT, core.bank(2, T), ACT.Identity))
                    nc.scalar.activation(sq, oT, ACT.Square).then_inc(sq_ready, 1)
                    act.wait_ge(stat_ready, i + 1)
                    own.link(nc.scalar.activation(hrstd, core.bank(4, T), ACT.Ln, bias=core.eps5[:, :],
                                                  scale=1.0 / HD))
                    nc.scalar.activation(hrstd, hrstd, ACT.Exp, scale=-0.5).then_inc(rstd_ready, 1)
                    own.restart()

            @block.vector
            def _(dve):
                dve.wait_ge(const, 16)
                with dve.Fori(0, HEADS) as i:
                    own = Chain(dve, dve_own)
                    def soft(q):
                        width = (q + 1) * P
                        dve.wait_ge(scores_ready, i * 8 + (q + 1))
                        if q >= 3:
                            dve.wait_ge(a_turned, i * 8 + (q - 2))
                        for m in range(2):
                            s = probs[:, ((q % 3) * 2 + m) * T:((q % 3) * 2 + m) * T + width]
                            own.mark(nc.vector.scalar_tensor_tensor(
                                out=s, in0=dist[:, T - width:T], scalar=cols(slopes, i, 1),
                                in1=core.bank(4 + 2 * m, width), op0=ALU.mult, op1=ALU.add))
                        own.join()
                        dve.sem_inc(scores_taken, 1)
                        for m in range(2):
                            s = probs[:, ((q % 3) * 2 + m) * T:((q % 3) * 2 + m) * T + width]
                            nc.vector.tensor_reduce(out=C(q, 0, m), in_=s, axis=AX.X, op=ALU.max,
                                                    negate=True).then_inc(max_ready, 1)

                    def combine(q):
                        width = (q + 1) * P
                        dve.wait_ge(exp_ready, i * 16 + (2 * q + 2))
                        s0 = probs[:, (q % 3) * 2 * T:(q % 3) * 2 * T + width]
                        s1 = probs[:, ((q % 3) * 2 + 1) * T:((q % 3) * 2 + 1) * T + width]
                        own.link(nc.vector.reciprocal(col[:, (q % 2) * 8 + 4:(q % 2) * 8 + 6],
                                                      col[:, (q % 2) * 8 + 2:(q % 2) * 8 + 4]))
                        own.mark(nc.vector.tensor_tensor(C(q, 3, 0), C(q, 2, 1), neg_lam, ALU.mult))
                        own.mark(nc.vector.tensor_scalar(s0, s0, C(q, 2, 0), None, ALU.mult))
                        own.join()
                        nc.vector.scalar_tensor_tensor(out=s0, in0=s1, scalar=C(q, 3, 0), in1=s0,
                                                       op0=ALU.mult, op1=ALU.add).then_inc(a_ready, 1)

                    for j, (dst, scale) in enumerate(((qT, 64 ** -0.5), (kT[:, :], 1.0), (vT, 1.0))):
                        wt.wait_product(dve, i * 3 + j)
                        own.link(nc.vector.scalar_tensor_tensor(out=dst, in0=core.bank(2 * (j % 2), T), scalar=scale,
                                                                in1=core.rstd[:, :], op0=ALU.mult, op1=ALU.mult))
                        dve.sem_inc(qkv_ready, 1)
                    soft(0)
                    for q in range(TT):
                        if q + 1 < TT:
                            soft(q + 1)
                        combine(q)
                    dve.wait_ge(rstd_ready, i + 1)
                    own.link(nc.vector.scalar_tensor_tensor(out=cols(mix, i * T), in0=oT, scalar=diff_gain,
                                                            in1=hrstd, op0=ALU.mult, op1=ALU.mult))
                    dve.sem_inc(head_done, 1)
                    own.restart()


def retention(core, w, c_in, mix, gain):
    nc, h = core.nc, core.h
    first = 3 * DIFF
    with ExitStack() as ctx:
        sb = lambda n, shape: core.sbuf("re_" + n, shape, ctx)
        wt = Weights(core, "re", ctx)
        qT, kT, gT = (sb(n, [P, T]) for n in ("qT", "kT", "gT"))
        vT = core.work[:, 2 * T:3 * T]
        qd = sb("q_decayed", [P, T])
        k_tok, v_tok, intra = sb("k_tok", [P, T]), sb("v_tok", [P, T]), sb("intra", [P, T])
        state = sb("state", [P, T])
        mask = sb("mask", [P, HEADS * P])
        qdec = sb("qdec", [P, HEADS * P])
        kdec = sb("kdec", [P, 2 * HEADS])
        oT, sq, hrstd = core.work[:, 0:T], core.work[:, T:2 * T], core.work[:, 3 * T:4 * T]
        sems = Weights.SIGNALS + ("const", "q_ready", "turned", "kv_ready", "intra_ready",
                "intra_masked", "update_ready", "state_ready", "o_done", "sq_ready", "stat_ready",
                "rstd_ready", "dve_own", "act_own", "mix_done", "v_ready", "silu_done")
        with core.phase("re", *sems) as (
                block, *ws, const, q_ready, turned, kv_ready, intra_ready,
                intra_masked, update_ready, state_ready, o_done, sq_ready, stat_ready,
                rstd_ready, dve_own, act_own, mix_done, v_ready, silu_done):
            wt.signals(ws)

            @block.sync
            def _(sp):
                for dst, name in ((mask, "ret_mask"), (qdec, "ret_qdec"), (kdec, "ret_kdec")):
                    sp.dma_start(dst[:, :], c_in[name]).then_inc(const, 16)
                with sp.Fori(0, HEADS) as i:
                    for j in range(4):
                        wt.load(sp, i * 4 + j, 0, plain_views(w, KT, i * HD + (first + j * DIFF)))

            @block.gpsimd
            def _(pool):
                wt.open_raw(pool)
                with pool.Fori(0, HEADS) as i:
                    for j in range(4):
                        wt.split(pool, i * 4 + j, 0)

            @block.tensor
            def _(pe):
                wt.open_slots(pe)
                with pe.Fori(0, HEADS) as i:
                    for j in range(4):
                        if j >= 2:
                            pe.wait_ge(q_ready, i * 4 + (j - 1))
                        wt.product(pe, core.bank(2 * (j % 2), T), h, i * 4 + j, 0)
                    pe.wait_ge(q_ready, i * 4 + 3)
                    for src, b in ((kT, 4), (vT, 6)):
                        for c in range(TT):
                            last = nc.tensor.transpose(core.bank(b, P, c * P), src[:, c * P:(c + 1) * P], core.ident[:, :])
                        last.then_inc(turned, 1)
                    pe.wait_ge(q_ready, i * 4 + 4)
                    for c in range(TT):
                        last = nc.tensor.matmul(core.bank(0, P, c * P), kT[:, c * P:(c + 1) * P], qT[:, c * P:(c + 1) * P],
                                                start=True, stop=True)
                    last.then_inc(intra_ready, 1)
                    pe.wait_ge(kv_ready, i + 1)
                    pe.wait_ge(v_ready, i + 1)
                    for c in range(TT - 1):
                        last = nc.tensor.matmul(core.bank(2, P, c * P), k_tok[:, c * P:(c + 1) * P],
                                                v_tok[:, c * P:(c + 1) * P], start=True, stop=True)
                    last.then_inc(update_ready, 1)
                    pe.wait_ge(intra_masked, i + 1)
                    pe.wait_ge(state_ready, i + 1)
                    for c in range(TT):
                        last = nc.tensor.matmul(core.bank(4, P, c * P), v_tok[:, c * P:(c + 1) * P],
                                                intra[:, c * P:(c + 1) * P], start=True, stop=(c == 0))
                        if c:
                            last = nc.tensor.matmul(core.bank(4, P, c * P), state[:, c * P:(c + 1) * P],
                                                    qd[:, c * P:(c + 1) * P], start=False, stop=True)
                    last.then_inc(o_done, 1)
                    pe.wait_ge(sq_ready, i + 1)
                    for c in range(0, T, BANK):
                        last = nc.tensor.matmul(core.bank(6, BANK, c), core.ones[:, :], sq[:, c:c + BANK],
                                                start=True, stop=True)
                    last.then_inc(stat_ready, 1)

            @block.scalar
            def _(act):
                with act.Fori(0, HEADS) as i:
                    own = Chain(act, act_own)
                    nc.scalar.preload_act_table_set(SILU)
                    act.wait_ge(q_ready, i * 4 + 4)
                    nc.scalar.activation(gT[:, :], gT[:, :], ACT.Silu).then_inc(silu_done, 1)
                    act.wait_ge(turned, i * 2 + 2)
                    nc.scalar.activation(v_tok[:, :], core.bank(6, T), ACT.Identity).then_inc(v_ready, 1)
                    nc.scalar.preload_act_table_set(EXP_LN)
                    act.wait_ge(o_done, i + 1)
                    own.link(nc.scalar.activation(oT, core.bank(4, T), ACT.Identity))
                    nc.scalar.activation(sq, oT, ACT.Square).then_inc(sq_ready, 1)
                    act.wait_ge(stat_ready, i + 1)
                    own.link(nc.scalar.activation(hrstd, core.bank(6, T), ACT.Ln, bias=core.eps5[:, :],
                                                  scale=1.0 / HD))
                    own.link(nc.scalar.activation(hrstd, hrstd, ACT.Exp, scale=-0.5))
                    act.sem_inc(rstd_ready, 1)
                    own.restart()
                    act.wait_ge(mix_done, i + 1)

            @block.vector
            def _(dve):
                dve.wait_ge(const, 48)
                nc.vector.memset(state[:, 0:P], 0.0)
                with dve.Fori(0, HEADS) as i:
                    own = Chain(dve, dve_own)
                    v3 = lambda b: b[:, 0:T].rearrange("p (c n) -> p c n", n=P)
                    for j, dst in enumerate((qT, kT, vT, gT)):
                        wt.wait_product(dve, i * 4 + j)
                        own.link(nc.vector.tensor_tensor(dst[:, :], core.bank(2 * (j % 2), T), core.rstd[:, :], ALU.mult))
                        dve.sem_inc(q_ready, 1)
                    own.mark(nc.vector.tensor_tensor(
                        v3(qd), v3(qT), cols(qdec, i * P, P).unsqueeze(1).to_broadcast([P, TT, P]), ALU.mult))
                    dve.wait_ge(turned, i * 2 + 1)
                    own.mark(nc.vector.tensor_scalar(k_tok[:, :], core.bank(4, T), cols(kdec, i, 1), None, ALU.mult))
                    own.join()
                    dve.sem_inc(kv_ready, 1)
                    dve.wait_ge(intra_ready, i + 1)
                    for b in range(2):
                        own.mark(nc.vector.tensor_tensor(
                            intra[:, b * BANK:(b + 1) * BANK].rearrange("p (c n) -> p c n", n=P),
                            core.bank(b).rearrange("p (c n) -> p c n", n=P),
                            cols(mask, i * P, P).unsqueeze(1).to_broadcast([P, BANK // P, P]), ALU.mult))
                    own.join()
                    dve.sem_inc(intra_masked, 1)
                    dve.wait_ge(update_ready, i + 1)
                    for c in range(TT - 1):
                        own.link(nc.vector.scalar_tensor_tensor(
                            out=state[:, (c + 1) * P:(c + 2) * P], in0=state[:, c * P:(c + 1) * P],
                            scalar=cols(kdec, i + HEADS, 1), in1=core.bank(2, P, c * P), op0=ALU.mult, op1=ALU.add))
                    dve.sem_inc(state_ready, 1)
                    dve.wait_ge(rstd_ready, i + 1)
                    dve.wait_ge(silu_done, i + 1)
                    own.link(nc.vector.scalar_tensor_tensor(out=sq, in0=oT, scalar=cols(gain, i, 1),
                                                            in1=hrstd, op0=ALU.mult, op1=ALU.mult))
                    own.link(nc.vector.tensor_tensor(cols(mix, i * T + HEADS * T), sq, gT[:, :], ALU.mult))
                    dve.sem_inc(mix_done, 1)
                    own.restart()


def squared_relu_ffn(core, w_up, w_down, gain):
    nc = core.nc
    with ExitStack() as ctx:
        up = tuple(core.sbuf(f"ff_up_{p}", [P, KT * T], ctx, F32R) for p in ("hi", "lo"))
        row = [core.work[:, 3 * T:4 * T], core.sbuf("ff_row", [P, T], ctx)[:, :]]

        def scaled(dve, own, i, s, product):
            return nc.vector.tensor_tensor(row[s], product, core.rstd[:, :], ALU.mult)

        def split(dve, own, i, s):
            own.link(nc.vector.scalar_tensor_tensor(out=row[s], in0=row[s], scalar=0.0, in1=row[s],
                                                    op0=ALU.max, op1=ALU.mult))
            hi, lo = (cols(u, i * (2 * T) + s * T) for u in up)
            own.link(nc.vector.tensor_copy(hi, row[s]))
            own.link(nc.vector.tensor_tensor(lo, row[s], hi.bitcast(F32), ALU.subtract))

        stages = []
        for n in range(FT1 // KT):
            stages.append(Stage(w_up[:, n * D:(n + 1) * D], KT, scaled, core.h, finish=split, feeds=(0, 1)))
            last = n == FT1 // KT - 1
            stages.append(Stage(w_down[n * D:(n + 1) * D, :], KT, add_to(nc, core.x), up,
                                **(sum_squares(core, core.x) if last else {})))
        linears(core, "ff", stages, Operand(core, core.x, gain, core.h, core.eps5))


def first_block(core, a, c_in, g):
    nc = core.nc
    norm_operand(core, "n1", core.x, g["norm1_g"], core.eps5)
    lambda_phase(core, [a[n] for n in ("lambda_q1", "lambda_k1", "lambda_q2", "lambda_k2")], g["neg_lam"])
    with ExitStack() as ctx:
        mix = core.sbuf("mix1", [P, KT * T], ctx)
        diff_attention(core, a["w_in"][0], c_in, mix, g["diff_norm_g"], g["neg_lam"], g["slopes"])
        retention(core, a["w_in"][0], c_in, mix, g["ret_norm_g"])
        linear(core, "out1", a["w_out"][0], KT, add_to(nc, core.x), operand=Operand(core, mix, None, core.h))
    squared_relu_ffn(core, a["w_up"][0], a["w_down"][0], g["norm2_g"])
    rms_norm(core, "nf1", core.x, g["final_norm_g"], core.x, core.eps5, squared_before=True)

GW = 256
COLS_W, ROWS = 64, T // 64
NA_H, NA_D, NA_KR, NA_KC = 8, 32, 8, 16
BAND = NA_KR * COLS_W
REL_R, REL_C = 2 * NA_KR - 1, 2 * NA_KC - 1
RPB_PAD = COLS_W - NA_KC
RPB_W = REL_C + 2 * RPB_PAD
CONV = 31
POOL_WINDOWS = (2, 4, 8, 16)
PADC = CONV // 2
POOL_PAD = 16
QKV2 = dict(q=0, k=2, v=4)
REST2 = dict(pool=0, u=2, v_gate=4)
CONV_STEP, CONV_LAST = 4, 3
POOL_EDGE = 8


def second_gains(core, a, c_in, g, column, by_tile):
    column("norm_g_2", by_tile(a["norm_g_2"][0]), KT)
    column("final_g_2", by_tile(a["final_g_2"]), KT)
    for name in ("conv_dw_b_2", "conv_ln_g_2", "conv_ln_b_2", "pool_scale_2", "sgu_ln_g_2", "sgu_ln_b_2"):
        column(name, by_tile(a[name][0]), 2)


def row_start(r):
    return min(max(r - NA_KR // 2, 0), ROWS - NA_KR)


def neighbourhood_attention(core, c_in, rpb, z, mix):
    nc = core.nc
    with ExitStack() as ctx:
        sb = lambda n, shape: core.sbuf("na_" + n, shape, ctx)
        qbd = sb("q_blockdiag", [P, ROWS * P])
        raw = mix[:, 4 * T:4 * T + REL_R * COLS_W]
        bias = sb("bias", [P, 2 * REL_R * COLS_W])
        probs, pT = mix[:, 5 * T:5 * T + 3 * BAND], mix[:, 5 * T + 3 * BAND:5 * T + 5 * BAND]
        flip, edge = sb("flip", [P, P]), sb("edge", [P, COLS_W])
        col = sb("col", [P, 2 * 4])
        kS, vS = core.work[:, 0:T], core.work[:, T:2 * T]
        v_al, v_sh = mix[:, 2 * T:3 * T], mix[:, 3 * T:4 * T]
        n_bias = REL_R * COLS_W
        units = [(p, r) for p in range(2) for r in range(ROWS)]
        U = len(units)
        sems = ("const", "raw_loaded", "staged", "flipped", "bias_ready", "v_turned", "v_ready", "scores_ready",
                "max_ready", "exp_ready", "p_ready", "p_turned", "pT_ready", "pv_done", "out_taken", "dve_own")
        with core.phase("na", *sems) as (
                block, const, raw_loaded, staged, flipped, bias_ready, v_turned, v_ready, scores_ready,
                max_ready, exp_ready, p_ready, p_turned, pT_ready, pv_done, out_taken, dve_own):

            def raw_view(i, pair):
                head = REL_R * RPB_W
                return [bass.AP(tensor=rpb.tensor, offset=i * (4 * head) + (2 * pair + hh) * head,
                                ap=[[1, COLS_W], [RPB_W, REL_R], [1, COLS_W]]) for hh in range(2)]

            @block.sync
            def _(sp):
                sp.dma_start(flip[:, :], c_in["flip"]).then_inc(const, 16)
                sp.dma_start(edge[:, :], c_in["edge"]).then_inc(const, 16)
                with sp.Fori(0, 2) as i:
                    for pair in range(2):
                        sp.wait_ge(flipped, i * 2 + (pair + 1))
                        for hh, view in enumerate(raw_view(i, pair)):
                            sp.dma_start(raw[hh * COLS_W:(hh + 1) * COLS_W, :].rearrange("p (r c) -> p r c", c=COLS_W),
                                         view).then_inc(raw_loaded, 16)

            @block.tensor
            def _(pe):
                pe.wait_ge(const, 32)
                pe.sem_inc(flipped, 1)
                def score(i, n):
                    p, r = units[n]
                    s0 = row_start(r) * COLS_W
                    if n >= 2:
                        pe.wait_ge(max_ready, i * U + (n - 1))
                    nc.tensor.matmul(core.bank(n % 2), qbd[64 * p:64 * p + 64, r * P:(r + 1) * P],
                                     kS[64 * p:64 * p + 64, s0:s0 + BAND], start=True, stop=True).then_inc(scores_ready, 1)
                def weigh(i, n):
                    p, r = units[n]
                    s0 = row_start(r)
                    v, first = (v_al, s0 // 2) if s0 % 2 == 0 else (v_sh, (s0 - 1) // 2)
                    pe.wait_ge(pT_ready, i * U + (n + 1))
                    for c in range(BAND // P):
                        vt = v[:, (first + c) * P + 64 * p:(first + c) * P + 64 * p + 64]
                        last = nc.tensor.matmul(core.ps[64 * p:64 * p + 64, 4 * BANK + r * P:4 * BANK + (r + 1) * P],
                                                vt, pT[:, (n % 2) * BAND + c * P:(n % 2) * BAND + (c + 1) * P],
                                                start=(c == 0), stop=(c == BAND // P - 1))
                    last.then_inc(pv_done, 1)
                with pe.Fori(0, 2) as i:
                    for pair in range(2):
                        pe.wait_ge(raw_loaded, i * 64 + (pair + 1) * 32)
                        if pair == 1:
                            pe.wait_ge(bias_ready, i * 2 + 1)
                        for at in range(0, n_bias, 480):
                            last = nc.tensor.matmul(core.bank(at // 480, 480), flip[:, :], raw[:, at:at + 480],
                                                    start=True, stop=True)
                        last.then_inc(flipped, 1)
                    pe.wait_ge(staged, i + 1)
                    for t in range(TT):
                        last = nc.tensor.transpose(core.bank(4, P, t * P), vS[:, t * P:(t + 1) * P], core.ident[:, :])
                    for t in range(TT - 1):
                        last = nc.tensor.transpose(core.bank(6, P, t * P), vS[:, t * P + 64:(t + 1) * P + 64],
                                                   core.ident[:, :])
                    last.then_inc(v_turned, 1)
                    pe.wait_ge(bias_ready, i * 2 + 2)
                    score(i, 0)
                    score(i, 1)
                    pe.wait_ge(v_ready, i + 1)
                    for n in range(U):
                        if n + 2 < U:
                            score(i, n + 2)
                        pe.wait_ge(p_ready, i * U + (n + 1))
                        if n >= 2:
                            pe.wait_ge(pT_ready, i * U + (n - 1))
                        for c in range(BAND // P):
                            last = nc.tensor.transpose(core.bank(2 + n % 2, P, c * P),
                                                       probs[:, (n % 3) * BAND + c * P:(n % 3) * BAND + (c + 1) * P],
                                                       core.ident[:, :])
                        last.then_inc(p_turned, 1)
                        if n >= 1:
                            weigh(i, n - 1)
                    weigh(i, U - 1)
                    pe.wait_ge(out_taken, i + 1)

            @block.scalar
            def _(act):
                with act.Fori(0, 2) as i:
                    nc.scalar.preload_act_table_set(EXP_LN)
                    act.wait_ge(v_turned, i + 1)
                    nc.scalar.activation(v_al, core.bank(4, T), ACT.Identity)
                    nc.scalar.activation(v_sh[:, 0:T - P], core.bank(6, T - P), ACT.Identity).then_inc(v_ready, 1)
                    def turned(n):
                        act.wait_ge(p_turned, i * U + (n + 1))
                        if n >= 2:
                            act.wait_ge(pv_done, i * U + (n - 1))
                        nc.scalar.activation(pT[:, (n % 2) * BAND:(n % 2 + 1) * BAND], core.bank(2 + n % 2),
                                             ACT.Identity).then_inc(pT_ready, 1)
                    for n in range(U):
                        act.wait_ge(max_ready, i * U + (n + 1))
                        s, c = probs[:, (n % 3) * BAND:(n % 3 + 1) * BAND], (n % 2) * 4
                        nc.scalar.activation(s, s, ACT.Exp, bias=col[:, c:c + 1], accum_out=col[:, c + 1:c + 2]) \
                            .then_inc(exp_ready, 1)
                        if n >= 1:
                            turned(n - 1)
                    turned(U - 1)

            @block.vector
            def _(dve):
                dve.wait_ge(const, 32)
                zeroed = Chain(dve, dve_own)
                zeroed.mark(nc.vector.memset(qbd[:, :], 0.0))
                zeroed.restart()
                with dve.Fori(0, 2) as i:
                    own = Chain(dve, dve_own)
                    for g in range(4):
                        rows = slice(32 * g, 32 * g + 32)
                        own.mark(nc.vector.tensor_scalar(
                            qbd[rows, :].rearrange("p (r n) -> p r n", n=P)[:, :, (g % 2) * 64:(g % 2) * 64 + 64],
                            z[rows, ds(i * T, T)].rearrange("p (r n) -> p r n", n=COLS_W),
                            NA_D ** -0.5, None, ALU.mult))
                    own.mark(nc.vector.tensor_copy(kS, cols(z, i * T + QKV2["k"] * T)))
                    own.mark(nc.vector.tensor_copy(vS, cols(z, i * T + QKV2["v"] * T)))
                    own.join()
                    dve.sem_inc(staged, 1)
                    for pair in range(2):
                        dve.wait_ge(flipped, i * 2 + (pair + 2))
                        for at in range(0, n_bias, 480):
                            own.mark(nc.vector.tensor_copy(bias[:, pair * n_bias + at:pair * n_bias + at + 480],
                                                           core.bank(at // 480, 480)))
                        own.join()
                        dve.sem_inc(bias_ready, 1)
                        b = bias[:, pair * n_bias:(pair + 1) * n_bias].rearrange("p (r c) -> p r c", c=COLS_W)
                        own.link(nc.vector.tensor_tensor(b, b, edge[:, :].unsqueeze(1).to_broadcast([P, REL_R, COLS_W]),
                                                         ALU.add))

                    def soft(n):
                        p, r = units[n]
                        off = (row_start(r) - r + NA_KR - 1) * COLS_W + p * n_bias
                        s, c = probs[:, (n % 3) * BAND:(n % 3 + 1) * BAND], (n % 2) * 4
                        dve.wait_ge(scores_ready, i * U + (n + 1))
                        if n >= 3:
                            dve.wait_ge(p_turned, i * U + (n - 2))
                        own.link(nc.vector.tensor_tensor(s, core.bank(n % 2), bias[:, off:off + BAND], ALU.add))
                        nc.vector.tensor_reduce(out=col[:, c:c + 1], in_=s, axis=AX.X, op=ALU.max,
                                                negate=True).then_inc(max_ready, 1)

                    def divide(n):
                        s, c = probs[:, (n % 3) * BAND:(n % 3 + 1) * BAND], (n % 2) * 4
                        dve.wait_ge(exp_ready, i * U + (n + 1))
                        own.link(nc.vector.reciprocal(col[:, c + 2:c + 3], col[:, c + 1:c + 2]))
                        nc.vector.tensor_scalar(s, s, col[:, c + 2:c + 3], None, ALU.mult).then_inc(p_ready, 1)

                    soft(0)
                    for n in range(U):
                        if n + 1 < U:
                            soft(n + 1)
                        divide(n)
                    dve.wait_ge(pv_done, i * U + U)
                    for g in range(4):
                        rows = slice(32 * g, 32 * g + 32)
                        own.mark(nc.vector.tensor_copy(
                            mix[rows, ds(i * T, T)].rearrange("p (r n) -> p r n", n=COLS_W),
                            core.ps[rows, 4 * BANK:8 * BANK].rearrange("p (r n) -> p r n", n=P)[
                                :, :, (g % 2) * 64:(g % 2) * 64 + 64]))
                    own.join()
                    dve.sem_inc(out_taken, 1)
                    own.restart()


def layer_norms(core, name, jobs):
    nc = core.nc
    sems = ("summed", "centred", "squared", "var_ready", "rstd_ready", "scaled", "dve_own", "act_own")
    with core.phase(name, *sems) as (block, summed, centred, squared, var_ready, rstd_ready, scaled, dve_own, act_own):
        @block.tensor
        def _(pe):
            def total(rows, bank):
                for c in range(0, T, BANK):
                    for k in range(2):
                        last = nc.tensor.matmul(core.bank(bank, BANK, c), core.ones[:, :],
                                                rows[:, k * T + c:k * T + c + BANK], start=(k == 0), stop=(k == 1))
                return last
            for n, job in enumerate(jobs):
                total(job[0], 4 * n).then_inc(summed, 1)
            for n, job in enumerate(jobs):
                pe.wait_ge(squared, 2 * n + 2)
                total(job[4], 4 * n + 2).then_inc(var_ready, 1)

        @block.vector
        def _(dve):
            own = Chain(dve, dve_own)
            for n, (src, *_) in enumerate(jobs):
                dve.wait_ge(summed, n + 1)
                for k in range(2):
                    own.link(nc.vector.scalar_tensor_tensor(out=src[:, k * T:(k + 1) * T], in0=core.bank(4 * n, T),
                                                            scalar=-1.0 / GW, in1=src[:, k * T:(k + 1) * T],
                                                            op0=ALU.mult, op1=ALU.add))
                    dve.sem_inc(centred, 1)
            for n, (src, gain, bias, func, sq, rstd) in enumerate(jobs):
                dve.wait_ge(rstd_ready, n + 1)
                for k in range(2):
                    nc.vector.scalar_tensor_tensor(out=sq[:, k * T:(k + 1) * T], in0=src[:, k * T:(k + 1) * T],
                                                   scalar=gain[:, k:k + 1], in1=rstd, op0=ALU.mult,
                                                   op1=ALU.mult).then_inc(scaled, 1)

        @block.scalar
        def _(act):
            own = Chain(act, act_own)
            nc.scalar.preload_act_table_set(EXP_LN)
            for n, (src, gain, bias, func, sq, rstd) in enumerate(jobs):
                for k in range(2):
                    act.wait_ge(centred, 2 * n + k + 1)
                    nc.scalar.activation(sq[:, k * T:(k + 1) * T], src[:, k * T:(k + 1) * T], ACT.Square) \
                        .then_inc(squared, 1)
            for n, (src, gain, bias, func, sq, rstd) in enumerate(jobs):
                act.wait_ge(var_ready, n + 1)
                own.link(nc.scalar.activation(rstd, core.bank(4 * n + 2, T), ACT.Ln, bias=core.eps5[:, :], scale=1.0 / GW))
                nc.scalar.activation(rstd, rstd, ACT.Exp, scale=-0.5).then_inc(rstd_ready, 1)
            for n, (src, gain, bias, func, sq, rstd) in enumerate(jobs):
                for k in range(2):
                    act.wait_ge(scaled, 2 * n + k + 1)
                    nc.scalar.activation(src[:, k * T:(k + 1) * T], sq[:, k * T:(k + 1) * T], func, bias=bias[:, k:k + 1])


def prepare_mixers(core, a, c_in, pad, taps, inv):
    nc = core.nc
    wide = T + 2 * PADC
    with core.phase("prep", "loaded") as (block, loaded):
        @block.sync
        def _(sp):
            sp.dma_start(inv[:, :], c_in["inv_count"]).then_inc(loaded, 16)
            with nc.allow_non_contiguous_dma("taps, a channel a partition"):
                for k in range(2):
                    sp.dma_start(taps[:, k * CONV:(k + 1) * CONV],
                                 a["conv_dw_w_2"][0][:, k * P:(k + 1) * P].rearrange("j p -> p j")).then_inc(loaded, 16)
            sp.wait_ge(loaded, 48)

        @block.vector
        def _(dve):
            for k in range(2):
                nc.vector.memset(pad[:, k * wide:k * wide + PADC], 0.0)
                nc.vector.memset(pad[:, (k + 1) * wide - PADC:(k + 1) * wide], 0.0)


def project_mixers(core, w, g, z, pad, taps, acc, inv, mix):
    nc = core.nc
    wide = T + 2 * PADC
    half = [core.work[:, s * T:(s + 1) * T] for s in range(2)]

    def scaled(dst):
        return lambda dve, own, i, s, product: nc.vector.tensor_tensor(dst(i, s), product, core.rstd[:, :], ALU.mult)

    def in_place(func, dst):
        return lambda act, i, s: nc.scalar.activation(dst(i, s), dst(i, s), func)

    def columns(first):
        return lambda i, s: plain_views(w, KT, i * (2 * P) + (s * P + first))

    def gate_input(dve, own, i, s):
        if s == 1:
            own.link(nc.vector.tensor_tensor(cols(pad, i * wide + PADC), half[0], half[1], ALU.mult))

    def tap(own, j, first=False):
        for k in range(2):
            o, x, c = acc[:, k * T:(k + 1) * T], cols(pad, j + k * wide), cols(taps, j + k * CONV, 1)
            if first:
                own.mark(nc.vector.tensor_scalar(o, x, c, g["conv_dw_b_2"][:, k:k + 1], ALU.mult, ALU.add))
            else:
                own.mark(nc.vector.scalar_tensor_tensor(out=o, in0=x, scalar=c, in1=o, op0=ALU.mult, op1=ALU.add))
        own.join()

    def taps_beside(first, start=False):
        def finish(dve, own, i, s):
            if start and isinstance(i, int) and i == 0 and s == 0:
                tap(own, 0, True)
            for j in range(CONV_STEP):
                tap(own, i * (2 * CONV_STEP) + (s * CONV_STEP + first + j))
        return finish

    def gate_attention(dve, own, i, s):
        own.link(nc.vector.tensor_tensor(cols(mix, i * (2 * T) + s * T), cols(mix, i * (2 * T) + s * T), half[s], ALU.mult))
        for j in range(CONV_LAST):
            tap(own, CONV - 2 * CONV_LAST + s * CONV_LAST + j)

    span = T + 2 * POOL_PAD
    sums = [core.work[:, n * span:(n + 1) * span] for n in range(2)]
    mean = core.work[:, 2 * span:2 * span + T]

    def pool_start(own, k):
        for buf in sums:
            own.mark(nc.vector.memset(buf, 0.0))
        own.join()
        own.link(nc.vector.tensor_copy(sums[0][:, POOL_PAD:POOL_PAD + T], z[:, (REST2["pool"] + k) * T:(REST2["pool"] + k + 1) * T]))

    def pool_level(own, k, level):
        window = POOL_WINDOWS[level]
        s, d = sums[level % 2], sums[1 - level % 2]
        lo, up = (-1, 0) if window == 2 else (-window // 4, window // 4)
        reach = sum(1 if v == 2 else v // 4 for v in POOL_WINDOWS[:level + 1])
        n = span - 2 * reach
        own.link(nc.vector.tensor_tensor(d[:, reach:reach + n], s[:, reach + lo:reach + lo + n],
                                         s[:, reach + up:reach + up + n], ALU.add))
        if level < 2 * k:
            return
        r = slice(64 * (level % 2), 64 * (level % 2) + 64)
        m, total, c = mean[r, :], d[r, POOL_PAD:POOL_PAD + T], k * (2 * POOL_EDGE + 1)
        for at, first in ((0, c), (T - POOL_EDGE, c + POOL_EDGE)):
            own.mark(nc.vector.tensor_tensor(m[:, at:at + POOL_EDGE], total[:, at:at + POOL_EDGE],
                                             inv[r, first:first + POOL_EDGE], ALU.mult))
        own.mark(nc.vector.tensor_scalar(m[:, POOL_EDGE:T - POOL_EDGE], total[:, POOL_EDGE:T - POOL_EDGE],
                                         inv[r, c + 2 * POOL_EDGE:c + 2 * POOL_EDGE + 1], None, ALU.mult))
        own.join()
        x = z[r, (REST2["pool"] + k) * T:(REST2["pool"] + k + 1) * T]
        own.link(nc.vector.tensor_tensor(x, m, x, ALU.subtract))

    def pool_beside(dve, own, i, s):
        k, part = divmod(2 * i + s, 3)
        if part == 0:
            pool_start(own, k)
            pool_level(own, k, 0)
        elif part == 1:
            pool_level(own, k, 1)
        elif k == 1:
            pool_level(own, k, 2)
            pool_level(own, k, 3)

    zt = lambda first: lambda i, s: cols(z, i * (2 * T) + (s * T + first * T))
    later = lambda i, s: cols(mix, i * (2 * T) + (s * T + 2 * T))
    linears(core, "mp", [
        Stage(w, 4, scaled(lambda i, s: half[s]), core.h, load=lambda i, s: plain_views(w, KT, i * P + (3 + s) * GW),
              mid=lambda act, i, s: nc.scalar.activation(half[1], half[1], ACT.Sigmoid), mids=(1,), finish=gate_input),
        Stage(w, 2, scaled(zt(0)), core.h, load=columns(5 * GW), finish=taps_beside(1, True)),
        Stage(w, 4, scaled(zt(2)), core.h, load=columns(6 * GW), mid=in_place(ACT.Gelu_apprx_tanh, zt(2)),
              finish=taps_beside(1 + 2 * CONV_STEP)),
        Stage(w, 2, scaled(lambda i, s: half[s]), core.h, load=columns(8 * GW),
              mid=in_place(ACT.Silu, lambda i, s: half[s]), finish=gate_attention),
        Stage(w, 6, scaled(later), core.h, load=columns(9 * GW), mid=in_place(ACT.Silu, later), finish=pool_beside,
              unroll=True)])


def pointwise(core, a, acc, mix):
    nc = core.nc
    with ExitStack() as ctx:
        pair = tuple(core.sbuf(f"cv_{p}", [P, 2 * T], ctx, F32R) for p in ("hi", "lo"))

        def gate(dve, own, i, s, product):
            tile = mix[:, (2 + s) * T:(3 + s) * T]
            return nc.vector.tensor_tensor(tile, tile, product, ALU.mult)

        linear(core, "pw", a["conv_pw_2"][0], 2, gate, pair, kts=2, operand=Operand(core, acc, None, pair, tiles=2))


def multiscale_pool(core, a, g, z, mix):
    nc = core.nc
    with ExitStack() as ctx:
        wts = core.sbuf("po_weights", [P, 2 * P], ctx)
        with core.phase("po", "zeroed", "weights", "mixed") as (block, zeroed, weights, mixed):
            @block.sync
            def _(sp):
                sp.wait_ge(zeroed, 1)
                for j in range(4):
                    r = 64 * (j % 2)
                    sp.dma_start(wts[r:r + 64, (j // 2) * P + r:(j // 2) * P + r + 64], a["pool_w_2"][0][j]) \
                        .then_inc(weights, 16)

            @block.vector
            def _(dve):
                nc.vector.memset(wts[:, :], 0.0).then_inc(zeroed, 1)
                dve.wait_ge(mixed, 1)
                for k in range(2):
                    tile = mix[:, (4 + k) * T:(5 + k) * T]
                    nc.vector.scalar_tensor_tensor(out=tile, in0=core.bank(2 * k, T), scalar=g["pool_scale_2"][:, k:k + 1],
                                                   in1=tile, op0=ALU.mult, op1=ALU.mult)

            @block.tensor
            def _(pe):
                pe.wait_ge(weights, 64)
                for k in range(2):
                    for c in range(0, T, BANK):
                        last = nc.tensor.matmul(core.bank(2 * k, BANK, c), wts[:, k * P:(k + 1) * P],
                                                z[:, (REST2["pool"] + k) * T + c:(REST2["pool"] + k) * T + c + BANK],
                                                start=True, stop=True)
                last.then_inc(mixed, 1)


def spatial_gating(core, a, g, z, mix):
    nc = core.nc
    u = z[:, REST2["u"] * T:(REST2["u"] + 2) * T]
    v = z[:, REST2["v_gate"] * T:(REST2["v_gate"] + 2) * T]
    with ExitStack() as ctx:
        sb = lambda n, shape: core.sbuf("sg_" + n, shape, ctx)
        ws, wsT = sb("ws", [P, 4 * P]), sb("wsT", [P, 4 * P])
        bs = sb("bs", [P, 2 * P])
        v_tok = sb("v_tok", [P, 2 * T])
        tmp = core.work[:, 0:2 * T]
        sems = ("loaded", "w_turned", "w_ready", "v_turned", "v_ready", "mixed", "dve_own")
        with core.phase("sg", *sems) as (block, loaded, w_turned, w_ready, v_turned, v_ready, mixed, dve_own):
            @block.sync
            def _(sp):
                sp.dma_start(ws[:, :].rearrange("p (h q) -> p h q", h=4),
                             a["sgu_w_2"][0].rearrange("h p q -> p h q")).then_inc(loaded, 16)
                for hh in range(4):
                    r = 64 * (hh % 2)
                    sp.dma_start(bs[r:r + 64, (hh // 2) * P:(hh // 2 + 1) * P],
                                 a["sgu_b_2"][0][hh:hh + 1, :].to_broadcast([64, P])).then_inc(loaded, 16)

            @block.tensor
            def _(pe):
                pe.wait_ge(loaded, 80)
                for hh in range(4):
                    last = nc.tensor.transpose(core.bank(0, P, hh * P), ws[:, hh * P:(hh + 1) * P], core.ident[:, :])
                last.then_inc(w_turned, 1)
                for k in range(2):
                    for n in range(TT):
                        last = nc.tensor.transpose(core.bank(2 + 2 * k, P, n * P), v[:, k * T + n * P:k * T + (n + 1) * P],
                                                   core.ident[:, :])
                    last.then_inc(v_turned, 1)
                pe.wait_ge(w_ready, 1)
                pe.wait_ge(v_ready, 2)
                for k in range(2):
                    for n in range(TT):
                        for hh in range(2):
                            last = nc.tensor.matmul(
                                core.ps[64 * hh:64 * hh + 64, (2 + 2 * k) * BANK + n * P:(2 + 2 * k) * BANK + (n + 1) * P],
                                v_tok[:, k * T + n * P + 64 * hh:k * T + n * P + 64 * hh + 64],
                                wsT[:, (2 * k + hh) * P:(2 * k + hh + 1) * P], start=True, stop=True)
                    last.then_inc(mixed, 1)

            @block.vector
            def _(dve):
                own = Chain(dve, dve_own)
                dve.wait_ge(w_turned, 1)
                nc.vector.tensor_copy(wsT[:, :], core.bank(0)).then_inc(w_ready, 1)
                for k in range(2):
                    dve.wait_ge(v_turned, k + 1)
                    nc.vector.tensor_copy(v_tok[:, k * T:(k + 1) * T], core.bank(2 + 2 * k, T)).then_inc(v_ready, 1)
                for k in range(2):
                    dve.wait_ge(mixed, k + 1)
                    t = tmp[:, k * T:(k + 1) * T]
                    own.link(nc.vector.tensor_tensor(t.rearrange("p (n q) -> p n q", q=P),
                                                     core.bank(2 + 2 * k, T).rearrange("p (n q) -> p n q", q=P),
                                                     bs[:, k * P:(k + 1) * P].unsqueeze(1).to_broadcast([P, TT, P]), ALU.add))
                    own.link(nc.vector.tensor_tensor(t, t, u[:, k * T:(k + 1) * T], ALU.mult))
                    tile = mix[:, (6 + k) * T:(7 + k) * T]
                    nc.vector.tensor_tensor(tile, tile, t, ALU.mult)


def second_block(core, a, c_in, g):
    nc = core.nc
    w = a["w_in_2"][0]
    with ExitStack() as block_ctx:
        mix = core.sbuf("mix2", [P, KT * T], block_ctx)
        with ExitStack() as ctx:
            z = core.sbuf("z_qkv", [P, 6 * T], ctx)
            linear(core, "qkv2", w, 6, scale_to(core, z), operand=Operand(core, core.x, g["norm_g_2"], core.h, core.eps6))
            neighbourhood_attention(core, c_in, a["na_rpb_2"], z, mix)
        with ExitStack() as ctx:
            acc = core.sbuf("cv_acc", [P, 2 * T], ctx)
            z_ctx = ctx.enter_context(ExitStack())
            z = core.sbuf("z_rest", [P, 6 * T], z_ctx)
            with ExitStack() as conv_ctx:
                pad = core.sbuf("cv_padded", [P, 2 * (T + 2 * PADC)], conv_ctx)
                taps = core.sbuf("cv_taps", [P, 2 * CONV], conv_ctx)
                inv = core.sbuf("po_inv_count", [P, 2 * (2 * POOL_EDGE + 1)], conv_ctx)
                prepare_mixers(core, a, c_in, pad, taps, inv)
                project_mixers(core, w, g, z, pad, taps, acc, inv, mix)
            row = core.sbuf("sg_rstd", [P, T], z_ctx)
            v = z[:, REST2["v_gate"] * T:(REST2["v_gate"] + 2) * T]
            layer_norms(core, "ln", [
                (v, g["sgu_ln_g_2"], g["sgu_ln_b_2"], ACT.Identity, core.work[:, 0:2 * T], core.rstd[:, :]),
                (acc, g["conv_ln_g_2"], g["conv_ln_b_2"], ACT.Silu, core.work[:, 2 * T:4 * T], row[:, :])])
            multiscale_pool(core, a, g, z, mix)
            spatial_gating(core, a, g, z, mix)
            z_ctx.close()
            pointwise(core, a, acc, mix)
        linear(core, "out2", a["w_out_2"][0], KT, add_to(nc, core.x), operand=Operand(core, mix, None, core.h),
               **sum_squares(core, core.x))
    rms_norm(core, "nf2", core.x, g["final_g_2"], core.x, core.eps6, squared_before=True)

AH, AKV, AD = 8, 2, 64
WIN = 128
MEM = 256
CA_D = 256
FF3 = 2816
FT3 = FF3 // P
FF3_GROUP = 4
W3 = dict(q=0, k=512, v=640, hq=768, hf=1280, hi=1792, hg=2304)
LEVELS = (64, 32, 16, 8, 4, 2, 1)
LN_LEAST = 6e-20


def third_gains(core, a, c_in, g, column, by_tile):
    for name in ("mix_pre_norm_3", "mix_post_norm_3", "ca_pre_norm_3", "mem_norm_3", "ca_post_norm_3",
                 "ffn_pre_norm_3", "ffn_post_norm_3"):
        column(name, by_tile(a[name][0]), KT)
    column("hgrn_out_norm_3", by_tile(a["hgrn_out_norm_3"][0]), 1)
    for n in range(2):
        column(f"lb_logits{n}", by_tile(a["hgrn_lb_logits_3"][n]), HEADS)
    column("sinks", a["attn_sinks_3"].to_broadcast([P, AH]), AH)
    g["lb"] = core.sbuf("g_lb", [P, 4 * HEADS])


def lower_bound(core, g):
    nc, lb = core.nc, g["lb"]
    l0, l1 = g["lb_logits0"], g["lb_logits1"]
    H = HEADS
    with core.phase("lb", "shifted", "exped", "dve_own") as (block, shifted, exped, dve_own):
        @block.vector
        def _(dve):
            own = Chain(dve, dve_own)
            own.link(nc.vector.tensor_tensor(lb[:, 0:H], l0[:, :], l1[:, :], ALU.max))
            nc.vector.tensor_tensor(lb[:, 2 * H:3 * H], l0[:, :], lb[:, 0:H], ALU.subtract).then_inc(shifted, 1)
            nc.vector.tensor_tensor(lb[:, 3 * H:4 * H], l1[:, :], lb[:, 0:H], ALU.subtract).then_inc(shifted, 1)
            dve.wait_ge(exped, 1)
            own.link(nc.vector.tensor_tensor(lb[:, H:2 * H], lb[:, 2 * H:3 * H], lb[:, 3 * H:4 * H], ALU.add))
            own.link(nc.vector.reciprocal(lb[:, H:2 * H], lb[:, H:2 * H]))
            own.link(nc.vector.tensor_tensor(lb[:, 0:H], lb[:, 2 * H:3 * H], lb[:, H:2 * H], ALU.mult))
            nc.vector.tensor_scalar(lb[:, H:2 * H], lb[:, 0:H], -1.0, 1.0, ALU.mult, ALU.add)

        @block.scalar
        def _(act):
            act.wait_ge(shifted, 2)
            nc.scalar.activation(lb[:, 2 * H:4 * H], lb[:, 2 * H:4 * H], ACT.Exp).then_inc(exped, 1)


def window_attention(core, w, c_in, sinks, mix):
    nc, h = core.nc, core.h
    with ExitStack() as ctx:
        sb = lambda n, shape: core.sbuf("wa_" + n, shape, ctx)
        wt = Weights(core, "wa", ctx)
        wt.geometry(KT, 0, (0, 0), (2, 2))
        kP, vT, qT = sb("k_padded", [P, WIN + T]), sb("vT", [P, T]), sb("qT", [P, T])
        v_tok = sb("v_tok", [P, WIN + T])
        mask = sb("mask", [P, 4 * WIN])
        probs, pT = sb("probs", [P, 3 * 4 * WIN]), sb("probsT", [P, 2 * 4 * WIN])
        col = sb("col", [P, 2 * 16])
        head = sb("head", [P, 4])
        sems = Weights.SIGNALS + ("const", "kv_taken", "v_turned", "kv_ready", "q_ready", "scores_ready",
                "max_ready", "exp_ready", "p_ready", "p_turned", "pT_ready", "pv_done", "o_taken", "dve_own", "scores_taken")
        with core.phase("wa", *sems) as (
                block, *ws, const, kv_taken, v_turned, kv_ready, q_ready, scores_ready,
                max_ready, exp_ready, p_ready, p_turned, pT_ready, pv_done, o_taken, dve_own, scores_taken):

            wt.signals(ws)

            def halves(first, second):
                views = [w[0:D, ds(c, AD)].rearrange("(k p) n -> p k n", p=P) for c in (first, second)]
                return [[(lambda d: d[:, :, 0:AD], views[0][:, 4 * r:4 * r + 4, :]),
                         (lambda d: d[:, :, AD:P], views[1][:, 4 * r:4 * r + 4, :])] for r in range(2)]

            @block.sync
            def _(sp):
                sp.dma_start(mask[:, :], c_in["window"]).then_inc(const, 16)
                wt.load(sp, 0, 0, halves(W3["k"], W3["k"] + AD))
                wt.load(sp, 1, 0, halves(W3["v"], W3["v"] + AD))
                with sp.Fori(0, 4) as i:
                    wt.load(sp, i + 2, 0, halves(i * AD + W3["q"], i * AD + (W3["q"] + AH // 2 * AD)))

            @block.gpsimd
            def _(pool):
                wt.open_raw(pool)
                wt.split(pool, 0, 0)
                wt.split(pool, 1, 0)
                with pool.Fori(0, 4) as i:
                    wt.split(pool, i + 2, 0)

            @block.tensor
            def _(pe):
                wt.open_slots(pe)
                for t in range(2):
                    wt.product(pe, core.bank(2 * t, T), h, t, 0)
                pe.wait_ge(kv_taken, 2)
                for t in range(TT):
                    last = nc.tensor.transpose(core.bank(4, P, t * P), vT[:, t * P:(t + 1) * P], core.ident[:, :])
                last.then_inc(v_turned, 1)

                def score(i, b):
                    if b >= 2:
                        pe.wait_ge(scores_taken, i * TT + (b - 1))
                    for g in range(2):
                        last = nc.tensor.matmul(core.bank(4 * (1 - b % 2) + g, 2 * WIN), qT[64 * g:64 * g + 64, b * WIN:(b + 1) * WIN],
                                                kP[64 * g:64 * g + 64, b * WIN:(b + 2) * WIN], start=True, stop=True)
                    last.then_inc(scores_ready, 1)

                def weigh(i, b):
                    pe.wait_ge(pT_ready, i * TT + (b + 1))
                    for g in range(2):
                        for j in range(2):
                            last = nc.tensor.matmul(
                                core.ps[64 * g:64 * g + 64, 2 * BANK + b * WIN:2 * BANK + (b + 1) * WIN],
                                v_tok[:, (b + j) * P + 64 * g:(b + j) * P + 64 * g + 64],
                                pT[:, (b % 2) * BANK + (2 * g + j) * P:(b % 2) * BANK + (2 * g + j + 1) * P],
                                start=(j == 0), stop=(j == 1))
                    last.then_inc(pv_done, 1)

                with pe.Fori(0, 4) as i:
                    pe.wait_ge(kv_ready, 3)
                    wt.product(pe, core.bank(0, T), h, i + 2, 0)
                    pe.wait_ge(q_ready, i + 1)
                    score(i, 0)
                    score(i, 1)
                    for b in range(TT):
                        if b + 2 < TT:
                            score(i, b + 2)
                        pe.wait_ge(p_ready, i * TT + (b + 1))
                        if b >= 2:
                            pe.wait_ge(pT_ready, i * TT + (b - 1))
                        for j in range(4):
                            last = nc.tensor.transpose(core.bank(6 + b % 2, P, j * P),
                                                       probs[:, (b % 3) * BANK + j * P:(b % 3) * BANK + (j + 1) * P],
                                                       core.ident[:, :])
                        last.then_inc(p_turned, 1)
                        if b >= 1:
                            weigh(i, b - 1)
                    weigh(i, TT - 1)
                    pe.wait_ge(o_taken, i + 1)

            @block.scalar
            def _(act):
                nc.scalar.preload_act_table_set(EXP_LN)
                act.wait_ge(v_turned, 1)
                nc.scalar.activation(v_tok[:, WIN:WIN + T], core.bank(4, T), ACT.Identity).then_inc(kv_ready, 1)
                with act.Fori(0, 4) as i:
                    def turned(b):
                        act.wait_ge(p_turned, i * TT + (b + 1))
                        if b >= 2:
                            act.wait_ge(pv_done, i * TT + (b - 1))
                        nc.scalar.activation(pT[:, (b % 2) * BANK:(b % 2 + 1) * BANK], core.bank(6 + b % 2),
                                             ACT.Identity).then_inc(pT_ready, 1)
                    for b in range(TT):
                        act.wait_ge(max_ready, i * TT + (b + 1))
                        c = (b % 2) * 16
                        for g in range(2):
                            s = probs[:, (b % 3) * BANK + 2 * g * WIN:(b % 3) * BANK + 2 * (g + 1) * WIN]
                            nc.scalar.activation(s, s, ACT.Exp, bias=col[:, c + g:c + g + 1],
                                                 accum_out=col[:, c + 2 + g:c + 3 + g]).then_inc(exp_ready, 1)
                            nc.scalar.activation(col[:, c + 6 + g:c + 7 + g], head[:, 2 + g:3 + g], ACT.Exp,
                                                 bias=col[:, c + g:c + g + 1]).then_inc(exp_ready, 1)
                        if b >= 1:
                            turned(b - 1)
                    turned(TT - 1)
                    act.wait_ge(pv_done, i * TT + TT)
                    nc.scalar.activation(cols(mix, i * T), core.bank(2, T), ACT.Identity).then_inc(o_taken, 1)

            @block.vector
            def _(dve):
                nc.vector.memset(kP[:, 0:WIN], 0.0).then_inc(kv_ready, 1)
                nc.vector.memset(v_tok[:, 0:WIN], 0.0).then_inc(kv_ready, 1)
                dve.wait_ge(const, 16)
                for t, dst in enumerate((kP[:, WIN:WIN + T], vT[:, :])):
                    wt.wait_product(dve, t)
                    nc.vector.tensor_tensor(dst, core.bank(2 * t, T), core.rstd[:, :], ALU.mult).then_inc(kv_taken, 1)
                with dve.Fori(0, 4) as i:
                    own = Chain(dve, dve_own)
                    wt.wait_product(dve, i + 2)
                    nc.vector.scalar_tensor_tensor(out=qT[:, :], in0=core.bank(0, T), scalar=AD ** -0.5,
                                                   in1=core.rstd[:, :], op0=ALU.mult, op1=ALU.mult).then_inc(q_ready, 1)
                    sink = sinks[:, :].rearrange("p (g n) -> p n g", g=2)[:, ds(i, 1), :].rearrange("p n g -> p (n g)")
                    neg_sink, head_sink = head[:, 0:2], head[:, 2:4]
                    own.mark(nc.vector.tensor_scalar(neg_sink, sink, -1.0, None, ALU.mult))
                    own.mark(nc.vector.tensor_copy(head_sink, sink))
                    own.join()

                    def soft(b):
                        dve.wait_ge(scores_ready, i * TT + (b + 1))
                        if b >= 3:
                            dve.wait_ge(p_turned, i * TT + (b - 2))
                        c = (b % 2) * 16
                        s = probs[:, (b % 3) * BANK:(b % 3 + 1) * BANK].rearrange("p (g k) -> p g k", g=2)
                        m = mask[:, (0 if b == 0 else 2 * WIN):(0 if b == 0 else 2 * WIN) + 2 * WIN]
                        own.link(nc.vector.tensor_tensor(
                            s, core.bank(4 * (1 - b % 2), 2 * BANK).rearrange("p (g k) -> p g k", g=2)[:, :, 0:2 * WIN],
                            m.unsqueeze(1).to_broadcast([P, 2, 2 * WIN]), ALU.add))
                        dve.sem_inc(scores_taken, 1)
                        own.link(nc.vector.tensor_reduce(out=col[:, c + 8:c + 10], in_=s, axis=AX.X, op=ALU.max,
                                                         negate=True))
                        nc.vector.tensor_tensor(col[:, c:c + 2], col[:, c + 8:c + 10], neg_sink, ALU.min) \
                            .then_inc(max_ready, 1)

                    def divide(b):
                        c = (b % 2) * 16
                        dve.wait_ge(exp_ready, i * (4 * TT) + (4 * b + 4))
                        own.link(nc.vector.tensor_tensor(col[:, c + 12:c + 14], col[:, c + 2:c + 4], col[:, c + 6:c + 8], ALU.add))
                        own.link(nc.vector.reciprocal(col[:, c + 14:c + 16], col[:, c + 12:c + 14]))
                        s = probs[:, (b % 3) * BANK:(b % 3 + 1) * BANK].rearrange("p (g k) -> p g k", g=2)
                        nc.vector.tensor_tensor(s, s, col[:, c + 14:c + 16].unsqueeze(2).to_broadcast([P, 2, 2 * WIN]),
                                                ALU.mult).then_inc(p_ready, 1)

                    soft(0)
                    for b in range(TT):
                        if b + 1 < TT:
                            soft(b + 1)
                        divide(b)
                    own.restart()


def hgrn(core, w, c_in, g, mix):
    nc, h = core.nc, core.h
    lb = g["lb"]
    with ExitStack() as ctx:
        sb = lambda n, shape: core.sbuf("hg_" + n, shape, ctx)
        wt = Weights(core, "hg", ctx)
        qT, kT, bT, iT, state = (sb(n, [P, T]) for n in ("qT", "kT", "bT", "iT", "state"))
        X = [sb(f"level{n}", [P, T]) for n in range(2)]
        dec = [sb(f"decay{n}", [P, T]) for n in range(2)]
        mask = sb("mask", [P, 8 * P])
        cdec = sb("chunk_decay", [P, TT])
        A, sig, k_tok, v_tok = (core.work[:, n * T:(n + 1) * T] for n in range(4))
        sig_g, qd, kd = state, X[0], X[1]
        oT, sq, hrstd = A, sig, dec[1]
        n_lev = len(LEVELS)
        sems = Weights.SIGNALS + ("const", "raw_ready", "sig_ready", "proj_taken", "ln_in", "ln_ready", "b_ready",
                "diff_ready", "e_ready", "level_in", "level_ready", "level_taken", "kd_ready", "turned", "kv_tok_ready",
                "update_ready", "state_ready", "o_done", "sq_ready", "stat_ready", "rstd_ready", "mix_done",
                "dve_own", "act_own", "level_seen")
        with core.phase("hg", *sems) as (
                block, *ws, const, raw_ready, sig_ready, proj_taken, ln_in, ln_ready, b_ready,
                diff_ready, e_ready, level_in, level_ready, level_taken, kd_ready, turned, kv_tok_ready,
                update_ready, state_ready, o_done, sq_ready, stat_ready, rstd_ready, mix_done,
                dve_own, act_own, level_seen):
            wt.signals(ws)
            gate = lambda i: cols(mix, i * T + HEADS * T)
            first = (W3["hf"], W3["hq"], W3["hi"], W3["hg"])
            v3 = lambda b: b.rearrange("p (c n) -> p c n", n=P)
            blocks = lambda x, size: x[:, :].rearrange("p (m s) -> p m s", s=2 * size)
            halves = lambda x, size, upper: blocks(x, size)[:, :, upper * size:(upper + 1) * size]

            @block.sync
            def _(sp):
                sp.dma_start(mask[:, :], c_in["levels"]).then_inc(const, 16)
                with sp.Fori(0, HEADS) as i:
                    for j in range(4):
                        wt.load(sp, i * 4 + j, 0, plain_views(w, KT, i * HD + first[j]))

            @block.gpsimd
            def _(pool):
                wt.open_raw(pool)
                with pool.Fori(0, HEADS) as i:
                    for j in range(3):
                        wt.split(pool, i * 4 + j, 0)
                    pool.wait_ge(b_ready, i + 1)
                    for n in range(n_lev):
                        if n >= 2:
                            pool.wait_ge(level_in, i * n_lev + (n - 1))
                        size = LEVELS[n]
                        nc.gpsimd.tensor_tensor(
                            blocks(dec[n % 2], size), blocks(bT, size),
                            blocks(bT, size)[:, :, size - 1:size].to_broadcast([P, T // (2 * size), 2 * size]),
                            ALU.subtract).then_inc(diff_ready, 1)
                        if n < 4:
                            wt.split(pool, i * 4 + 3, 0, chunks=(n,))
                    pool.wait_ge(level_in, i * n_lev + (n_lev - 1))
                    nc.gpsimd.tensor_tensor(
                        v3(dec[n_lev % 2][:, :]), v3(bT[:, :]), v3(bT[:, :])[:, :, P - 1:P].to_broadcast([P, TT, P]),
                        ALU.subtract).then_inc(diff_ready, 1)

            @block.tensor
            def _(pe):
                wt.open_slots(pe)
                with pe.Fori(0, HEADS) as i:
                    for j in range(2):
                        wt.product(pe, core.bank(2 * j, T), h, i * 4 + j, 0)
                    pe.wait_ge(proj_taken, i * 4 + 2)
                    pe.wait_ge(raw_ready, i + 1)
                    for n in range(n_lev + 1):
                        if n == 0:
                            a, b = kT, qT
                        else:
                            pe.wait_ge(level_in, i * n_lev + n)
                            a = b = X[(n - 1) % 2]
                        if n >= 2:
                            pe.wait_ge(level_taken, i * (n_lev + 1) + (n - 1))
                        for c in range(TT):
                            last = nc.tensor.matmul(core.bank(2 * (n % 2), P, c * P), a[:, c * P:(c + 1) * P],
                                                    b[:, c * P:(c + 1) * P], start=True, stop=True)
                        last.then_inc(level_ready, 1)
                        wt.product(pe, core.bank(4 + 2 * (n // 4), T), h, i * 4 + (2 + n // 4), 0, chunks=(n % 4,))
                    pe.wait_ge(proj_taken, i * 4 + 3)
                    for c in range(TT):
                        last = nc.tensor.transpose(core.bank(4, P, c * P), iT[:, c * P:(c + 1) * P], core.ident[:, :])
                    last.then_inc(turned, 1)
                    pe.wait_ge(kd_ready, i + 1)
                    pe.wait_ge(proj_taken, i * 4 + 4)
                    for c in range(TT):
                        last = nc.tensor.transpose(core.bank(6, P, c * P), kd[:, c * P:(c + 1) * P], core.ident[:, :])
                    last.then_inc(turned, 1)
                    pe.wait_ge(kv_tok_ready, i * 2 + 2)
                    pe.wait_ge(level_taken, (i + 1) * (n_lev + 1))
                    for c in range(TT - 1):
                        last = nc.tensor.matmul(core.bank(0, P, c * P), k_tok[:, c * P:(c + 1) * P],
                                                v_tok[:, c * P:(c + 1) * P], start=True, stop=True)
                    last.then_inc(update_ready, 1)
                    pe.wait_ge(state_ready, i + 1)
                    for c in range(TT):
                        last = nc.tensor.matmul(core.bank(2, P, c * P), v_tok[:, c * P:(c + 1) * P],
                                                A[:, c * P:(c + 1) * P], start=True, stop=(c == 0))
                        if c:
                            last = nc.tensor.matmul(core.bank(2, P, c * P), state[:, c * P:(c + 1) * P],
                                                    qd[:, c * P:(c + 1) * P], start=False, stop=True)
                    last.then_inc(o_done, 1)
                    pe.wait_ge(sq_ready, i + 1)
                    for c in range(0, T, BANK):
                        last = nc.tensor.matmul(core.bank(4, BANK, c), core.ones[:, :], sq[:, c:c + BANK],
                                                start=True, stop=True)
                    last.then_inc(stat_ready, 1)

            @block.scalar
            def _(act):
                with act.Fori(0, HEADS) as i:
                    own = Chain(act, act_own)
                    nc.scalar.preload_act_table_set("sigmoid_and_others")
                    act.wait_ge(proj_taken, i * 4 + 1)
                    nc.scalar.activation(kT[:, :], bT[:, :], ACT.Sigmoid, scale=-1.0).then_inc(sig_ready, 1)
                    nc.scalar.activation(bT[:, :], bT[:, :], ACT.Sigmoid).then_inc(sig_ready, 1)
                    act.wait_ge(proj_taken, i * 4 + 2)
                    nc.scalar.activation(sig, qT[:, :], ACT.Sigmoid).then_inc(sig_ready, 1)
                    nc.scalar.preload_act_table_set(EXP_LN)
                    act.wait_ge(ln_in, i + 1)
                    nc.scalar.activation(dec[0][:, :], bT[:, :], ACT.Ln).then_inc(ln_ready, 1)
                    for n in range(n_lev + 1):
                        act.wait_ge(diff_ready, i * (n_lev + 1) + (n + 1))
                        d = dec[n % 2][:, :]
                        if n < n_lev:
                            own.link(nc.scalar.activation(d, d, ACT.Abs))
                        nc.scalar.activation(d, d, ACT.Exp, scale=-1.0).then_inc(e_ready, 1)
                    act.wait_ge(level_in, i * n_lev + n_lev)
                    nc.scalar.activation(cdec[:, :], v3(bT[:, :])[:, :, P - 1:P].rearrange("p c n -> p (c n)"), ACT.Exp) \
                        .then_inc(e_ready, 1)
                    nc.scalar.activation(dec[0][:, :], bT[:, :], ACT.Exp).then_inc(e_ready, 1)
                    act.wait_ge(turned, i * 2 + 1)
                    nc.scalar.activation(v_tok, core.bank(4, T), ACT.Identity).then_inc(kv_tok_ready, 1)
                    act.wait_ge(turned, i * 2 + 2)
                    nc.scalar.activation(k_tok, core.bank(6, T), ACT.Identity).then_inc(kv_tok_ready, 1)
                    act.wait_ge(o_done, i + 1)
                    own.link(nc.scalar.activation(oT, core.bank(2, T), ACT.Identity))
                    nc.scalar.activation(sq, oT, ACT.Square).then_inc(sq_ready, 1)
                    act.wait_ge(stat_ready, i + 1)
                    own.link(nc.scalar.activation(hrstd[:, :], core.bank(4, T), ACT.Ln, bias=core.eps6[:, :],
                                                  scale=1.0 / HD))
                    nc.scalar.activation(hrstd[:, :], hrstd[:, :], ACT.Exp, scale=-0.5).then_inc(rstd_ready, 1)
                    own.join()
                    nc.scalar.preload_act_table_set("sigmoid_and_others")
                    nc.scalar.activation(sig_g[:, :], gate(i), ACT.Sigmoid).then_inc(sig_ready, 1)
                    own.restart()
                    act.wait_ge(mix_done, i + 1)

            @block.vector
            def _(dve):
                dve.wait_ge(const, 16)
                with dve.Fori(0, HEADS) as i:
                    own = Chain(dve, dve_own)
                    lower, rest = cols(lb, i, 1), cols(lb, i + HEADS, 1)
                    own.mark(nc.vector.memset(A, 0.0))

                    def take_raw(j, bank, dst):
                        wt.wait_product(dve, i * 4 + j)
                        own.link(nc.vector.tensor_tensor(dst, core.bank(bank, T), core.rstd[:, :], ALU.mult))
                        dve.sem_inc(proj_taken, 1)

                    take_raw(0, 0, bT[:, :])
                    dve.wait_ge(sig_ready, i * 4 + 2)
                    own.mark(nc.vector.tensor_scalar(kT[:, :], kT[:, :], rest, None, ALU.mult))
                    own.link(nc.vector.tensor_scalar(bT[:, :], bT[:, :], rest, lower, ALU.mult, ALU.add))
                    own.link(nc.vector.tensor_scalar(bT[:, :], bT[:, :], LN_LEAST, None, ALU.max))
                    dve.sem_inc(ln_in, 1)
                    take_raw(1, 2, qT[:, :])
                    dve.wait_ge(ln_ready, i + 1)
                    for c in range(0, T, P):
                        own.mark(nc.vector.tensor_tensor_scan(bT[:, c:c + P], core.ones[:, :], dec[0][:, c:c + P], 0.0,
                                                              ALU.mult, ALU.add))
                    own.join()
                    dve.sem_inc(b_ready, 1)
                    dve.wait_ge(sig_ready, i * 4 + 3)
                    own.link(nc.vector.scalar_tensor_tensor(out=qT[:, :], in0=sig, scalar=HD ** -0.5, in1=qT[:, :],
                                                            op0=ALU.mult, op1=ALU.mult))
                    dve.sem_inc(raw_ready, 1)

                    def take(n):
                        dve.wait_ge(level_ready, i * (n_lev + 1) + (n + 1))
                        dve.sem_inc(level_seen, 1)
                        own.link(nc.vector.copy_predicated(
                            v3(A), mask[:, n * P:(n + 1) * P].bitcast(mybir.dt.uint32)
                            .unsqueeze(1).to_broadcast([P, TT, P]), v3(core.bank(2 * (n % 2), T))))
                        dve.sem_inc(level_taken, 1)

                    for n in range(1, n_lev + 1):
                        size, slot = LEVELS[n - 1], (n - 1) % 2
                        dve.wait_ge(e_ready, i * (n_lev + 3) + n)
                        if n >= 3:
                            dve.wait_ge(level_ready, i * (n_lev + 1) + (n - 1))
                        for upper, src in enumerate((kT, qT)):
                            own.mark(nc.vector.tensor_tensor(halves(X[slot], size, upper), halves(src, size, upper),
                                                             halves(dec[slot], size, upper), ALU.mult))
                        own.join()
                        dve.sem_inc(level_in, 1)
                        take(n - 1)
                        if n == 5:
                            take_raw(2, 4, iT[:, :])
                    dve.wait_ge(e_ready, i * (n_lev + 3) + (n_lev + 1))
                    own.link(nc.vector.tensor_tensor(kd[:, :], kT[:, :], dec[n_lev % 2][:, :], ALU.mult))
                    dve.sem_inc(kd_ready, 1)
                    take(n_lev)
                    take_raw(3, 6, gate(i))
                    own.mark(nc.vector.memset(state[:, 0:P], 0.0))
                    dve.wait_ge(e_ready, i * (n_lev + 3) + (n_lev + 3))
                    own.link(nc.vector.tensor_tensor(qd[:, :], qT[:, :], dec[0][:, :], ALU.mult))
                    dve.wait_ge(update_ready, i + 1)
                    for c in range(TT - 1):
                        own.link(nc.vector.scalar_tensor_tensor(
                            out=state[:, (c + 1) * P:(c + 2) * P], in0=state[:, c * P:(c + 1) * P],
                            scalar=cdec[:, c:c + 1], in1=core.bank(0, P, c * P), op0=ALU.mult, op1=ALU.add))
                    dve.sem_inc(state_ready, 1)
                    dve.wait_ge(rstd_ready, i + 1)
                    own.mark(nc.vector.scalar_tensor_tensor(out=sq, in0=oT, scalar=g["hgrn_out_norm_3"][:, 0:1],
                                                            in1=hrstd[:, :], op0=ALU.mult, op1=ALU.mult))
                    dve.wait_ge(sig_ready, i * 4 + 4)
                    own.link(nc.vector.tensor_tensor(sig_g[:, :], sig_g[:, :], gate(i), ALU.mult))
                    own.link(nc.vector.tensor_tensor(gate(i), sq, sig_g[:, :], ALU.mult))
                    dve.sem_inc(mix_done, 1)
                    own.restart()


def cross_attention(core, a, mem, mix):
    nc, h = core.nc, core.h
    W = [a["ca_wq_3"][0], a["ca_wk_3"][0], a["ca_wv_3"][0]]
    with ExitStack() as ctx:
        sb = lambda n, shape: core.sbuf("ca_" + n, shape, ctx)
        wt = Weights(core, "ca", ctx)
        qT = sb("qT", [P, 2 * T])
        kT, vT, v_tok = sb("kT", [P, 2 * MEM]), sb("vT", [P, 2 * MEM]), sb("v_tok", [P, 2 * MEM])
        probs = sb("probs", [P, 2 * MEM])
        pT = sb("probsT", [P, 2 * T])
        col = sb("col", [P, 2 * 4])
        sems = Weights.SIGNALS + ("proj_taken", "v_turned", "v_ready", "scores_ready",
                "max_ready", "exp_ready", "p_ready", "p_turned", "pT_ready", "o_done", "o_taken", "dve_own")
        with core.phase("ca", *sems) as (
                block, *ws, proj_taken, v_turned, v_ready, scores_ready,
                max_ready, exp_ready, p_ready, p_turned, pT_ready, o_done, o_taken, dve_own):
            wt.signals(ws)

            @block.sync
            def _(sp):
                with sp.Fori(0, 4) as i:
                    for j in range(6):
                        wt.load(sp, i * 6 + j, 0, plain_views(W[j // 2], KT, i * CA_D + (j % 2) * P))

            @block.gpsimd
            def _(pool):
                wt.open_raw(pool)
                with pool.Fori(0, 4) as i:
                    for j in range(2):
                        wt.split(pool, i * 6 + j, 0)
                    for j in range(2, 6):
                        wt.split_lo(pool, i * 6 + j, 0)

            @block.tensor
            def _(pe):
                def score(i, b):
                    if b >= 2:
                        pe.wait_ge(exp_ready, i * TT + (b - 1))
                    for k in range(2):
                        last = nc.tensor.matmul(core.bank(4 + b % 2, MEM), qT[:, k * T + b * P:k * T + (b + 1) * P],
                                                kT[:, k * MEM:(k + 1) * MEM], start=(k == 0), stop=(k == 1))
                    last.then_inc(scores_ready, 1)
                wt.open_slots(pe)
                with pe.Fori(0, 4) as i:
                    for j in range(6):
                        if j >= 2:
                            pe.wait_ge(proj_taken, i * 6 + (j - 1))
                        src, n = (h, T) if j < 2 else (mem, MEM)
                        wt.product(pe, core.bank(2 * (j % 2), n), src, i * 6 + j, 0, n, n)
                    pe.wait_ge(proj_taken, i * 6 + 6)
                    for k in range(2):
                        for m in range(2):
                            last = nc.tensor.transpose(core.bank(6, P, m * MEM + k * P),
                                                       vT[:, k * MEM + m * P:k * MEM + (m + 1) * P], core.ident[:, :])
                    last.then_inc(v_turned, 1)
                    score(i, 0)
                    score(i, 1)
                    pe.wait_ge(v_ready, i + 1)
                    for b in range(TT):
                        if b + 2 < TT:
                            score(i, b + 2)
                        pe.wait_ge(p_ready, i * TT + (b + 1))
                        if b >= 2:
                            pe.wait_ge(pT_ready, i * TT + (b - 1))
                        for m in range(2):
                            last = nc.tensor.transpose(core.bank(6 + b % 2, P, m * P),
                                                       probs[:, (b % 2) * MEM + m * P:(b % 2) * MEM + (m + 1) * P],
                                                       core.ident[:, :])
                        last.then_inc(p_turned, 1)
                    pe.wait_ge(pT_ready, i * TT + TT)
                    for k in range(2):
                        for c in range(0, T, BANK):
                            for m in range(2):
                                last = nc.tensor.matmul(core.bank(2 * k, BANK, c), v_tok[:, m * MEM + k * P:m * MEM + (k + 1) * P],
                                                        pT[:, m * T + c:m * T + c + BANK], start=(m == 0), stop=(m == 1))
                    last.then_inc(o_done, 1)
                    pe.wait_ge(o_taken, i + 1)

            @block.scalar
            def _(act):
                with act.Fori(0, 4) as i:
                    nc.scalar.preload_act_table_set(EXP_LN)
                    for j in range(2, 6):
                        wt.split_hi(act, i * 6 + j, 0, in_turn=True)
                    act.wait_ge(v_turned, i + 1)
                    nc.scalar.activation(v_tok[:, :], core.bank(6), ACT.Identity).then_inc(v_ready, 1)
                    def turned(b):
                        act.wait_ge(p_turned, i * TT + (b + 1))
                        nc.scalar.activation(pT[:, :].rearrange("p (m n) -> p m n", m=2)[:, :, b * P:(b + 1) * P],
                                             core.bank(6 + b % 2, MEM).rearrange("p (m n) -> p m n", m=2),
                                             ACT.Identity).then_inc(pT_ready, 1)
                    for b in range(TT):
                        act.wait_ge(max_ready, i * TT + (b + 1))
                        if b >= 2:
                            act.wait_ge(p_turned, i * TT + (b - 1))
                        c = (b % 2) * 4
                        nc.scalar.activation(probs[:, (b % 2) * MEM:(b % 2 + 1) * MEM], core.bank(4 + b % 2, MEM), ACT.Exp,
                                             bias=col[:, c:c + 1], accum_out=col[:, c + 1:c + 2]).then_inc(exp_ready, 1)
                        if b >= 1:
                            turned(b - 1)
                    turned(TT - 1)
                    act.wait_ge(o_done, i + 1)
                    nc.scalar.activation(cols(mix, i * (2 * T), 2 * T), core.bank(0, 2 * T), ACT.Identity).then_inc(o_taken, 1)

            @block.vector
            def _(dve):
                with dve.Fori(0, 4) as i:
                    own = Chain(dve, dve_own)
                    for j in range(6):
                        wt.wait_product(dve, i * 6 + j)
                        if j < 2:
                            own.link(nc.vector.scalar_tensor_tensor(out=qT[:, j * T:(j + 1) * T], in0=core.bank(2 * j, T),
                                                                    scalar=CA_D ** -0.5, in1=core.rstd[:, :],
                                                                    op0=ALU.mult, op1=ALU.mult))
                        else:
                            own.link(nc.vector.tensor_copy((kT, vT)[j // 2 - 1][:, (j % 2) * MEM:(j % 2 + 1) * MEM],
                                                           core.bank(2 * (j % 2), MEM)))
                        dve.sem_inc(proj_taken, 1)

                    def peak(b):
                        dve.wait_ge(scores_ready, i * TT + (b + 1))
                        nc.vector.tensor_reduce(out=col[:, (b % 2) * 4:(b % 2) * 4 + 1], in_=core.bank(4 + b % 2, MEM),
                                                axis=AX.X, op=ALU.max, negate=True).then_inc(max_ready, 1)
                    peak(0)
                    for b in range(TT):
                        if b + 1 < TT:
                            peak(b + 1)
                        c, s = (b % 2) * 4, probs[:, (b % 2) * MEM:(b % 2 + 1) * MEM]
                        dve.wait_ge(exp_ready, i * TT + (b + 1))
                        own.link(nc.vector.reciprocal(col[:, c + 2:c + 3], col[:, c + 1:c + 2]))
                        nc.vector.tensor_scalar(s, s, col[:, c + 2:c + 3], None, ALU.mult).then_inc(p_ready, 1)
                    own.restart()


def conv_ffn(core, a, gain, dst):
    nc = core.nc
    w_up, w_down = a["ffn_w_up_3"][0], a["ffn_w_down_3"][0]
    wide = T + 2
    with ExitStack() as ctx:
        sb = lambda n, shape, dt=F32: core.sbuf("cf_" + n, shape, ctx, dt)
        gated = tuple(sb(f"gated_{p}", [P, FF3_GROUP * T], F32R) for p in ("hi", "lo"))
        taps, bias = sb("taps", [P, 3 * 2 * FT3]), sb("bias", [P, 2 * FT3])
        pad = sb("padded", [P, wide])
        conv = [core.work[:, s * T:(s + 1) * T] for s in range(2)]
        with core.phase("cfc", "loaded") as (block, loaded):
            @block.sync
            def _(sp):
                with nc.allow_non_contiguous_dma("taps, a channel a partition"):
                    for j in range(3):
                        sp.dma_start(taps[:, j * 2 * FT3:(j + 1) * 2 * FT3],
                                     a["ffn_conv_w_3"][0][j].rearrange("(k p) -> p k", p=P)).then_inc(loaded, 16)
                    sp.dma_start(bias[:, :], a["ffn_conv_b_3"][0].rearrange("(k p) -> p k", p=P)).then_inc(loaded, 16)
                sp.wait_ge(loaded, 64)

            @block.vector
            def _(dve):
                nc.vector.memset(pad[:, 0:2], 0.0)

        def up(base, tiles):
            def take(dve, own, i, s, product):
                tap = lambda j: cols(taps, i + (base + j * 2 * FT3 + s * FT3), 1)
                own.link(nc.vector.tensor_tensor(pad[:, 2:2 + T], product, core.rstd[:, :], ALU.mult))
                own.link(nc.vector.tensor_scalar(conv[s], pad[:, 2:2 + T], tap(2), cols(bias, i + (base + s * FT3), 1),
                                                 ALU.mult, ALU.add))
                own.link(nc.vector.scalar_tensor_tensor(out=conv[s], in0=pad[:, 0:T], scalar=tap(0), in1=conv[s],
                                                        op0=ALU.mult, op1=ALU.add))
                return nc.vector.scalar_tensor_tensor(out=conv[s], in0=pad[:, 1:1 + T], scalar=tap(1), in1=conv[s],
                                                      op0=ALU.mult, op1=ALU.add)

            def gelu(act, i, s):
                return nc.scalar.activation(conv[0], conv[0], ACT.Gelu_apprx_tanh)

            def gate(dve, own, i, s):
                if s == 1:
                    hi, lo = (cols(part, i * T) for part in gated)
                    own.link(nc.vector.tensor_tensor(conv[1], conv[1], conv[0], ALU.mult))
                    own.link(nc.vector.tensor_copy(hi, conv[1]))
                    own.link(nc.vector.tensor_tensor(lo, conv[1], hi.bitcast(F32), ALU.subtract))

            return Stage(w_up, 2 * tiles, take, core.h, mid=gelu, mids=(0,), finish=gate, feeds=(1,),
                         load=lambda i, s: plain_views(w_up, KT, i * P + (base * P + s * FF3)))

        stages = []
        for base in range(0, FT3, FF3_GROUP):
            tiles = min(FF3_GROUP, FT3 - base)
            stages.append(up(base, tiles))
            stages.append(Stage(w_down[base * P:(base + tiles) * P, :], KT, (add_to if base else copy_to)(nc, dst),
                                gated, kts=tiles, **(sum_squares(core, dst) if base + tiles == FT3 else {})))
        linears(core, "cf", stages, Operand(core, core.x, gain, core.h, core.eps6))


def third_block(core, a, c_in, g):
    nc = core.nc
    w = a["w_in_3"][0]
    w_out = a["w_out_3"][0]
    lower_bound(core, g)

    def out_views(i, s):
        c = i * (2 * P) + s * P
        heads = [(lambda d, at=AD * n: d[at:at + AD, :, :],
                  w_out[n * 256:(n + 1) * 256, ds(c, P)].rearrange("(k p) n -> p k n", p=AD)) for n in range(2)]
        return [heads, [(lambda d: d, w_out[512:1024, ds(c, P)].rearrange("(k p) n -> p k n", p=P))]]

    with ExitStack() as ctx:
        mix = core.sbuf("mix3", [P, KT * T], ctx)
        norm_operand(core, "n4", core.x, g["mix_pre_norm_3"], core.eps6)
        window_attention(core, w, c_in, g["sinks"], mix)
        hgrn(core, w, c_in, g, mix)
        linear(core, "out3", w_out, KT, copy_to(nc, mix), load=out_views, dmas=(2, 1),
               operand=Operand(core, mix, None, core.h), **sum_squares(core, mix))
        rms_norm(core, "np1", mix, g["mix_post_norm_3"], None, core.eps6, residual=core.x, squared_before=True)
        with ExitStack() as mem_ctx:
            mem = tuple(core.sbuf(f"mem_{p}", [P, KT * MEM], mem_ctx, F32R) for p in ("hi", "lo"))
            with ExitStack() as raw_ctx:
                memT = core.sbuf("memT", [P, KT * MEM], raw_ctx)
                load_transposed(core, "mem", a["mem_3"][0], memT, MEM // P)
                rms_norm(core, "nm", memT, g["mem_norm_3"], memT, core.eps6, tok=MEM)
                split_operand(core, "ms", memT, mem, MEM)
            norm_operand(core, "n5", core.x, g["ca_pre_norm_3"], core.eps6)
            cross_attention(core, a, mem, mix)
        linear(core, "cao", a["ca_wo_3"][0], KT, copy_to(nc, mix), operand=Operand(core, mix, None, core.h),
               **sum_squares(core, mix))
        rms_norm(core, "np2", mix, g["ca_post_norm_3"], None, core.eps6, residual=core.x, squared_before=True)
        conv_ffn(core, a, g["ffn_pre_norm_3"], mix)
        rms_norm(core, "np3", mix, g["ffn_post_norm_3"], None, core.eps6, residual=core.x, squared_before=True)

def shape_constants():
    f = np.float32
    p = np.arange(P, dtype=np.float64)
    j = np.arange(T, dtype=np.float64)
    rel = j[None, :] - (T - P) - p[:, None]
    dist = np.where(rel > 0, MASKED, rel)
    log_g = np.log1p(-np.exp2(-5.0 - np.arange(HEADS)))
    d = p[None, :] - p[:, None]
    mask = np.concatenate([np.where(d >= 0, np.exp(g * np.maximum(d, 0)), 0) * RET_K_SCALE for g in log_g], 1)
    qdec = np.concatenate([np.broadcast_to(np.exp(g * (p + 1)), (P, P)) for g in log_g], 1)
    kdec = np.concatenate([np.stack([np.exp(g * (P - 1 - p)) * RET_K_SCALE for g in log_g], 1),
                           np.broadcast_to(np.exp(log_g * P), (P, HEADS))], 1)
    slopes = np.broadcast_to(np.exp2(-8.0 * np.arange(1, HEADS + 1) / HEADS), (P, HEADS))
    flip = np.kron(np.eye(2), np.eye(COLS_W)[::-1])
    c = np.arange(COLS_W)
    start = np.clip(c - NA_KC // 2, 0, COLS_W - NA_KC)
    ok = (c[None, :] >= start[:, None]) & (c[None, :] < start[:, None] + NA_KC)
    edge = np.tile(np.where(ok, 0.0, MASKED), (2, 1))
    t = np.arange(T)
    inv = np.concatenate([1.0 / (np.clip(t - w // 2 + w, 0, T) - np.clip(t - w // 2, 0, T)) for w in POOL_WINDOWS])
    inv = np.repeat(inv.reshape(2, 2, T), 64, 1).reshape(2, P, T)
    inv = np.concatenate([inv[:, :, :POOL_EDGE], inv[:, :, -POOL_EDGE:], inv[:, :, T // 2:T // 2 + 1]], 2)
    inv = inv.transpose(1, 0, 2).reshape(P, 2 * (2 * POOL_EDGE + 1))
    q, k = np.arange(WIN)[:, None], np.arange(2 * WIN)[None, :]
    diff = q + WIN - k
    seen = (diff >= 0) & (diff < WIN)
    window = np.where(np.concatenate([seen & (k >= WIN), seen], 1), 0.0, MASKED)
    key, query = np.arange(P)[:, None], np.arange(P)[None, :]
    levels = [np.eye(P)] + [(key // (2 * s) == query // (2 * s)) & (key // s % 2 == 0) & (query // s % 2 == 1)
                            for s in LEVELS]
    return {k: np.ascontiguousarray(v.astype(f)) for k, v in dict(
        ident=np.eye(P), dist=dist, ret_mask=mask, ret_qdec=qdec, ret_kdec=kdec, slopes=slopes,
        flip=flip, edge=edge, inv_count=inv, window=window,
        levels=np.concatenate(levels, 1)).items()}


def build(nc, a, c_in, out, blocks=(1, 2, 3)):
    with ExitStack() as ctx:
        core = Core(nc, ctx)
        g, small = {}, []
        by_tile = lambda v: v.rearrange("(k p) -> p k", p=P)
        def column(name, src, n):
            g[name] = core.sbuf("g_" + name, [P, n])
            small.append((g[name][:, :], src))
        for name in ("norm1_g", "norm2_g"):
            column(name, by_tile(a[name][0]), KT)
        column("final_norm_g", by_tile(a["final_norm_g"]), KT)
        column("diff_norm_g0", by_tile(a["diff_norm_g"][0]), 1)
        column("ret_norm_g", by_tile(a["ret_norm_g"][0]), HEADS)
        column("slopes", c_in["slopes"], HEADS)
        g["neg_lam"] = core.sbuf("g_neg_lam", [P, 1])[:, :]
        g["diff_norm_g"] = core.sbuf("g_diff_gain", [P, 1])[:, :]
        if 2 in blocks:
            second_gains(core, a, c_in, g, column, by_tile)
        if 3 in blocks:
            third_gains(core, a, c_in, g, column, by_tile)
        setup(core, c_in, small)
        with core.phase("fold") as (block,):
            @block.vector
            def _(dve):
                nc.vector.tensor_scalar(g["diff_norm_g"], g["diff_norm_g0"][:, :], 1.0 - LAMBDA_INIT, None, ALU.mult)
        load_transposed(core, "xin", a["x"][0], core.x, TT)
        if 1 in blocks:
            first_block(core, a, c_in, g)
        if 2 in blocks:
            second_block(core, a, c_in, g)
        if 3 in blocks:
            third_block(core, a, c_in, g)
        store_transposed(core, "xout", core.x, out[0])


def kernel(**inputs):
    import concourse.bacc as bacc
    from concourse.bass_utils import run_bass_kernel_spmd

    nc = bacc.Bacc("TRN2", target_bir_lowering=False, num_devices=1)
    arrays, handles, c_in = {}, {}, {}
    for name, value in inputs.items():
        v = np.ascontiguousarray(value)
        if name == "na_rpb_2":
            v = np.pad(v, ((0, 0), (0, 0), (0, 0), (RPB_PAD, RPB_PAD)))
        arrays[name + "_dram"] = v
        handles[name] = nc.dram_tensor(name + "_dram", v.shape, F32, kind="ExternalInput").ap()
    for name, value in shape_constants().items():
        arrays["const_" + name] = value
        c_in[name] = nc.dram_tensor("const_" + name, value.shape, F32, kind="ExternalInput").ap()
    out = nc.dram_tensor("y_dram", (1, T, D), F32, kind="ExternalOutput").ap()
    build(nc, handles, c_in, out)
    result = run_bass_kernel_spmd(nc, [arrays], core_ids=[0])
    return result.results[0]["y_dram"]
```
